# Optimizing a Trainium2 kernel written in Bass

```python
import math
import jax, jax.numpy as jnp
from jax import lax
import numpy as np

D_MODEL = 1024
BATCH = 1
SEQ = 256
DEPTH = 1

LRU_WIDTH = D_MODEL // 4
LRU_BLOCKS = 4
LRU_BLOCK_W = LRU_WIDTH // LRU_BLOCKS
LRU_CONV = 4
LRU_C = 8.0
GLA_HEADS = 4
GLA_DV = (D_MODEL // 4) // GLA_HEADS
GLA_DK = GLA_DV // 2
GLA_GATE_RANK = 16
GLA_TAU = 16.0
GLA_CHUNK = 64
MOBA_HEADS = 8
MOBA_DH = (D_MODEL // 2) // MOBA_HEADS
MOBA_BLOCK = 256
MOBA_TOPK = 3
MOBA_Q_CHUNK = 128
REL_BUCKETS = 32
REL_MAX_DIST = 128
D_FF = -(-8 * D_MODEL // (3 * 256)) * 256

GLA_QK_W = GLA_HEADS * GLA_DK
GLA_V_W = GLA_HEADS * GLA_DV
MOBA_W = MOBA_HEADS * MOBA_DH
D_MIX = LRU_WIDTH + GLA_V_W + MOBA_W
IN_SPLITS = (LRU_WIDTH, LRU_WIDTH, GLA_QK_W, GLA_QK_W, GLA_V_W, GLA_GATE_RANK, GLA_V_W, MOBA_W, MOBA_W, MOBA_W)
D_IN = sum(IN_SPLITS)
RMS_EPS = 1e-6
NEG_INF = -1e30


def rms_norm(x, g):
    xf = x.astype(jnp.float32)
    y = xf * lax.rsqrt(jnp.mean(xf * xf, axis=-1, keepdims=True) + RMS_EPS)
    return (y * g.astype(jnp.float32)).astype(x.dtype)

def split_heads(t, n):
    b, s, w = t.shape
    return t.astype(jnp.float32).reshape(b, s, n, w // n).transpose(0, 2, 1, 3)

def t5_bucket(rel):
    n = jnp.maximum(rel, 0)
    max_exact = REL_BUCKETS // 2
    nf = jnp.maximum(n, 1).astype(jnp.float32)
    large = max_exact + (jnp.log(nf / max_exact) / math.log(REL_MAX_DIST / max_exact)
                         * (REL_BUCKETS - max_exact)).astype(jnp.int32)
    large = jnp.minimum(large, REL_BUCKETS - 1)
    return jnp.where(n < max_exact, n, large)

def rg_lru_branch(xb, gb, conv_w, conv_b, wa, ba, wx, bx, lam):
    b, s, c = xb.shape
    xc = lax.conv_general_dilated(xb, conv_w[:, None, :].astype(xb.dtype), window_strides=(1,),
                                  padding=[(LRU_CONV - 1, 0)],
                                  dimension_numbers=('NWC', 'WIO', 'NWC'),
                                  feature_group_count=c)
    xc = xc.astype(jnp.float32) + conv_b.astype(jnp.float32)
    xg = xc.reshape(b, s, LRU_BLOCKS, LRU_BLOCK_W)
    r = jax.nn.sigmoid(jnp.einsum('bsgi,gij->bsgj', xg, wa.astype(jnp.float32)).reshape(b, s, c)
                       + ba.astype(jnp.float32))
    i = jax.nn.sigmoid(jnp.einsum('bsgi,gij->bsgj', xg, wx.astype(jnp.float32)).reshape(b, s, c)
                       + bx.astype(jnp.float32))
    log_a = -LRU_C * r * jax.nn.softplus(-lam.astype(jnp.float32))
    a = jnp.exp(log_a)
    mult = jnp.sqrt(-jnp.expm1(2.0 * log_a))
    mult = mult.at[:, 0].set(1.0)
    u = mult * (i * xc)

    def combine(left, right):
        a1, b1 = left
        a2, b2 = right
        return a1 * a2, a2 * b1 + b2

    _, h = lax.associative_scan(combine, (a, u), axis=1)
    return h * jax.nn.gelu(gb.astype(jnp.float32))

def gla_chunked(q, k, v, g):
    b, h, s, dk = q.shape
    dv = v.shape[-1]
    c = GLA_CHUNK
    n = s // c
    q = q.reshape(b, h, n, c, dk) * (dk ** -0.5)
    k = k.reshape(b, h, n, c, dk)
    v = v.reshape(b, h, n, c, dv)
    cum = jnp.cumsum(g.reshape(b, h, n, c, dk), axis=3)
    last = cum[:, :, :, -1:, :]
    q_d = q * jnp.exp(cum)
    k_d = k * jnp.exp(-cum)
    causal = jnp.tril(jnp.ones((c, c), dtype=bool))
    attn = jnp.where(causal, jnp.einsum('bhncd,bhned->bhnce', q_d, k_d), 0.0)
    intra = jnp.einsum('bhnce,bhnev->bhncv', attn, v)
    kv = jnp.einsum('bhncd,bhncv->bhndv', k * jnp.exp(last - cum), v)
    decay = jnp.exp(last[:, :, :, 0, :])

    def step(state, inp):
        kv_n, d_n = inp
        return d_n[..., None] * state + kv_n, state

    init = jnp.zeros((b, h, dk, dv), jnp.float32)
    _, s_prev = lax.scan(step, init, (kv.transpose(2, 0, 1, 3, 4), decay.transpose(2, 0, 1, 3)))
    s_prev = s_prev.transpose(1, 2, 0, 3, 4)
    inter = jnp.einsum('bhncd,bhndv->bhncv', q_d, s_prev)
    return (intra + inter).reshape(b, h, s, dv)

def moba_attention(q, k, v, rel_bias):
    b, h, s, d = q.shape
    nb = -(-s // MOBA_BLOCK)
    pad = nb * MOBA_BLOCK - s
    k_blk = jnp.pad(k, ((0, 0), (0, 0), (0, pad), (0, 0))).reshape(b, h, nb, MOBA_BLOCK, d)
    v_blk = jnp.pad(v, ((0, 0), (0, 0), (0, pad), (0, 0))).reshape(b, h, nb, MOBA_BLOCK, d)
    k_mean = jnp.mean(k_blk, axis=3)
    topk = min(MOBA_TOPK, nb)
    scale = d ** -0.5
    bias_h = rel_bias.T.astype(jnp.float32)
    bi = jnp.arange(b)[:, None, None]
    hi = jnp.arange(h)[None, :, None]
    blk_ids = jnp.arange(nb)
    offs = jnp.arange(MOBA_BLOCK)

    def chunk(ci):
        q0 = ci * MOBA_Q_CHUNK
        qc = lax.dynamic_slice_in_dim(q, q0, MOBA_Q_CHUNK, axis=2)
        qpos = q0 + jnp.arange(MOBA_Q_CHUNK)
        n_past = q0 // MOBA_BLOCK
        gate = jnp.einsum('bhqd,bhnd->bhqn', qc, k_mean)
        gate = jnp.where(blk_ids < n_past, gate, -jnp.inf)
        _, sel = lax.top_k(gate, topk)
        k_own = lax.dynamic_index_in_dim(k_blk, n_past, axis=2, keepdims=False)
        v_own = lax.dynamic_index_in_dim(v_blk, n_past, axis=2, keepdims=False)
        rel_own = qpos[:, None] - (n_past * MOBA_BLOCK + offs)[None, :]
        logit_own = (jnp.einsum('bhqd,bhkd->bhqk', qc, k_own) * scale
                     + bias_h[:, t5_bucket(rel_own)])
        logit_own = jnp.where(rel_own >= 0, logit_own, NEG_INF)
        logits = []
        for j in range(topk):
            idx = sel[..., j]
            kj = k_blk[bi, hi, idx]
            rel = qpos[:, None] - (idx[..., None] * MOBA_BLOCK + offs)
            bias = bias_h[hi[..., None], t5_bucket(rel)]
            lj = jnp.einsum('bhqd,bhqkd->bhqk', qc, kj) * scale + bias
            logits.append(jnp.where(j < n_past, lj, NEG_INF))
        logits.append(logit_own)
        p = jax.nn.softmax(jnp.concatenate(logits, axis=-1), axis=-1)
        p = p.reshape(b, h, MOBA_Q_CHUNK, topk + 1, MOBA_BLOCK)
        out = jnp.einsum('bhqk,bhkd->bhqd', p[..., topk, :], v_own)
        for j in range(topk):
            vj = v_blk[bi, hi, sel[..., j]]
            out = out + jnp.einsum('bhqk,bhqkd->bhqd', p[..., j, :], vj)
        return out

    out = lax.map(chunk, jnp.arange(s // MOBA_Q_CHUNK))
    return out.transpose(1, 2, 0, 3, 4).reshape(b, h, s, d)

def hybrid_mixer(h, w_in, conv_w, conv_b, wa, ba, wx, bx, lam, gate_w2, gate_b, gla_gain, rel_bias):
    bsz, s, _ = h.shape
    proj = h @ w_in
    split_points = [int(p) for p in np.cumsum(IN_SPLITS)[:-1]]
    lru_x, lru_g, gq, gk, gv, g_lr, g_out, mq, mk, mv = jnp.split(proj, split_points, axis=-1)
    y_lru = rg_lru_branch(lru_x, lru_g, conv_w, conv_b, wa, ba, wx, bx, lam)
    log_alpha = jax.nn.log_sigmoid((g_lr @ gate_w2 + gate_b).astype(jnp.float32)) / GLA_TAU
    o = gla_chunked(split_heads(gq, GLA_HEADS), split_heads(gk, GLA_HEADS),
                    split_heads(gv, GLA_HEADS), split_heads(log_alpha, GLA_HEADS))
    o = o.transpose(0, 2, 1, 3)
    o = o * lax.rsqrt(jnp.mean(o * o, axis=-1, keepdims=True) + RMS_EPS)
    y_gla = (o.reshape(bsz, s, GLA_V_W) * gla_gain.astype(jnp.float32)
             * jax.nn.silu(g_out.astype(jnp.float32)))
    y_moba = moba_attention(split_heads(mq, MOBA_HEADS), split_heads(mk, MOBA_HEADS),
                            split_heads(mv, MOBA_HEADS), rel_bias)
    y_moba = y_moba.transpose(0, 2, 1, 3).reshape(bsz, s, MOBA_W)
    return jnp.concatenate([y_lru, y_gla, y_moba], axis=-1).astype(h.dtype)

def first_inputs(seed: int = 0) -> dict:
    key = jax.random.key(seed)
    ks = jax.random.split(key, 24)
    f32 = jnp.float32
    L = DEPTH

    def nrm(k, shape, scale):
        return jax.random.normal(k, shape, f32) * scale

    u = jax.random.uniform(ks[12], (L, LRU_WIDTH), f32, 0.9, 0.999) ** (1.0 / LRU_C)
    return {
        'x': nrm(ks[0], (BATCH, SEQ, D_MODEL), 1.0),
        'pre_mix_norm': 1.0 + nrm(ks[1], (L, D_MODEL), 0.02),
        'post_mix_norm': 1.0 + nrm(ks[2], (L, D_MODEL), 0.02),
        'pre_ffn_norm': 1.0 + nrm(ks[3], (L, D_MODEL), 0.02),
        'post_ffn_norm': 1.0 + nrm(ks[4], (L, D_MODEL), 0.02),
        'w_in': nrm(ks[5], (L, D_MODEL, D_IN), D_MODEL ** -0.5),
        'w_out': nrm(ks[6], (L, D_MIX, D_MODEL), D_MIX ** -0.5),
        'lru_conv_w': nrm(ks[7], (L, LRU_CONV, LRU_WIDTH), LRU_CONV ** -0.5),
        'lru_conv_b': nrm(ks[8], (L, LRU_WIDTH), 0.01),
        'lru_wa': nrm(ks[9], (L, LRU_BLOCKS, LRU_BLOCK_W, LRU_BLOCK_W), LRU_BLOCK_W ** -0.5),
        'lru_ba': nrm(ks[10], (L, LRU_WIDTH), 0.01),
        'lru_wx': nrm(ks[11], (L, LRU_BLOCKS, LRU_BLOCK_W, LRU_BLOCK_W), LRU_BLOCK_W ** -0.5),
        'lru_bx': nrm(ks[13], (L, LRU_WIDTH), 0.01),
        'lru_lambda': jnp.log(u) - jnp.log1p(-u),
        'gla_gate_w2': nrm(ks[14], (L, GLA_GATE_RANK, GLA_QK_W), GLA_GATE_RANK ** -0.5),
        'gla_gate_b': nrm(ks[15], (L, GLA_QK_W), 0.01),
        'gla_norm': 1.0 + nrm(ks[16], (L, GLA_V_W), 0.02),
        'rel_bias': nrm(ks[17], (REL_BUCKETS, MOBA_HEADS), 0.2),
        'w_ffn_gate': nrm(ks[18], (L, D_MODEL, D_FF), D_MODEL ** -0.5),
        'w_ffn_up': nrm(ks[19], (L, D_MODEL, D_FF), D_MODEL ** -0.5),
        'w_ffn_down': nrm(ks[20], (L, D_FF, D_MODEL), D_FF ** -0.5),
    }

def first_block(x, pre_mix_norm, post_mix_norm, pre_ffn_norm, post_ffn_norm, w_in, w_out,
              lru_conv_w, lru_conv_b, lru_wa, lru_ba, lru_wx, lru_bx, lru_lambda,
              gla_gate_w2, gla_gate_b, gla_norm, rel_bias, w_ffn_gate, w_ffn_up, w_ffn_down):
    for l in range(DEPTH):
        h = rms_norm(x, pre_mix_norm[l])
        mix = hybrid_mixer(h, w_in[l], lru_conv_w[l], lru_conv_b[l], lru_wa[l], lru_ba[l],
                           lru_wx[l], lru_bx[l], lru_lambda[l], gla_gate_w2[l], gla_gate_b[l],
                           gla_norm[l], rel_bias)
        x = x + rms_norm(mix @ w_out[l], post_mix_norm[l])
        h = rms_norm(x, pre_ffn_norm[l])
        f = (jax.nn.silu(h @ w_ffn_gate[l]) * (h @ w_ffn_up[l])) @ w_ffn_down[l]
        x = x + rms_norm(f, post_ffn_norm[l])
    return x


DEPTH_2 = 2

NORM_EPS = 1e-6
ROPE_THETA = 500000.0

A_HEADS = 4
A_HEAD_DIM = 64
A_WIDTH = A_HEADS * A_HEAD_DIM
A_DECAY_LORA = 64
A_ICLR_LORA = 64
A_GATE_LORA = 160
A_GN_EPS = 64e-5
A_SIZES = (A_WIDTH, A_WIDTH, A_WIDTH, A_DECAY_LORA, A_ICLR_LORA, A_GATE_LORA)
A_PROJ = sum(A_SIZES)

B_HEADS = 4
B_HEAD_DIM = 64
B_WIDTH = B_HEADS * B_HEAD_DIM
B_ROT_DIM = B_HEAD_DIM // 4
B_PATTERNS = ((128, 1), (512, 4), (2048, 16))
B_BLOCK = 128
B_PROJ = 3 * B_WIDTH

C_HEADS = 4
C_NOPE_DIM = 128
C_ROPE_DIM = 64
C_V_DIM = 128
C_Q_LORA = 256
C_KV_LORA = 128
C_WIDTH = C_HEADS * C_V_DIM
C_Q_BLOCK = 128
C_PROJ = C_Q_LORA + C_KV_LORA + C_ROPE_DIM

MIX_WIDTH = A_WIDTH + B_WIDTH + C_WIDTH
P_TOTAL = A_PROJ + B_PROJ + C_PROJ
D_FF_2 = ((8 * D_MODEL + 767) // 768) * 256


def split_sizes(t, sizes):
    idx = [int(i) for i in np.cumsum(sizes)[:-1]]
    return jnp.split(t, idx, axis=-1)

def rms_norm_2(x, g):
    xf = x.astype(jnp.float32)
    y = xf * lax.rsqrt(jnp.mean(xf * xf, axis=-1, keepdims=True) + NORM_EPS)
    return (y * g.astype(jnp.float32)).astype(x.dtype)

def rope_tables(positions, dim):
    inv_freq = 1.0 / (ROPE_THETA ** (jnp.arange(0, dim, 2, dtype=jnp.float32) / dim))
    ang = positions.astype(jnp.float32)[..., None] * inv_freq
    return jnp.cos(ang), jnp.sin(ang)

def apply_rope(t, cos, sin):
    t1, t2 = jnp.split(t, 2, axis=-1)
    c = cos[:, :, None, :].astype(t.dtype)
    s = sin[:, :, None, :].astype(t.dtype)
    return jnp.concatenate([t1 * c - t2 * s, t1 * s + t2 * c], axis=-1)

def partial_rope(t, cos, sin):
    rot, rest = jnp.split(t, [B_ROT_DIM], axis=-1)
    return jnp.concatenate([apply_rope(rot, cos, sin), rest], axis=-1)

def token_shift(t):
    return jnp.pad(t, ((0, 0), (1, 0), (0, 0)))[:, :-1]

def rwkv7_mixer(pa, mu, w0, decay_up, a0, iclr_up, gate_up, k_k, k_a, r_k, ln_w, ln_b):
    bsz, seq, _ = pa.shape
    pf = pa.astype(jnp.float32)
    pf = pf + (token_shift(pf) - pf) * mu
    r, k, v, xw, xa, xg = split_sizes(pf, A_SIZES)
    w_log = -jax.nn.softplus(-(w0 + jnp.tanh(xw) @ decay_up)) - 0.5
    decay = jnp.exp(-jnp.exp(w_log))
    a = jax.nn.sigmoid(a0 + xa @ iclr_up)
    g = jax.nn.sigmoid(xg) @ gate_up

    def heads(t):
        return t.reshape(bsz, seq, A_HEADS, A_HEAD_DIM)

    kk = heads(k * k_k)
    kk = kk / jnp.maximum(jnp.linalg.norm(kk, axis=-1, keepdims=True), 1e-12)
    k = k * (1.0 + (a - 1.0) * k_a)
    r_h, k_h, v_h, w_h, a_h = heads(r), heads(k), heads(v), heads(decay), heads(a)
    b_h = kk * a_h

    def step(state, inp):
        r_t, w_t, k_t, v_t, kk_t, b_t = inp
        sa = jnp.einsum('bhvk,bhk->bhv', state, kk_t)
        state = (state * w_t[:, :, None, :] - sa[..., None] * b_t[:, :, None, :]
                 + v_t[..., None] * k_t[:, :, None, :])
        y = jnp.einsum('bhvk,bhk->bhv', state, r_t)
        return state, y

    seq_first = lambda t: jnp.moveaxis(t, 1, 0)
    state0 = jnp.zeros((bsz, A_HEADS, A_HEAD_DIM, A_HEAD_DIM), jnp.float32)
    _, y = lax.scan(step, state0, tuple(seq_first(t) for t in (r_h, w_h, k_h, v_h, kk, b_h)))
    y = jnp.moveaxis(y, 0, 1)
    mean = jnp.mean(y, axis=-1, keepdims=True)
    var = jnp.mean(jnp.square(y - mean), axis=-1, keepdims=True)
    y = ((y - mean) * lax.rsqrt(var + A_GN_EPS)).reshape(bsz, seq, A_WIDTH) * ln_w + ln_b
    bonus = jnp.sum(r_h * k_h * r_k, axis=-1, keepdims=True) * v_h
    y = y + bonus.reshape(bsz, seq, A_WIDTH)
    return (y * g).astype(pa.dtype)

def dilated_branch(q, k, v, dil, band):
    bsz, seq, nh, hd = q.shape
    span = dil * B_BLOCK
    seq_pad = -(-seq // span) * span
    pad = ((0, 0), (0, seq_pad - seq), (0, 0), (0, 0))
    q, k, v = (jnp.pad(t, pad) for t in (q, k, v))
    sub = seq_pad // dil
    nb = sub // B_BLOCK

    def to_blocks(t):
        return t.reshape(bsz, sub, dil, nh, hd).transpose(0, 2, 1, 3, 4).reshape(bsz, dil, nb, B_BLOCK, nh, hd)

    def with_prev(t):
        prev = jnp.pad(t, ((0, 0), (0, 0), (1, 0), (0, 0), (0, 0), (0, 0)))[:, :, :-1]
        return jnp.concatenate([prev, t], axis=3)

    qb = to_blocks(q)
    kw, vw = with_prev(to_blocks(k)), with_prev(to_blocks(v))
    s = jnp.einsum('brnqhd,brnkhd->brnhqk', qb, kw).astype(jnp.float32) * (hd ** -0.5)
    qi = jnp.arange(B_BLOCK)[:, None] + B_BLOCK
    ki = jnp.arange(2 * B_BLOCK)[None, :]
    dist = qi - ki
    in_band = (dist >= 0) & (dist <= band)
    has_prev = (jnp.arange(nb) > 0)[:, None, None] | (ki >= B_BLOCK)[None]
    mask = in_band[None] & has_prev
    s = jnp.where(mask[None, None, :, None], s, -jnp.inf)
    lse = jax.nn.logsumexp(s, axis=-1)
    p = jnp.exp(s - lse[..., None])
    o = jnp.einsum('brnhqk,brnkhd->brnqhd', p.astype(v.dtype), vw)
    o = o.reshape(bsz, dil, sub, nh, hd).transpose(0, 2, 1, 3, 4).reshape(bsz, seq_pad, nh, hd)[:, :seq]
    lse = lse.transpose(0, 1, 2, 4, 3).reshape(bsz, dil, sub, nh).transpose(0, 2, 1, 3).reshape(bsz, seq_pad, nh)[:, :seq]
    return o, lse

def dilated_mixer(pb, cos, sin):
    bsz, seq, _ = pb.shape
    q, k, v = (t.reshape(bsz, seq, B_HEADS, B_HEAD_DIM) for t in jnp.split(pb, 3, axis=-1))
    q = partial_rope(q, cos, sin)
    k = partial_rope(k, cos, sin)
    outs, lses = zip(*[dilated_branch(q, k, v, d, w // d) for (w, d) in B_PATTERNS])
    wts = jax.nn.softmax(jnp.stack(lses), axis=0)
    o = jnp.sum(wts[..., None] * jnp.stack(outs).astype(jnp.float32), axis=0)
    return o.reshape(bsz, seq, B_WIDTH).astype(pb.dtype)

def mla_mixer(pc, cos, sin, q_norm_g, kv_norm_g, w_uq, w_ukv):
    bsz, seq, _ = pc.shape
    cq, ckv, k_rope = split_sizes(pc, (C_Q_LORA, C_KV_LORA, C_ROPE_DIM))
    q = (rms_norm_2(cq, q_norm_g) @ w_uq).reshape(bsz, seq, C_HEADS, C_NOPE_DIM + C_ROPE_DIM)
    kv = (rms_norm_2(ckv, kv_norm_g) @ w_ukv).reshape(bsz, seq, C_HEADS, C_NOPE_DIM + C_V_DIM)
    q_nope, q_rope = jnp.split(q, [C_NOPE_DIM], axis=-1)
    k_nope, v = jnp.split(kv, [C_NOPE_DIM], axis=-1)
    q_rope = apply_rope(q_rope, cos, sin)
    k_rope = apply_rope(k_rope[:, :, None, :], cos, sin)[:, :, 0]
    nq = seq // C_Q_BLOCK
    scale = (C_NOPE_DIM + C_ROPE_DIM) ** -0.5
    key_pos = jnp.arange(seq)

    def blocks(t):
        return jnp.moveaxis(t.reshape(bsz, nq, C_Q_BLOCK, *t.shape[2:]), 1, 0)

    def attend(args):
        qn, qr, start = args
        s = (jnp.einsum('bqhd,bkhd->bhqk', qn, k_nope)
             + jnp.einsum('bqhd,bkd->bhqk', qr, k_rope)).astype(jnp.float32) * scale
        q_pos = start + jnp.arange(C_Q_BLOCK)
        s = jnp.where(key_pos[None, :] <= q_pos[:, None], s, -jnp.inf)
        p = jax.nn.softmax(s, axis=-1)
        return jnp.einsum('bhqk,bkhd->bqhd', p.astype(v.dtype), v)

    o = lax.map(attend, (blocks(q_nope), blocks(q_rope), jnp.arange(nq) * C_Q_BLOCK))
    return jnp.moveaxis(o, 0, 1).reshape(bsz, seq, C_WIDTH)

def second_inputs(seed: int = 0) -> dict:
    key = jax.random.key(seed)
    ks = iter(jax.random.split(key, 32))
    L = DEPTH_2

    def nrm(shape, scale):
        return jax.random.normal(next(ks), shape, jnp.float32) * scale

    def uni(shape, lo, hi):
        return jax.random.uniform(next(ks), shape, jnp.float32, lo, hi)

    return {
        'x': nrm((BATCH, SEQ, D_MODEL), 1.0),
        'positions': jnp.tile(jnp.arange(SEQ, dtype=jnp.int32)[None, :], (BATCH, 1)),
        'attn_norm_g': 1.0 + nrm((L, D_MODEL), 0.02),
        'w_in': nrm((L, D_MODEL, P_TOTAL), D_MODEL ** -0.5),
        'a_mu': uni((L, A_PROJ), 0.0, 1.0),
        'a_w0': uni((L, A_WIDTH), -6.0, -1.0),
        'a_decay_up': nrm((L, A_DECAY_LORA, A_WIDTH), 0.5 * A_DECAY_LORA ** -0.5),
        'a_a0': nrm((L, A_WIDTH), 0.1),
        'a_iclr_up': nrm((L, A_ICLR_LORA, A_WIDTH), A_ICLR_LORA ** -0.5),
        'a_gate_up': nrm((L, A_GATE_LORA, A_WIDTH), A_GATE_LORA ** -0.5),
        'a_k_k': 0.85 + nrm((L, A_WIDTH), 0.02),
        'a_k_a': 1.0 + nrm((L, A_WIDTH), 0.02),
        'a_r_k': nrm((L, A_HEADS, A_HEAD_DIM), 0.1),
        'a_ln_w': 1.0 + nrm((L, A_WIDTH), 0.02),
        'a_ln_b': nrm((L, A_WIDTH), 0.02),
        'c_q_norm_g': 1.0 + nrm((L, C_Q_LORA), 0.02),
        'c_kv_norm_g': 1.0 + nrm((L, C_KV_LORA), 0.02),
        'c_w_uq': nrm((L, C_Q_LORA, C_HEADS * (C_NOPE_DIM + C_ROPE_DIM)), C_Q_LORA ** -0.5),
        'c_w_ukv': nrm((L, C_KV_LORA, C_HEADS * (C_NOPE_DIM + C_V_DIM)), C_KV_LORA ** -0.5),
        'w_out': nrm((L, MIX_WIDTH, D_MODEL), MIX_WIDTH ** -0.5),
        'ffn_norm_g': 1.0 + nrm((L, D_MODEL), 0.02),
        'ffn_w_gate': nrm((L, D_MODEL, D_FF_2), D_MODEL ** -0.5),
        'ffn_w_up': nrm((L, D_MODEL, D_FF_2), D_MODEL ** -0.5),
        'ffn_w_down': nrm((L, D_FF_2, D_MODEL), D_FF_2 ** -0.5),
        'final_norm_g': 1.0 + nrm((D_MODEL,), 0.02),
    }

def second_block(x, positions, attn_norm_g, w_in, a_mu, a_w0, a_decay_up, a_a0, a_iclr_up,
              a_gate_up, a_k_k, a_k_a, a_r_k, a_ln_w, a_ln_b, c_q_norm_g, c_kv_norm_g,
              c_w_uq, c_w_ukv, w_out, ffn_norm_g, ffn_w_gate, ffn_w_up, ffn_w_down,
              final_norm_g):
    cos_b, sin_b = rope_tables(positions, B_ROT_DIM)
    cos_c, sin_c = rope_tables(positions, C_ROPE_DIM)
    for l in range(DEPTH_2):
        h = rms_norm_2(x, attn_norm_g[l])
        pa, pb, pc = split_sizes(h @ w_in[l], (A_PROJ, B_PROJ, C_PROJ))
        ya = rwkv7_mixer(pa, a_mu[l], a_w0[l], a_decay_up[l], a_a0[l], a_iclr_up[l],
                         a_gate_up[l], a_k_k[l], a_k_a[l], a_r_k[l], a_ln_w[l], a_ln_b[l])
        yb = dilated_mixer(pb, cos_b, sin_b)
        yc = mla_mixer(pc, cos_c, sin_c, c_q_norm_g[l], c_kv_norm_g[l], c_w_uq[l], c_w_ukv[l])
        x = x + jnp.concatenate([ya, yb, yc], axis=-1) @ w_out[l]
        h = rms_norm_2(x, ffn_norm_g[l])
        x = x + (jax.nn.silu(h @ ffn_w_gate[l]) * (h @ ffn_w_up[l])) @ ffn_w_down[l]
    return rms_norm_2(x, final_norm_g)


def setup_inputs(seed=0):
    out = dict(first_inputs(seed))
    for name, value in second_inputs(seed + 1).items():
        if name != "x":
            out[name + "_2"] = value
    return out


def reference(
    x, pre_mix_norm, post_mix_norm, pre_ffn_norm, post_ffn_norm, w_in, w_out, lru_conv_w,
    lru_conv_b, lru_wa, lru_ba, lru_wx, lru_bx, lru_lambda, gla_gate_w2, gla_gate_b, gla_norm,
    rel_bias, w_ffn_gate, w_ffn_up, w_ffn_down, positions_2, attn_norm_g_2, w_in_2, a_mu_2,
    a_w0_2, a_decay_up_2, a_a0_2, a_iclr_up_2, a_gate_up_2, a_k_k_2, a_k_a_2, a_r_k_2, a_ln_w_2,
    a_ln_b_2, c_q_norm_g_2, c_kv_norm_g_2, c_w_uq_2, c_w_ukv_2, w_out_2, ffn_norm_g_2,
    ffn_w_gate_2, ffn_w_up_2, ffn_w_down_2, final_norm_g_2,
):
    x = first_block(
        x, pre_mix_norm, post_mix_norm, pre_ffn_norm, post_ffn_norm, w_in, w_out, lru_conv_w,
        lru_conv_b, lru_wa, lru_ba, lru_wx, lru_bx, lru_lambda, gla_gate_w2, gla_gate_b,
        gla_norm, rel_bias, w_ffn_gate, w_ffn_up, w_ffn_down,
    )
    return second_block(
        x, positions_2, attn_norm_g_2, w_in_2, a_mu_2, a_w0_2, a_decay_up_2, a_a0_2,
        a_iclr_up_2, a_gate_up_2, a_k_k_2, a_k_a_2, a_r_k_2, a_ln_w_2, a_ln_b_2, c_q_norm_g_2,
        c_kv_norm_g_2, c_w_uq_2, c_w_ukv_2, w_out_2, ffn_norm_g_2, ffn_w_gate_2, ffn_w_up_2,
        ffn_w_down_2, final_norm_g_2,
    )


_drawn_inputs = setup_inputs


def setup_inputs(seed=0):
    import zlib

    import numpy as np

    out = dict(_drawn_inputs(seed))
    spreads = {}
    factors = {'post_mix_norm': 2.871,
     'pre_ffn_norm': 3.108,
     'post_ffn_norm': 4.24,
     'lru_ba': 21.903,
     'lru_bx': 8.0,
     'gla_gate_b': 8.0,
     'gla_norm': 3.647,
     'attn_norm_g_2': 5.274,
     'a_decay_up_2': 8.0,
     'a_a0_2': 6.247,
     'a_k_k_2': 200.0,
     'a_k_a_2': 8.0,
     'a_ln_w_2': 200.0,
     'a_ln_b_2': 200.0,
     'c_q_norm_g_2': 8.0,
     'c_kv_norm_g_2': 26.697,
     'ffn_norm_g_2': 21.011,
     'final_norm_g_2': 22.992}
    for name, (base, spread) in spreads.items():
        noise = np.random.default_rng([zlib.crc32(name.encode()), seed]).standard_normal(out[name].shape)
        drawn = base * np.exp(spread * noise) if base else spread * noise
        out[name] = __import__('jax').numpy.asarray(drawn.astype(out[name].dtype))
    for name, factor in factors.items():
        out[name] = (out[name] * factor).astype(out[name].dtype)
    return out
```

```python
import math
from contextlib import ExitStack

import numpy as np

import concourse.bass as bass
from concourse import mybir

ALU = mybir.AluOpType
ACT = mybir.ActivationFunctionType
AX = mybir.AxisListType
F32 = mybir.dt.float32
F32R = mybir.dt.float32r
I32 = mybir.dt.int32
U32 = mybir.dt.uint32

P = 128
D = 1024
KT = D // P
T = 256
TT = T // P
D_FF = 2816
FT = D_FF // P
CH = 2048
RING = 3
NEG = -1e30
EPS = 1e-6
LAYERS = 3

B1_SPLITS = dict(lru_x=256, lru_g=256, gq=128, gk=128, gv=256, g_lr=16, g_out=256, mq=512, mk=512, mv=512)
B2_SPLITS = dict(r=256, k=256, v=256, xw=64, xa=64, xg=160, bq=256, bk=256, bv=256, cq=256, ckv=128, kr=64)


def columns(splits):
    at, out = 0, {}
    for name, width in splits.items():
        out[name] = at
        at += width
    return out


C1, C2 = columns(B1_SPLITS), columns(B2_SPLITS)


def span(c, name, a, b):
    return (c[name] + a, c[name] + b)


IN1 = [
    [span(C1, "lru_x", 0, 256)],
    [span(C1, "g_lr", 0, 16), span(C1, "gk", 0, 128)],
    [span(C1, "gq", 0, 128), span(C1, "mq", 0, 128)],
    [span(C1, "gv", 0, 256)],
    [span(C1, "lru_g", 0, 256)],
    [span(C1, "g_out", 0, 256)],
    [span(C1, "mk", 0, 256)],
    [span(C1, "mq", 128, 384)],
    [span(C1, "mk", 256, 512)],
    [span(C1, "mq", 384, 512)],
    [span(C1, "mv", 0, 256)],
    [span(C1, "mv", 256, 512)],
]
IN2 = [
    [span(C2, "xw", 0, 64), span(C2, "xa", 0, 64), span(C2, "xg", 0, 128)],
    [span(C2, "k", 0, 256)],
    [span(C2, "r", 0, 256)],
    [span(C2, "v", 0, 256)],
    [span(C2, "kr", 0, 64), span(C2, "xg", 128, 160), span(C2, "ckv", 0, 128)],
    [span(C2, "cq", 0, 256)],
    [span(C2, "bq", 0, 256)],
    [span(C2, "bk", 0, 256)],
    [span(C2, "bv", 0, 256)],
]


def stream():
    out = []
    for l in range(LAYERS):
        for i, spans in enumerate(IN1 if l == 0 else IN2):
            out.append((l, "in", i, KT * sum(b - a for a, b in spans)))
        if l:
            out += [(l, "uq", 0, 2 * 768), (l, "ukv", 0, 1024)]
        out += [(l, "out", i, CH) for i in range(4)]
        out += [(l, "gu", 0, CH), (l, "gu", 1, CH)]
        for p in range(1, FT // 2):
            out += [(l, "gu", 2 * p, CH), (l, "gu", 2 * p + 1, CH), (l, "down", p - 1, CH)]
        out.append((l, "down", FT // 2 - 1, CH))
    return out


STREAM = stream()
NCH = len(STREAM)
CHUNK = {(l, kind, i): n for n, (l, kind, i, _) in enumerate(STREAM)}

CONSTS = {}


def t5_bucket(n):
    n = np.maximum(n, 0)
    nf = np.maximum(n, 1).astype(np.float32)
    large = 16 + (np.log(nf / 16).astype(np.float32) / np.float32(math.log(8)) * 16).astype(np.int32)
    return np.where(n < 16, n, np.minimum(large, 31))


def block_ones(size):
    i = np.arange(P) // size
    return (i[:, None] == i[None, :]).astype(np.float32)


def constants():
    i = np.arange(P)
    out = {"ident": np.eye(P), "ones": np.ones((P, P)), "bones": block_ones(64)}
    out["gla_mask"] = block_ones(64) * (i[:, None] <= i[None, :])
    out["flip"] = np.eye(P)[::-1]
    out["before"] = np.stack([i[:, None] < i[None, :], i[:, None] <= i[None, :]], 1).reshape(P, 2 * P)
    for n in range(7):
        b = i >> n
        out[f"level{n}"] = (b[None, :] % 2 == 1) & (b[:, None] == b[None, :] - 1)
    q = np.concatenate([np.tile(P + i[:, None], (1, T)), np.tile(i[:, None], (1, P))], 1)
    k = np.concatenate([np.tile(np.arange(T), (P, 1)), np.tile(i, (P, 1))], 1)
    dist = q - k
    out["causal"] = np.where(dist >= 0, 0.0, NEG)
    count = (dist <= 128).astype(int) + (dist % 4 == 0) + (dist % 16 == 0)
    out["dilated"] = np.where((dist >= 0) & (count > 0), np.log(np.maximum(count, 1)), NEG)
    rb, rc = np.zeros((P, P)), np.zeros((P, P))
    for h in (0, 64):
        for j in range(8):
            rb[h + j + 8, h + j], rb[h + j, h + j + 8] = -1, 1
        for j in range(32):
            rc[h + j + 32, h + j], rc[h + j, h + j + 32] = -1, 1
    dup = np.zeros((P, P))
    dup[i % 64, i] = 1
    out |= {"rot_b": rb, "rot_c": rc, "dup": dup}
    dupr = np.zeros((P, P))
    dupr[:64] = rc[:64, :64] @ dup[:64]
    out["dup_rot"] = dupr
    freq = np.zeros((P, 4), np.float32)
    for h in (0, 64):
        for j in range(8):
            freq[[h + j, h + j + 8], 0] = np.float32(1.0) / np.float32(500000.0) ** np.float32(2 * j / 16)
        for j in range(32):
            freq[[h + j, h + j + 32], 1] = np.float32(1.0) / np.float32(500000.0) ** np.float32(2 * j / 64)
    freq[:, 2], freq[:, 3] = EPS, 64e-5
    out["freq"] = freq
    return {k: np.asarray(v, np.float32) for k, v in out.items()}


def offsets(widths):
    at, out = 0, {}
    for name, width in widths:
        out[name] = (at, at + width)
        at += width
    return out, at


CONST_ARRAYS = constants()
CONST_AT, NCONST = offsets([(k, v.shape[1]) for k, v in CONST_ARRAYS.items()])
PAR_AT, NPAR = offsets([("pre_mix", 8), ("post_mix", 8), ("pre_ffn", 8), ("post_ffn", 8), ("conv_w", 8),
                        ("conv_b", 2), ("ba", 2), ("bx", 2), ("lam", 2), ("gate_b", 1), ("gla_norm", 2)]
                       + [(f"{n}{l}", w) for l in (1, 2) for n, w in
                          (("attn", 8), ("mu", 9), ("w0", 2), ("a0", 2), ("k_k", 2), ("k_a", 2), ("r_k", 2),
                           ("ln_w", 2), ("ln_b", 2), ("qn", 2), ("kvn", 1), ("ffn", 8))]
                       + [("final", 8)])
MAT1_AT, NMAT1 = offsets([("wa", 256), ("wx", 256), ("gate_w2", 128), ("rel", 8)])
MAT2_AT, NMAT2 = offsets([("lora", 256), ("gate_up", 256), ("gate_up2", 256)])
NMAT = max(NMAT1, NMAT2)


class Steps:

    def __init__(self, sem, names):
        self.sem, self.names, self.n = sem, names or [], 0
        self.value = {name: i + 1 for i, name in enumerate(self.names)}
        self.log = []

    def at(self, *name):
        name = "_".join(map(str, name))
        return self.value[name] if self.names else 1

    def mark(self, *name):
        name = "_".join(map(str, name))
        self.log.append(name)
        if self.names:
            assert self.names[self.n] == name, (self.names[self.n], name)
        self.n += 1
        return 1


def program(nc, ins, out, plan):
    with ExitStack() as ctx:
        def sb(name, shape, dt=F32):
            return ctx.enter_context(nc.sbuf_tensor(name, shape, dt))

        def sem(name):
            return ctx.enter_context(nc.semaphore(name))

        x = sb("x", [P, KT, T])
        h_hi, h_lo = sb("h_hi", [P, KT, T], F32R), sb("h_lo", [P, KT, T], F32R)
        mix_hi, mix_lo = sb("mix_hi", [P, KT, T], F32R), sb("mix_lo", [P, KT, T], F32R)
        raw = sb("raw", [P, RING, CH])
        w_hi, w_lo = sb("w_hi", [P, RING, CH], F32R), sb("w_lo", [P, RING, CH], F32R)
        cst = sb("cst", [P, NCONST])
        par = sb("par", [P, NPAR])
        mat = sb("mat", [P, NMAT])
        rope = sb("rope", [P, 4, T])
        rstd = sb("rstd", [P, T])
        rstd_col = sb("rstd_col", [P, TT])
        ARENA = 18688
        arena = sb("arena", [P, ARENA])
        bank = [ctx.enter_context(nc.psum_tensor(f"bank{i}", [P, 512], F32)) for i in range(8)]

        def pairs(b):
            return bank[b][:, :].rearrange("p (a t) -> p a t", a=2)

        def quads(b):
            return bank[b][:, :].rearrange("p (a t) -> p a t", a=4)

        def C(name):
            a, b = CONST_AT[name]
            return cst[:, a:b]

        def Par(name, i=None, j=None):
            a, b = PAR_AT[name]
            return par[:, a:b] if i is None else par[:, a + i:a + (i + 1 if j is None else j)]

        def area(*tiles):
            at, views = tiles[0], {}
            for name, shape in tiles[1].items():
                n = int(np.prod(shape))
                v = arena[:, at:at + n]
                if len(shape) == 2:
                    v = v.rearrange("p (a b) -> p a b", a=shape[0])
                if len(shape) == 3:
                    v = v.rearrange("p (a b c) -> p a b c", a=shape[0], b=shape[1])
                if len(shape) == 4:
                    v = v.rearrange("p (a b c d) -> p a b c d", a=shape[0], b=shape[1], c=shape[2])
                views[name] = v
                at += n
            assert at <= ARENA, (at, list(tiles[1]))
            return views, at

        NORM, _ = area(ARENA - 4096, dict(xg=(KT, T), sq=(KT, T)))
        xg, sq = NORM["xg"], NORM["sq"]
        FF, _ = area(0, dict(gu=(2, 2, T), sg=(2, T), act=(2, T)))
        act_hi, act_lo = mix_hi[:, 0:4, :], mix_lo[:, 0:4, :]
        B1, _ = area(0, dict(
            lx=(2, 259), lg=(2, T), glr=(T,), gk=(T,), gq=(T,), gv=(TT, T), gout=(2, T), mq=(4, T), mk=(4, T),
            mv=(TT, 512), bias=(8, T), lru=(6, 512), qm=(4, T), kd=(T,), ke=(T,), g0=(T,), g1=(T,), g2=(T,),
            keT=(TT, P), att=(TT, 512), st=(3, T), go=(2, T), gt=(2, T), att_l=(2, 384), att_p=(2, 384)))
        REL, _ = area(T, dict(onehot=(384,), relrow=(384,), relneg=(384,), hankel=(8, T)))
        B2, at2 = area(0, dict(
            pm=(9, T), a=(2, T), kkn=(2, T), gate=(2, T), kp=(2, T), kr=(2, 2, 2, P), bh=(2, T), kh=(2, T),
            vt=(TT, T), kbt=(2, T), rs=(T,), nsa=(2, T), s1=(2, P), y=(2, T),
            bq=(2, T), bk=(2, T), bv=(TT, T), cq=(2, T), ckv=(T,), krope=(T,)))
        G2, at3 = area(at2, dict(gram=(8, 4, P)))
        PF, _ = area(at2, dict(pf=(9, 257)))
        INV, _ = area(at3, dict(x=(8, P), xt=(8, P), bt=(8, P)))
        INV["yy"] = area(9 * T, dict(yy=(8, P)))[0]["yy"]
        EARLY, _ = area(at3, dict(sg=(2, T), cs=(2, T), cx=(2, T), ep=(2, T), en=(2, T), t0=(2, T)))
        AT2, _ = area(at2, dict(cqs=(2, T), ckvs=(T,), rq=(T,), rkv=(T,), cqn=(2, T),
                                ckvn=(T,), qn=(4, T), qr=(2, T), kn=(4, T), kro=(T,), cv=(TT, 512)))
        AT2 |= area(0, dict(t0=(2, T), t1=(2, T), att_l=(2, 384), att_p=(2, 384)))[0]
        cq_hi, cq_lo = h_hi[:, 0:3, :], h_lo[:, 0:3, :]
        small = sb("small", [P, 96])
        pos = arena[:, 0:T].bitcast(I32)

        loaded = [sem(f"weights_loaded{i}") for i in range(RING)]
        hi_pool, hi_act = sem("hi_split_by_gpsimd"), sem("hi_split_by_scalar")
        lo_pool, lo_dve = sem("lo_split_by_gpsimd"), sem("lo_split_by_vector")
        tables = sem("tables_loaded")
        positions = sem("positions_loaded")
        mats = sem("mixer_matrices_loaded")
        rel_out, rel_in = sem("bias_row_stored"), sem("bias_hankel_loaded")
        stored = sem("output_stored")
        V = Steps(sem("vector_step"), plan.get("V"))
        A = Steps(sem("scalar_step"), plan.get("A"))
        M = Steps(sem("tensor_step"), plan.get("M"))

        onehot_in, rel_scratch = ins["onehot"], ins["scratch"]

        by_act = [kind in ("gu", "down") for _, kind, _, _ in STREAM]
        n_hi = [sum(b == by_act[n] for b in by_act[:n + 1]) for n in range(NCH)]

        def split(engine, c):
            engine.wait_ge(lo_dve if by_act[c] else lo_pool, n_hi[c])

        def released(c):
            l, kind, i, _ = STREAM[c]
            return M.at(l, *{"in": ("in", i), "uq": ("up", 2), "ukv": ("up", 6), "out": ("mixed", i),
                             "gu": ("gu", i), "down": ("down", i)}[kind])

        block = ctx.enter_context(nc.Block())

        @block.sync
        def _(sp):
            sp.dma_start(cst[:, :], ins["consts"]).then_inc(tables, 16)
            sp.dma_start(par[:, :], ins["params"]).then_inc(tables, 16)
            sp.dma_start(x[:, :, :], ins["x"].rearrange("p (k t) -> p k t", k=KT)).then_inc(tables, 16)
            for c, (l, kind, i, n) in enumerate(STREAM):
                if c >= RING:
                    split(sp, c - RING)
                sp.dma_start(raw[:, c % RING, 0:n], ins["w"][c, :, 0:n]).then_inc(loaded[c % RING], 16)

        @block.gpsimd
        def _(pool):
            pool.dma_start(pos, ins["pos"]).then_inc(positions, 16)
            pool.dma_start(mat[:, 0:NMAT1], ins["mat"][0, :, 0:NMAT1]).then_inc(mats, 16)
            pool.dma_start(REL["onehot"][0:32, :], ins["onehot"][0:32, :]).then_inc(positions, 16)
            pool.dma_start(REL["relneg"][0:8, :], ins["onehot"][32:40, :]).then_inc(positions, 16)
            pool.wait_ge(V.sem, V.at("rel_row"))
            pool.dma_start(rel_scratch, REL["relrow"][0:8, :]).then_inc(rel_out, 16)
            pool.wait_ge(rel_out, 16)
            pool.dma_start(REL["hankel"], ins["hankel"]).then_inc(rel_in, 16)
            for c, (l, kind, i, n) in enumerate(STREAM):
                s = c % RING
                if by_act[c]:
                    continue
                pool.wait_ge(loaded[s], 16 * (c // RING + 1))
                if c >= RING:
                    pool.wait_ge(M.sem, released(c - RING))
                pool.tensor_scalar(w_hi[:, s, 0:n], raw[:, s, 0:n], 1.0, None, ALU.mult).then_inc(hi_pool, 1)
                pool.wait_ge(hi_pool, n_hi[c])
                pool.tensor_tensor(w_lo[:, s, 0:n], raw[:, s, 0:n], w_hi[:, s, 0:n].bitcast(F32),
                                   ALU.subtract).then_inc(lo_pool, 1)
                if kind == "out" and i == 3 and l + 1 < LAYERS:
                    pool.wait_ge(M.sem, released(c))
                    pool.dma_start(mat[:, 0:NMAT2], ins["mat"][l + 1, :, 0:NMAT2]).then_inc(mats, 16)

        @block.tensor
        def _(pe):
            def weights(c, view):
                s = c % RING
                return view(w_hi[:, s, :]), view(w_lo[:, s, :])

            def product(dst, w, k_tiles, act, start=True, stop=True, loose=False):
                n = len(k_tiles)
                for i, k in enumerate(k_tiles):
                    for j, (a, b) in enumerate(((0, 0), (0, 1), (1, 0))):
                        last = pe.matmul(dst, w[a](k), act[b](k), start=start and i == 0 and j == 0,
                                         stop=stop and i == n - 1 and j == 2, skip_group_check=loose)
                return last

            def tile_of(c, k_tiles, width, at, size=P):
                s = c % RING
                return [lambda k, part=part: part[:, s, k * width + at:k * width + at + size]
                        for part in (w_hi, w_lo)]

            H = [lambda k: h_hi[:, k, :], lambda k: h_lo[:, k, :]]
            MX = [lambda k: mix_hi[:, k, :], lambda k: mix_lo[:, k, :]]
            IDENT, ONES, BONES = C("ident"), C("ones"), C("bones")

            def norm_sum(l, what, into=6):
                for k in range(KT):
                    if k % 2 == 0 and what in ("mixed", "fed"):
                        pe.wait_ge(A.sem, A.at(l, what, "sq", k // 2))
                    last = pe.matmul(bank[into][:, 0:T], ONES, sq[:, k, :], start=(k == 0), stop=(k == KT - 1))
                last.then_inc(M.sem, M.mark(l, what, "sum"))

            def project(l, *which):
                for i in which:
                    if i == 0:
                        pe.wait_ge(V.sem, V.at(l, "in", "lo", 1))
                    c = CHUNK[l, "in", i]
                    width = STREAM[c][3] // KT
                    split(pe, c)
                    b = 4 + i % 2
                    if i >= 2:
                        pe.wait_ge(V.sem, V.at(l, "in", i - 2))
                    token_major = i in ((3, 10, 11) if l == 0 else (8,))
                    if token_major:
                        s = c % RING
                        for t in range(TT):
                            last = product(pairs(b)[:, t, 0:width],
                                           [lambda k, p=p: p[:, k, t * P:(t + 1) * P] for p in (h_hi, h_lo)],
                                           range(KT),
                                           [lambda k, p=p: p[:, s, k * width:(k + 1) * width] for p in (w_hi, w_lo)])
                    else:
                        for t in range(2 if width > P else 1):
                            at = t * P if width == 2 * P else t * (width - P)
                            last = product(pairs(b)[:, t, :], tile_of(c, KT, width, at), range(KT), H)
                    last.then_inc(M.sem, M.mark(l, "in", i))
                    if i == 0:
                        pe.wait_ge(A.sem, A.at(l, "in", "sq"))
                        norm_sum(l, "in")
                    if i == 1:
                        pe.wait_ge(A.sem, A.at(l, "in", "rstd"))
                        for t in range(TT):
                            last = pe.transpose(bank[7][:, t * P:(t + 1) * P], rstd[:, t * P:(t + 1) * P], IDENT)
                        last.then_inc(M.sem, M.mark(l, "in", "rstd"))

            def attention(l, tag, heads, scores, value, out_bank, masks=None):
                v = B1 if l == 0 else AT2
                for i in range(heads + 2):
                    if i < heads:
                        if i >= 2:
                            pe.wait_ge(V.sem, V.at(l, tag, "logits", i - 2))
                        scores(i, bank[i % 2]).then_inc(M.sem, M.mark(l, tag, "scores", i))
                    if 1 <= i <= heads:
                        j = i - 1
                        pe.wait_ge(V.sem, V.at(l, tag, "probs", j))
                        if j >= 2:
                            pe.wait_ge(A.sem, A.at(l, tag, "turned", j - 2))
                        L, b = v["att_l"][:, j % 2, :], bank[2 + j % 2]
                        pe.transpose(b[:, 0:P], L[:, 2 * P:3 * P], IDENT)
                        pe.transpose(b[:, P:2 * P], L[:, 0:P], IDENT)
                        pe.transpose(b[:, 2 * P:3 * P], L[:, P:2 * P], IDENT)\
                            .then_inc(M.sem, M.mark(l, tag, "turn", j))
                    if i >= 2:
                        j = i - 2
                        pe.wait_ge(A.sem, A.at(l, tag, "turned", j))
                        PT = v["att_p"][:, j % 2, :]
                        dst = out_bank(j)
                        pe.matmul(dst, value(j, 0), PT[:, 0:T], start=True, stop=False)
                        pe.matmul(dst[:, P:T], value(j, 1), PT[:, T:T + P], start=False, stop=True)\
                            .then_inc(M.sem, M.mark(l, tag, "values", j))

            def w_out(l):
                for m in range(4):
                    c = CHUNK[l, "out", m]
                    split(pe, c)
                    for t in range(2):
                        last = product(pairs(m)[:, t, :], tile_of(c, KT, 2 * P, t * P), range(KT), MX)
                    last.then_inc(M.sem, M.mark(l, "mixed", m))

            def ffn(l):
                def gate_up(j):
                    c = CHUNK[l, "gu", j]
                    split(pe, c)
                    if j >= 2:
                        pe.wait_ge(V.sem, V.at(l, "gu", j - 2))
                    for t in range(2):
                        last = product(pairs(4 + j % 2)[:, t, :], tile_of(c, KT, 2 * P, t * P), range(KT), H)
                    last.then_inc(M.sem, M.mark(l, "gu", j))
                    if j == 1:
                        norm_sum(l, "ffn")

                def down(p):
                    c = CHUNK[l, "down", p]
                    split(pe, c)
                    for s in range(2):
                        j = 2 * p + s
                        pe.wait_ge(V.sem, V.at(l, "act", "lo", j))
                        for d in range(KT):
                            last = product(pairs(d // 2)[:, d % 2, :], tile_of(c, 2, D, d * P), [s],
                                           [lambda k, q=q: q[:, j % 4, :] for q in (act_hi, act_lo)],
                                           start=(j == 0 and d % 2 == 0), stop=(j == FT - 1), loose=True)
                    last.then_inc(M.sem, M.mark(l, "down", p))

                pe.wait_ge(V.sem, V.at(l, "ffn", "lo", 1))
                pe.wait_ge(A.sem, A.at(l, "ffn", "sq"))
                gate_up(0)
                gate_up(1)
                for p in range(1, FT // 2):
                    gate_up(2 * p)
                    gate_up(2 * p + 1)
                    down(p - 1)
                down(FT // 2 - 1)

            def block1():
                l = 0
                Mt = lambda n: mat[:, MAT1_AT[n][0]:MAT1_AT[n][1]]
                project(l, 0, 1)
                pe.wait_ge(V.sem, V.at(l, "in", 1))
                pe.matmul(bank[6][:, 0:T], Mt("gate_w2")[0:16, :], B1["glr"][0:16, :], start=True, stop=True)\
                    .then_inc(M.sem, M.mark("gla_gate"))
                project(l, 2, 3)
                pe.wait_ge(V.sem, V.at("lru_conv"))
                for b, name in ((0, "wa"), (1, "wx")):
                    for t in range(2):
                        last = pe.matmul(pairs(b)[:, t, :], Mt(name)[:, t * P:(t + 1) * P],
                                         B1["lru"][:, 0, t * T:(t + 1) * T], start=True, stop=True)
                last.then_inc(M.sem, M.mark("lru_gates"))
                project(l, 4, 5)
                pe.wait_ge(V.sem, V.at("gla_ke"))
                for t in range(TT):
                    last = pe.matmul(bank[2 + t][:, :].rearrange("p (h t) -> p h t", h=4), B1["kd"][:, t * P:(t + 1) * P],
                                     B1["qm"][:, :, t * P:(t + 1) * P], start=True, stop=True)
                last.then_inc(M.sem, M.mark("gla_scores"))
                for t in range(TT):
                    last = pe.transpose(bank[6][:, t * P:(t + 1) * P], B1["ke"][:, t * P:(t + 1) * P], IDENT)
                last.then_inc(M.sem, M.mark("gla_turn"))
                project(l, 6)
                pe.wait_ge(A.sem, A.at("gla_turned"))
                pe.wait_ge(A.sem, A.at("lru_sig"))
                for n in range(3):
                    half = slice(64 * (n % 2), 64 * (n % 2) + 64)
                    dst = bank[7][:, 0:T] if n == 1 else pairs(0)[:, n // 2, :]
                    last = pe.matmul(dst, B1["keT"][half, n // 2, :], B1["gv"][half, n // 2, :], start=True, stop=True)
                last.then_inc(M.sem, M.mark("gla_kv"))
                project(l, 7)
                pe.wait_ge(V.sem, V.at("gla_att", 1))
                pe.wait_ge(V.sem, V.at("gla_state", 2))
                for pr in range(2):
                    for t in range(TT):
                        for s in range(2):
                            h = 2 * pr + s
                            dst = bank[1][64 * s:64 * s + 64, pr * T + t * P:pr * T + (t + 1) * P]
                            pe.matmul(dst, B1["gv"][:, t, h * 64:(h + 1) * 64],
                                      B1["att"][:, t, h * P:(h + 1) * P], start=True, stop=False)
                            for n in range(2 * t, 2 * t + 2):
                                if n:
                                    last = pe.matmul(dst[:, (n % 2) * 64:(n % 2) * 64 + 64],
                                                     B1["st"][:, n - 1, h * 64:(h + 1) * 64],
                                                     B1["qm"][:, h, n * 64:(n + 1) * 64], start=False,
                                                     stop=(n % 2 == 1))
                last.then_inc(M.sem, M.mark("gla_out"))
                project(l, 8)
                pe.wait_ge(A.sem, A.at("gla_sq"))
                pe.matmul(bank[0][:, :], BONES, B1["gt"].rearrange("p a b -> p (a b)"), start=True, stop=True)\
                    .then_inc(M.sem, M.mark("gla_ss"))

                project(l, 9, 10, 11)
                pe.wait_ge(A.sem, A.at("gla_rstd"))
                pe.wait_ge(V.sem, V.at(l, "in", 11))

                def scores(i, b):
                    rows = slice(64 * (i % 2), 64 * (i % 2) + 64)
                    q, k = B1["mq"][rows, i // 2, :], B1["mk"][rows, i // 2, :]
                    pe.matmul(b[:, 0:T], q[:, P:T], k, start=True, stop=True)
                    return pe.matmul(b[:, T:T + P], q[:, 0:P], k[:, 0:P], start=True, stop=True)

                def out_bank(j):
                    return pairs(6 + j // 4)[64 * (j % 2):64 * (j % 2) + 64, (j // 2) % 2, :]

                attention(l, "moba", 8, scores, lambda j, t: B1["mv"][:, t, j * 64:(j + 1) * 64], out_bank)

            def rwkv(l):
                Mt = lambda n: mat[:, MAT2_AT[n][0]:MAT2_AT[n][1]]
                pm, kr, bh, kh, gram = B2["pm"], B2["kr"], B2["bh"], B2["kh"], G2["gram"]
                project(l, 0, 1)
                pe.wait_ge(A.sem, A.at(l, "lora_in"))
                for t in range(2):
                    pe.matmul(pairs(0)[:, t, :], Mt("lora")[0:64, t * P:(t + 1) * P], pm[0:64, 0, :],
                              start=True, stop=True)
                for t in range(2):
                    last = pe.matmul(pairs(1)[:, t, :], Mt("lora")[64:128, t * P:(t + 1) * P], pm[64:128, 0, :],
                                     start=True, stop=True)
                last.then_inc(M.sem, M.mark(l, "lora"))
                project(l, 2)
                pe.wait_ge(A.sem, A.at(l, "kk_sq"))
                pe.matmul(bank[3][:, :], BONES, EARLY["t0"].rearrange("p a b -> p (a b)"), start=True, stop=True)\
                    .then_inc(M.sem, M.mark(l, "kk_ss"))
                project(l, 3, 4)
                pe.wait_ge(A.sem, A.at(l, "gate_in"))
                for t in range(2):
                    pe.matmul(pairs(2)[:, t, :], Mt("gate_up")[:, t * P:(t + 1) * P], pm[:, 1, :],
                              start=True, stop=False)
                    last = pe.matmul(pairs(2)[:, t, :], Mt("gate_up2")[64:96, t * P:(t + 1) * P], pm[64:96, 8, :],
                                     start=False, stop=True)
                last.then_inc(M.sem, M.mark(l, "gate"))
                for c in range(TT):
                    for t in range(2):
                        last = pe.transpose(bank[6][:, c * T + t * P:c * T + (t + 1) * P],
                                            pm[:, 6 + t, c * P:(c + 1) * P], IDENT)
                last.then_inc(M.sem, M.mark(l, "v_turn"))
                project(l, 5)
                pe.wait_ge(V.sem, V.at(l, "kr"))
                for n, m in enumerate((kh, bh)):
                    for t in range(2):
                        last = pe.transpose(bank[7][:, n * T + t * P:n * T + (t + 1) * P], m[:, t, 0:P], IDENT)
                last.then_inc(M.sem, M.mark(l, "kb_turn"))
                for g in range(8):
                    c, t, rows = g // 4, (g % 4) // 2, slice(64 * (g % 2), 64 * (g % 2) + 64)
                    if g >= 4:
                        pe.wait_ge(V.sem, V.at(l, "gram", g - 4))
                    elif g == 2:
                        pe.wait_ge(A.sem, A.at(l, "gate"))
                    for n, m in enumerate((bh, kh)):
                        last = pe.matmul(pairs(g % 4)[:, n, :], m[rows, t, c * P:(c + 1) * P],
                                         kr[rows, t, c, :, :].rearrange("p a b -> p (a b)"), start=True, stop=True)
                    last.then_inc(M.sem, M.mark(l, "gram", g))
                project(l, 6)
                Xm, XT, BT, Y = INV["x"], INV["xt"], INV["bt"], INV["yy"]
                for q in range(2):
                    pe.wait_ge(V.sem, V.at(l, "inv0", q))
                    for m in range(4):
                        last = pe.transpose(bank[q][:, m * P:(m + 1) * P], XT[:, 4 * q + m, :], IDENT)
                    last.then_inc(M.sem, M.mark(l, "inv0", q))
                for n in range(1, 7):
                    for q in range(2):
                        pe.wait_ge(V.sem, V.at(l, "inv_bt", n, q))
                        pe.wait_ge(A.sem, A.at(l, "inv0", q)) if n == 1 else pe.wait_ge(V.sem, V.at(l, "inv_x", n - 1, q))
                        for m in range(4 * q, 4 * q + 4):
                            last = pe.matmul(quads(q)[:, m % 4, :], BT[:, m, :], Xm[:, m, :], start=True, stop=True)
                        last.then_inc(M.sem, M.mark(l, "inv_y", n, q))
                    if n <= 2:
                        project(l, 6 + n)
                    for q in range(2):
                        pe.wait_ge(A.sem, A.at(l, "inv_y", n, q))
                        for m in range(4 * q, 4 * q + 4):
                            last = pe.matmul(quads(2 + q)[:, m % 4, :], Y[:, m, :], XT[:, m, :], start=True, stop=True)
                        last.then_inc(M.sem, M.mark(l, "inv_zt", n, q))
                        if n < 6:
                            for m in range(4 * q, 4 * q + 4):
                                last = pe.matmul(quads(6 + q)[:, m % 4, :], XT[:, m, :], Y[:, m, :], start=True,
                                                 stop=True)
                            last.then_inc(M.sem, M.mark(l, "inv_z", n, q))
                vt, kbt, rs, nsa, s1 = B2["vt"], B2["kbt"], B2["rs"], B2["nsa"], B2["s1"]
                for c in range(TT):
                    pe.wait_ge(V.sem, V.at(l, "inv_xt", 6, c))
                    if c:
                        pe.wait_ge(V.sem, V.at(l, "s1"))
                    for h in range(4):
                        t, cols = h // 2, slice(h * 64, (h + 1) * 64)
                        if c and h % 2 == 0:
                            pe.matmul(bank[0][:, t * P:(t + 1) * P], kr[:, t, 1, 0, :], s1[:, t, :],
                                      start=True, stop=False)
                        last = pe.matmul(bank[0][:, cols], gram[:, 4 * c + h, 2, :], vt[:, c, cols],
                                         start=(c == 0), stop=(c == 0 or h % 2 == 1))
                    last.then_inc(M.sem, M.mark(l, "r", c))
                    pe.wait_ge(A.sem, A.at(l, "r", c))
                    for h in range(4):
                        cols = slice(h * 64, (h + 1) * 64)
                        last = pe.matmul(bank[1][:, cols], INV["xt"][:, 4 * c + h, :], rs[:, cols],
                                         start=True, stop=True)
                    last.then_inc(M.sem, M.mark(l, "sa", c))
                    pe.wait_ge(V.sem, V.at(l, "nsa", c))
                    if c == 0:
                        for h in range(4):
                            t, rows, cols = h // 2, slice(64 * (h % 2), 64 * (h % 2) + 64), slice(h * 64, (h + 1) * 64)
                            pe.matmul(bank[2][rows, t * 64:(t + 1) * 64], kbt[:, 0, cols], vt[:, 0, cols],
                                      start=True, stop=False)
                            last = pe.matmul(bank[2][rows, t * 64:(t + 1) * 64], kbt[:, 1, cols], nsa[:, 0, cols],
                                             start=False, stop=True)
                        last.then_inc(M.sem, M.mark(l, "s1"))
                    for h in range(4):
                        t, rows, cols = h // 2, slice(64 * (h % 2), 64 * (h % 2) + 64), slice(h * 64, (h + 1) * 64)
                        both = pairs(3 if c == 0 else 6)[:, t, 0:P]
                        dst = both[rows, :]
                        if c and h % 2 == 0:
                            pe.matmul(both, s1[:, t, :], kr[:, t, 1, 1, :], start=True, stop=False)
                        pe.matmul(dst, vt[:, c, cols], gram[:, 4 * c + h, 3, :], start=(c == 0), stop=False)
                        last = pe.matmul(dst, nsa[:, c, cols], gram[:, 4 * c + h, 1, :], start=False, stop=True)
                    last.then_inc(M.sem, M.mark(l, "y", c))
                flat = lambda v: v.rearrange("p a b -> p (a b)")
                pe.wait_ge(A.sem, A.at(l, "y", 1))
                pe.matmul(bank[0][:, :], BONES, flat(B2["y"]), start=True, stop=True)\
                    .then_inc(M.sem, M.mark(l, "mean"))
                pe.wait_ge(V.sem, V.at(l, "bonus_in"))
                pe.matmul(bank[2][:, :], BONES, flat(EARLY["t0"]), start=True, stop=True)\
                    .then_inc(M.sem, M.mark(l, "bonus"))
                pe.wait_ge(A.sem, A.at(l, "y_sq"))
                pe.matmul(bank[1][:, :], BONES, flat(EARLY["sg"]), start=True, stop=True)\
                    .then_inc(M.sem, M.mark(l, "var"))

            def mla_project(l):
                b = AT2
                pe.wait_ge(A.sem, A.at(l, "c_sq"))
                pe.matmul(bank[0][:, 0:T], ONES, b["cqs"][:, 0, :], start=True, stop=False)
                pe.matmul(bank[0][:, 0:T], ONES, b["cqs"][:, 1, :], start=False, stop=True)
                pe.matmul(bank[0][:, T:2 * T], ONES, b["ckvs"], start=True, stop=True)\
                    .then_inc(M.sem, M.mark(l, "c_ss"))
                pe.wait_ge(V.sem, V.at(l, "bonus"))
                pe.wait_ge(A.sem, A.at(l, "y_rstd"))
                pe.matmul(bank[1][:, :], C("rot_b"), B2["bq"].rearrange("p a b -> p (a b)"), start=True, stop=True)
                pe.matmul(bank[2][:, :], C("rot_b"), B2["bk"].rearrange("p a b -> p (a b)"), start=True, stop=True)\
                    .then_inc(M.sem, M.mark(l, "b_rot"))
                pe.matmul(bank[3][:, 0:T], C("dup")[0:64, :], B2["krope"][0:64, :], start=True, stop=True)
                pe.matmul(bank[3][:, T:2 * T], C("dup_rot")[0:64, :], B2["krope"][0:64, :], start=True, stop=True)\
                    .then_inc(M.sem, M.mark(l, "k_rot"))
                CQ = [lambda k: cq_hi[:, k, :], lambda k: cq_lo[:, k, :]]
                CKV = [lambda k: cq_hi[:, 2, :], lambda k: cq_lo[:, 2, :]]
                pe.wait_ge(V.sem, V.at(l, "c_lo"))
                c = CHUNK[l, "uq", 0]
                split(pe, c)
                for i in range(3):
                    if i == 2:
                        pe.wait_ge(A.sem, A.at(l, "up", 0))
                    for t in range(2):
                        last = product(pairs(4 + i % 2)[:, t, :], tile_of(c, 2, 768, (2 * i + t) * P), range(2), CQ)
                    last.then_inc(M.sem, M.mark(l, "up", i))
                c = CHUNK[l, "ukv", 0]
                split(pe, c)
                for i in range(3, 5):
                    pe.wait_ge(A.sem, A.at(l, "up", i - 2))
                    for t in range(2):
                        last = product(pairs(4 + i % 2)[:, t, :], tile_of(c, 1, 1024, (2 * (i - 3) + t) * P), [0], CKV)
                    last.then_inc(M.sem, M.mark(l, "up", i))
                s = c % RING
                for t in range(TT):
                    i = 5 + t
                    pe.wait_ge(A.sem, A.at(l, "up", i - 2))
                    last = product(bank[4 + i % 2][:, :],
                                   [lambda k, p=p: p[:, 2, t * P:(t + 1) * P] for p in (cq_hi, cq_lo)], [0],
                                   [lambda k, p=p: p[:, s, 512:1024] for p in (w_hi, w_lo)])
                    last.then_inc(M.sem, M.mark(l, "up", i))
                pe.wait_ge(A.sem, A.at(l, "up", 2))
                pe.wait_ge(V.sem, V.at(l, "b_rope"))
                pe.matmul(bank[0][:, :], C("rot_c"), b["qr"].rearrange("p a b -> p (a b)"), start=True, stop=True)\
                    .then_inc(M.sem, M.mark(l, "q_rot"))

            def b_attention(l):
                def scores(i, b):
                    rows = slice(64 * (i % 2), 64 * (i % 2) + 64)
                    q, k = B2["bq"][rows, i // 2, :], B2["bk"][rows, i // 2, :]
                    pe.matmul(b[:, 0:T], q[:, P:T], k, start=True, stop=True)
                    return pe.matmul(b[:, T:T + P], q[:, 0:P], k[:, 0:P], start=True, stop=True)

                pe.wait_ge(V.sem, V.at(l, "c_rope"))
                attention(l, "dil", 4, scores, lambda j, t: B2["bv"][:, t, j * 64:(j + 1) * 64],
                          lambda j: pairs(6)[64 * (j % 2):64 * (j % 2) + 64, j // 2, :])

            def c_attention(l):
                b2 = AT2

                def scores(i, b):
                    rows = slice(64 * (i % 2), 64 * (i % 2) + 64)
                    q, k = b2["qn"][:, i, :], b2["kn"][:, i, :]
                    qr, kr = b2["qr"][rows, i // 2, :], b2["kro"][rows, :]
                    pe.matmul(b[:, 0:T], q[:, P:T], k, start=True, stop=False)
                    pe.matmul(b[:, 0:T], qr[:, P:T], kr, start=False, stop=True)
                    pe.matmul(b[:, T:T + P], q[:, 0:P], k[:, 0:P], start=True, stop=False)
                    return pe.matmul(b[:, T:T + P], qr[:, 0:P], kr[:, 0:P], start=False, stop=True)

                pe.wait_ge(A.sem, A.at(l, "up", 6))
                pe.wait_ge(V.sem, V.at(l, "dil", "probs", 3))
                attention(l, "mla", 4, scores, lambda j, t: b2["cv"][:, t, j * P:(j + 1) * P],
                          lambda j: pairs((7, 4)[j // 2])[:, j % 2, :])

            pe.wait_ge(tables, 48)
            pe.wait_ge(mats, 16)
            pe.wait_ge(positions, 48)
            a, b = MAT1_AT["rel"]
            pe.matmul(bank[0][0:8, 0:384], mat[0:32, a:b], REL["onehot"][0:32, :], start=True, stop=True)\
                .then_inc(M.sem, M.mark("rel_row"))
            pe.wait_ge(rel_in, 16)
            a, b = CONST_AT["flip"]
            for i in range(4):
                if i >= 2:
                    pe.wait_ge(A.sem, A.at("bias", i - 2))
                pe.matmul(bank[i % 2][:, :], cst[:, a:b], REL["hankel"][:, 2 * i:2 * i + 2, :].rearrange("p a b -> p (a b)"),
                          start=True, stop=True).then_inc(M.sem, M.mark("bias", i))

            for l in range(LAYERS):
                if l:
                    pe.wait_ge(mats, 16 * (l + 1))
                if l == 0:
                    block1()
                    pe.wait_ge(V.sem, V.at("lru_lo"))
                    pe.wait_ge(V.sem, V.at("gla_lo"))
                    pe.wait_ge(V.sem, V.at("moba_lo"))
                else:
                    rwkv(l)
                    pe.wait_ge(A.sem, A.at(l, "c_sq"))
                    mla_project(l)
                    b_attention(l)
                    c_attention(l)
                    pe.wait_ge(V.sem, V.at(l, "a_lo"))
                    pe.wait_ge(V.sem, V.at(l, "bc_lo"))
                w_out(l)
                if l == 0:
                    norm_sum(l, "mixed")
                ffn(l)
                if l == 0:
                    norm_sum(l, "fed")
            pe.wait_ge(A.sem, A.at("final_sq"))
            for k in range(KT):
                last = pe.matmul(bank[6][:, 0:T], ONES, sq[:, k, :], start=(k == 0), stop=(k == KT - 1))
            last.then_inc(M.sem, M.mark("final_sum"))

        @block.scalar
        def _(act):
            Mc = lambda name: C("freq")[:, 2:3] if name == "eps" else C("freq")[:, 3:4]

            def copy(dst, src, **kw):
                return act.activation(dst, src, ACT.Copy, **kw)

            def hi_of(c):
                l, kind, i, n = STREAM[c]
                act.wait_ge(loaded[c % RING], 16 * (c // RING + 1))
                act.wait_ge(M.sem, released(c - RING))
                copy(w_hi[:, c % RING, 0:n], raw[:, c % RING, 0:n]).then_inc(hi_act, 1)

            def inverse_root(dst, src, scale, bias, name, power=-0.5):
                act.activation(dst, src, ACT.Ln, bias=bias, scale=scale).then_inc(A.sem, A.mark(*name, "ln"))
                act.wait_ge(A.sem, A.at(*name, "ln"))
                act.activation(dst, dst, ACT.Exp, scale=power).then_inc(A.sem, A.mark(*name))

            def split_h(l, what):
                for h in range(2):
                    act.wait_ge(V.sem, V.at(l, what, "xg", h))
                    if h == 0 and not (l == 0 and what == "in"):
                        pass
                    copy(h_hi[:, 4 * h:4 * h + 4, :], xg[:, 4 * h:4 * h + 4, :]).then_inc(A.sem, A.mark(l, what, "hi", h))
                act.activation(sq[:, :, :], x[:, :, :], ACT.Square).then_inc(A.sem, A.mark(l, what, "sq"))

            def norm_factor(l, what, tag):
                act.wait_ge(M.sem, M.at(l, tag, "sum"))
                inverse_root(rstd[:, :], bank[6][:, 0:T], 1.0 / D, Mc("eps"), (l, what, "rstd"))

            def attention(l, tag, heads):
                v = B1 if l == 0 else AT2
                for i in range(heads + 1):
                    if i < heads:
                        act.wait_ge(V.sem, V.at(l, tag, "max", i))
                        L, o = v["att_l"][:, i % 2, :], 2 * (i % 2)
                        act.activation(L[:, 0:T], L[:, 0:T], ACT.Exp, bias=small[:, 8 + o:9 + o],
                                       accum_out=small[:, 16 + o:17 + o])
                        act.activation(L[:, T:T + P], L[:, T:T + P], ACT.Exp, bias=small[:, 9 + o:10 + o],
                                       accum_out=small[:, 17 + o:18 + o]).then_inc(A.sem, A.mark(l, tag, "exp", i))
                    if i >= 1:
                        j = i - 1
                        act.wait_ge(M.sem, M.at(l, tag, "turn", j))
                        if j >= 2:
                            act.wait_ge(M.sem, M.at(l, tag, "values", j - 2))
                        copy(v["att_p"][:, j % 2, :], bank[2 + j % 2][:, 0:3 * P])\
                            .then_inc(A.sem, A.mark(l, tag, "turned", j))

            def mix(t, src, name):
                copy(mix_hi[:, t:t + 2, :], src).then_inc(A.sem, A.mark(*name))

            def ffn(l):
                c0 = CHUNK[l, "gu", 0]
                split_h(l, "ffn")
                todo = list(range(c0 + RING, CHUNK[l, "down", FT // 2 - 1] + 1))

                def after(c):
                    if todo and todo[0] <= c + RING:
                        hi_of(todo.pop(0))

                def silu(j):
                    if j >= 1:
                        act.wait_ge(V.sem, V.at(l, "act", "lo", j - 1))
                    act.wait_ge(V.sem, V.at(l, "gu", j))
                    act.activation(FF["sg"][:, j % 2, :], FF["gu"][:, j % 2, 0, :], ACT.Silu)\
                        .then_inc(A.sem, A.mark(l, "silu", j))
                    act.wait_ge(V.sem, V.at(l, "act", j))
                    copy(act_hi[:, j % 4, :], FF["act"][:, j % 2, :]).then_inc(A.sem, A.mark(l, "act", "hi", j))

                after(c0)
                after(c0 + 1)
                norm_factor(l, "ffn", "ffn")
                silu(0)
                silu(1)
                for p in range(1, FT // 2):
                    for j in (2 * p, 2 * p + 1):
                        after(CHUNK[l, "gu", j])
                        silu(j)
                    after(CHUNK[l, "down", p - 1])
                assert not todo

            def first_hi(l, n):
                hi_of(CHUNK[l, "gu", 0] + n)

            def block1():
                l, lru = 0, B1["lru"]
                flat = lambda v: v.rearrange("p a b -> p (a b)")
                act.wait_ge(V.sem, V.at("gla_abs"))
                act.activation(B1["g1"], B1["g1"], ACT.Exp, scale=-1.0).then_inc(A.sem, A.mark("gla_e"))
                act.wait_ge(A.sem, A.at("gla_e"))
                act.activation(B1["g1"], B1["g1"], ACT.Ln, bias=1.0).then_inc(A.sem, A.mark("gla_l"))
                act.wait_ge(V.sem, V.at("gla_last"))
                act.activation(B1["g0"], B1["g2"], ACT.Exp, scale=1 / 16).then_inc(A.sem, A.mark("gla_ep"))
                act.activation(B1["g1"], B1["g2"], ACT.Exp, scale=-1 / 16).then_inc(A.sem, A.mark("gla_en"))
                act.activation(small[:, 4:8], small[:, 0:4], ACT.Exp)
                for n in range(4):
                    s = slice(64 * n, 64 * n + 64)
                    last = act.activation(B1["ke"][:, s], B1["g2"][:, s], ACT.Exp, scale=-1 / 16, bias=small[:, n:n + 1])
                last.then_inc(A.sem, A.mark("gla_ee"))
                act.wait_ge(M.sem, M.at("gla_turn"))
                copy(flat(B1["keT"]), bank[6][:, 0:T]).then_inc(A.sem, A.mark("gla_turned"))
                act.wait_ge(M.sem, M.at("lru_gates"))
                act.wait_ge(tables, 48)
                for b, name in ((0, "ba"), (1, "bx")):
                    for t in range(2):
                        last = act.activation(lru[:, 1 + b, t * T:(t + 1) * T], pairs(b)[:, t, :], ACT.Sigmoid,
                                              bias=Par(name, t))
                last.then_inc(A.sem, A.mark("lru_sig"))
                act.wait_ge(V.sem, V.at("lru_log"))
                act.activation(lru[:, 3, :], lru[:, 1, :], ACT.Tanh, scale=-1.0).then_inc(A.sem, A.mark("lru_tanh"))
                act.activation(lru[:, 4, :], lru[:, 1, :], ACT.Exp).then_inc(A.sem, A.mark("lru_a"))
                act.wait_ge(V.sem, V.at("lru_m2"))
                act.activation(lru[:, 3, :], lru[:, 3, :], ACT.Sqrt).then_inc(A.sem, A.mark("lru_mult"))
                act.wait_ge(V.sem, V.at(l, "in", 5))
                act.activation(lru[:, 5, :], flat(B1["lg"]), ACT.Gelu_apprx_tanh).then_inc(A.sem, A.mark("lru_gelu"))
                act.activation(flat(B1["gout"]), flat(B1["gout"]), ACT.Silu).then_inc(A.sem, A.mark("gla_silu"))
                act.wait_ge(M.sem, M.at("gla_out"))
                copy(flat(B1["go"]), bank[1][:, :])
                act.activation(flat(B1["gt"]), bank[1][:, :], ACT.Square).then_inc(A.sem, A.mark("gla_sq"))
                act.wait_ge(M.sem, M.at("gla_ss"))
                inverse_root(flat(B1["gt"]), bank[0][:, :], 1 / 64, Mc("eps"), ("gla_rstd",))
                act.wait_ge(V.sem, V.at("lru_y"))
                mix(0, lru[:, 2, :].rearrange("p (a b) -> p a b", a=2), ("lru_hi",))
                act.wait_ge(V.sem, V.at("gla_y"))
                mix(2, B1["go"], ("gla_hi",))
                attention(l, "moba", 8)
                act.wait_ge(M.sem, M.at(l, "moba", "values", 7))
                mix(4, pairs(6), ("moba_hi", 0))
                mix(6, pairs(7), ("moba_hi", 1))

            def rwkv(l):
                flat = lambda v: v.rearrange("p a b -> p (a b)")
                pm, E = B2["pm"], EARLY
                act.wait_ge(V.sem, V.at(l, "mix", 0))
                act.activation(pm[0:64, 0, :], pm[0:64, 0, :], ACT.Tanh)
                act.activation(pm[:, 1, :], pm[:, 1, :], ACT.Sigmoid).then_inc(A.sem, A.mark(l, "lora_in"))
                act.wait_ge(M.sem, M.at(l, "lora"))
                for t in range(2):
                    last = act.activation(E["sg"][:, t, :], pairs(0)[:, t, :], ACT.Sigmoid, bias=Par(f"w0{l}", t))
                last.then_inc(A.sem, A.mark(l, "sg"))
                for t in range(2):
                    last = act.activation(B2["a"][:, t, :], pairs(1)[:, t, :], ACT.Sigmoid, bias=Par(f"a0{l}", t))
                last.then_inc(A.sem, A.mark(l, "a"))
                act.wait_ge(V.sem, V.at(l, "kk"))
                act.activation(flat(E["t0"]), flat(B2["kkn"]), ACT.Square).then_inc(A.sem, A.mark(l, "kk_sq"))
                act.wait_ge(V.sem, V.at(l, "mix", 4))
                act.activation(pm[64:96, 8, :], pm[64:96, 8, :], ACT.Sigmoid).then_inc(A.sem, A.mark(l, "gate_in"))
                c0 = math.exp(-0.5)
                act.wait_ge(V.sem, V.at(l, "kk_max"))
                inverse_root(flat(E["t0"]), flat(E["t0"]), 1.0, 0.0, (l, "kk_rn"))
                act.wait_ge(V.sem, V.at(l, "cx"))
                act.activation(flat(E["ep"]), flat(E["cs"]), ACT.Exp, scale=-c0)
                act.activation(flat(E["en"]), flat(E["cs"]), ACT.Exp, scale=c0).then_inc(A.sem, A.mark(l, "ep"))
                act.activation(flat(E["cx"]), flat(E["cx"]), ACT.Exp, scale=-c0)
                act.activation(small[:, 36:38], small[:, 34:36], ACT.Exp, scale=-c0).then_inc(A.sem, A.mark(l, "ex"))
                act.wait_ge(M.sem, M.at(l, "gate"))
                copy(flat(B2["gate"]), bank[2][:, :]).then_inc(A.sem, A.mark(l, "gate"))
                act.wait_ge(M.sem, M.at(l, "v_turn"))
                copy(flat(B2["vt"]), bank[6][:, :]).then_inc(A.sem, A.mark(l, "v_turned"))
                act.wait_ge(M.sem, M.at(l, "kb_turn"))
                copy(flat(B2["kbt"]), bank[7][:, :]).then_inc(A.sem, A.mark(l, "kb_turned"))
                Xm, Y = INV["x"], INV["yy"]
                for q in range(2):
                    act.wait_ge(M.sem, M.at(l, "inv0", q))
                    copy(Xm[:, 4 * q:4 * q + 4, :], quads(q)).then_inc(A.sem, A.mark(l, "inv0", q))
                for n in range(1, 7):
                    for q in range(2):
                        act.wait_ge(M.sem, M.at(l, "inv_y", n, q))
                        if n >= 2:
                            act.wait_ge(M.sem, M.at(l, "inv_z", n - 1, q))
                        copy(Y[:, 4 * q:4 * q + 4, :], quads(q)).then_inc(A.sem, A.mark(l, "inv_y", n, q))
                for c in range(TT):
                    act.wait_ge(M.sem, M.at(l, "r", c))
                    if c:
                        act.wait_ge(M.sem, M.at(l, "sa", 0))
                    copy(B2["rs"], bank[0][:, 0:T]).then_inc(A.sem, A.mark(l, "r", c))
                    act.wait_ge(M.sem, M.at(l, "y", c))
                    copy(B2["y"][:, :, c * P:(c + 1) * P], pairs(3 if c == 0 else 6)[:, :, 0:P])\
                        .then_inc(A.sem, A.mark(l, "y", c))
                act.wait_ge(V.sem, V.at(l, "yc"))
                act.activation(flat(E["sg"]), flat(B2["y"]), ACT.Square).then_inc(A.sem, A.mark(l, "y_sq"))
                act.wait_ge(M.sem, M.at(l, "var"))
                inverse_root(flat(E["cs"]), bank[1][:, :], 1 / 64, Mc("gn"), (l, "y_rstd"))
                b = AT2
                act.activation(flat(b["cqs"]), flat(B2["cq"]), ACT.Square)
                act.activation(b["ckvs"], B2["ckv"], ACT.Square).then_inc(A.sem, A.mark(l, "c_sq"))
                act.wait_ge(V.sem, V.at(l, "a_y"))
                mix(0, B2["y"], (l, "a_hi"))
                act.wait_ge(M.sem, M.at(l, "c_ss"))
                inverse_root(b["rq"], bank[0][:, 0:T], 1 / 256, Mc("eps"), (l, "rq"))
                inverse_root(b["rkv"], bank[0][:, T:2 * T], 1 / 128, Mc("eps"), (l, "rkv"))
                act.wait_ge(V.sem, V.at(l, "c_n"))
                copy(cq_hi[:, 0:2, :], b["cqn"])
                copy(cq_hi[:, 2, :], b["ckvn"]).then_inc(A.sem, A.mark(l, "c_hi"))
                scale = 192 ** -0.5
                dst = [b["qn"][:, 0:2, :], b["qn"][:, 2:4, :], b["qr"], b["kn"][:, 0:2, :], b["kn"][:, 2:4, :],
                       b["cv"][:, 0, :], b["cv"][:, 1, :]]
                for i in range(7):
                    act.wait_ge(M.sem, M.at(l, "up", i))
                    src = bank[4 + i % 2][:, :] if i >= 5 else pairs(4 + i % 2)
                    act.activation(dst[i], src, ACT.Copy, scale=scale if i < 3 else 1.0)\
                        .then_inc(A.sem, A.mark(l, "up", i))
                attention(l, "dil", 4)
                attention(l, "mla", 4)
                act.wait_ge(M.sem, M.at(l, "dil", "values", 3))
                mix(2, pairs(6), (l, "b_hi"))
                act.wait_ge(M.sem, M.at(l, "mla", "values", 3))
                mix(4, pairs(7), (l, "c_hi", 0))
                mix(6, pairs(4), (l, "c_hi", 1))

            act.wait_ge(tables, 48)
            act.wait_ge(V.sem, V.at("angles"))
            for i in range(4):
                last = act.activation(rope[:, i, :], rope[:, i, :], ACT.Sin)
            last.then_inc(A.sem, A.mark("rope"))
            act.activation(small[:, 40:42], Par("lam"), ACT.Abs).then_inc(A.sem, A.mark("lam_abs"))
            act.wait_ge(A.sem, A.at("lam_abs"))
            act.activation(small[:, 40:42], small[:, 40:42], ACT.Exp, scale=-1.0).then_inc(A.sem, A.mark("lam_e"))
            for i in range(4):
                act.wait_ge(M.sem, M.at("bias", i))
                copy(B1["bias"][:, 2 * i:2 * i + 2, :], pairs(i % 2)).then_inc(A.sem, A.mark("bias", i))

            for l in range(LAYERS):
                split_h(l, "in")
                norm_factor(l, "in", "in")
                block1() if l == 0 else rwkv(l)
                if l == 0:
                    for m in range(4):
                        act.wait_ge(M.sem, M.at(l, "mixed", m))
                        act.activation(sq[:, 2 * m:2 * m + 2, :], pairs(m), ACT.Square)\
                            .then_inc(A.sem, A.mark(l, "mixed", "sq", m))
                        if m < 3:
                            first_hi(l, m)
                    norm_factor(l, "mixed", "mixed")
                else:
                    for m in range(3):
                        first_hi(l, m)
                ffn(l)
                if l == 0:
                    act.wait_ge(M.sem, M.at(l, "down", FT // 2 - 1))
                    for m in range(4):
                        act.activation(sq[:, 2 * m:2 * m + 2, :], pairs(m), ACT.Square)\
                            .then_inc(A.sem, A.mark(l, "fed", "sq", m))
                    norm_factor(l, "fed", "fed")
            act.wait_ge(V.sem, V.at(2, "fed", 3))
            act.activation(sq[:, :, :], x[:, :, :], ACT.Square).then_inc(A.sem, A.mark("final_sq"))
            act.wait_ge(M.sem, M.at("final_sum"))
            inverse_root(rstd[:, :], bank[6][:, 0:T], 1.0 / D, Mc("eps"), ("final_rstd",))
            act.wait_ge(V.sem, V.at("final", KT - 1))
            act.dma_start(out, xg[:, :, :].rearrange("p k t -> p (k t)")).then_inc(stored, 16)
            act.wait_ge(stored, 16)

        @block.vector
        def _(dve):
            def wide(v, n):
                return v.unsqueeze(1).broadcast_to([P, n, v.shape[-1]])

            def tt(dst, a, b, op, *name):
                ins_ = dve.tensor_tensor(dst, a, b, op)
                if name:
                    ins_.then_inc(V.sem, V.mark(*name))
                return ins_

            def after_v(*name):
                dve.wait_ge(V.sem, V.at(*name))

            def after_a(*name):
                dve.wait_ge(A.sem, A.at(*name))

            def after_m(*name):
                dve.wait_ge(M.sem, M.at(*name))

            def lo_of(c):
                s, n = c % RING, STREAM[c][3]
                dve.wait_ge(hi_act, n_hi[c])
                dve.tensor_tensor(w_lo[:, s, 0:n], raw[:, s, 0:n], w_hi[:, s, 0:n].bitcast(F32), ALU.subtract)\
                    .then_inc(lo_dve, 1)

            def split_h(l, what, g):
                for h in range(2):
                    s = slice(4 * h, 4 * h + 4)
                    gain = Par(g)[:, s].unsqueeze(2).broadcast_to([P, 4, T])
                    if not (l == 0 and what == "in"):
                        after_v(*((l, "mixed") if what == "ffn" else (l - 1, "fed")), 2 * h + 1)
                    tt(xg[:, s, :], x[:, s, :], gain, ALU.mult, l, what, "xg", h)
                for h in range(2):
                    s = slice(4 * h, 4 * h + 4)
                    after_a(l, what, "hi", h)
                    tt(h_lo[:, s, :], xg[:, s, :], h_hi[:, s, :].bitcast(F32), ALU.subtract, l, what, "lo", h)

            def residual(l, what, gain):
                c0 = CHUNK[l, "gu", 0]
                if gain is not None and what == "mixed":
                    for m in range(RING):
                        lo_of(c0 + m)
                if gain is not None:
                    after_a(l, what, "rstd")
                for m in range(4):
                    if gain is None:
                        if what == "mixed" and m < RING:
                            lo_of(c0 + m)
                        after_m(l, *(("mixed", m) if what == "mixed" else ("down", FT // 2 - 1)))
                        tt(x[:, 2 * m:2 * m + 2, :], x[:, 2 * m:2 * m + 2, :], pairs(m), ALU.add, l, what, m)
                    else:
                        for t in range(2):
                            last = dve.scalar_tensor_tensor(xg[:, 2 * m + t, :], pairs(m)[:, t, :],
                                                            Par(gain, 2 * m + t), rstd[:, :], ALU.mult, ALU.mult)
                        last.then_inc(V.sem, V.mark(l, what, "normed", m))
                if gain is not None:
                    for m in range(4):
                        after_v(l, what, "normed", m)
                        tt(x[:, 2 * m:2 * m + 2, :], x[:, 2 * m:2 * m + 2, :], xg[:, 2 * m:2 * m + 2, :], ALU.add,
                           l, what, m)

            def evacuate(l, i, dst, scale=None, token_major=False, single=False):
                after_m(l, "in", i)
                src = pairs(4 + i % 2)
                if i == 0:
                    after_a(l, "in", "rstd")
                if token_major:
                    for t in range(TT):
                        last = dve.tensor_scalar(dst[:, t, :], src[:, t, :], rstd_col[:, t:t + 1], None, ALU.mult)
                else:
                    parts = list(dst) if isinstance(dst, (list, tuple)) else [dst]
                    for t, d in enumerate(parts):
                        s = src if len(parts) == 1 and not single else src[:, t, :]
                        r = wide(rstd[:, :], 2) if len(parts) == 1 and not single else rstd[:, :]
                        if scale and scale[t]:
                            last = dve.scalar_tensor_tensor(d, s, scale[t], r, ALU.mult, ALU.mult)
                        else:
                            last = dve.tensor_tensor(d, s, r, ALU.mult)
                last.then_inc(V.sem, V.mark(l, "in", i))

            def column_factor(l):
                after_m(l, "in", "rstd")
                dve.tensor_copy(rstd_col[:, :], bank[7][:, 0:2 * P].rearrange("p (a b) -> p a b", a=2)[:, :, 0])\
                    .then_inc(V.sem, V.mark(l, "in", "rstd_col"))
                after_v(l, "in", "rstd_col")

            def attention(l, tag, heads, mask):
                v = B1 if l == 0 else AT2
                for i in range(heads + 1):
                    if i < heads:
                        after_m(l, tag, "scores", i)
                        if i >= 2:
                            after_m(l, tag, "turn", i - 2)
                        L, b, o = v["att_l"][:, i % 2, :], bank[i % 2], 2 * (i % 2)
                        late, early = mask(i)
                        dve.tensor_tensor_reduce(L[:, 0:T], b[:, 0:T], late, 1.0, -3e38, ALU.add, ALU.max,
                                                 small[:, 24 + o:25 + o])
                        dve.tensor_tensor_reduce(L[:, T:T + P], b[:, T:T + P], early, 1.0, -3e38, ALU.add, ALU.max,
                                                 small[:, 25 + o:26 + o]).then_inc(V.sem, V.mark(l, tag, "logits", i))
                        after_v(l, tag, "logits", i)
                        dve.tensor_scalar(small[:, 8 + o:10 + o], small[:, 24 + o:26 + o], -1.0, None, ALU.mult)\
                            .then_inc(V.sem, V.mark(l, tag, "max", i))
                    if i >= 1:
                        j = i - 1
                        L, o = v["att_l"][:, j % 2, :], 2 * (j % 2)
                        after_a(l, tag, "exp", j)
                        dve.reciprocal(small[:, 28 + o:30 + o], small[:, 16 + o:18 + o])\
                            .then_inc(V.sem, V.mark(l, tag, "inv", j))
                        after_v(l, tag, "inv", j)
                        dve.tensor_scalar(L[:, 0:T], L[:, 0:T], small[:, 28 + o:29 + o], None, ALU.mult)
                        dve.tensor_scalar(L[:, T:T + P], L[:, T:T + P], small[:, 29 + o:30 + o], None, ALU.mult)\
                            .then_inc(V.sem, V.mark(l, tag, "probs", j))

            def mix_lo_of(t, src, hi_name, *name):
                after_a(*hi_name)
                tt(mix_lo[:, t:t + 2, :], src, mix_hi[:, t:t + 2, :].bitcast(F32), ALU.subtract, *name)

            def block1():
                l, lru = 0, B1["lru"]
                flat = lambda v: v.rearrange("p a b -> p (a b)")
                small_ = small
                dve.memset(B1["lx"][:, :, 0:3], 0.0)
                dve.memset(flat(B1["qm"]), 0.0).then_inc(V.sem, V.mark("zeros"))
                evacuate(l, 0, B1["lx"][:, :, 3:259])
                after_v(l, "in", 0)
                for j in range(4):
                    if j:
                        after_v("lru_conv", j - 1)
                    for t in range(2):
                        dst, src = lru[:, 0, t * T:(t + 1) * T], B1["lx"][:, t, j:j + T]
                        w = Par("conv_w", 2 * j + t)
                        if j == 0:
                            last = dve.tensor_scalar(dst, src, w, Par("conv_b", t), ALU.mult, ALU.add)
                        else:
                            last = dve.scalar_tensor_tensor(dst, src, w, dst, ALU.mult, ALU.add)
                    last.then_inc(V.sem, V.mark("lru_conv", j) if j < 3 else V.mark("lru_conv"))
                evacuate(l, 1, [B1["glr"], B1["gk"]])
                column_factor(l)
                after_m("gla_gate")
                dve.tensor_scalar(B1["g0"], bank[6][:, 0:T], Par("gate_b"), None, ALU.add)\
                    .then_inc(V.sem, V.mark("gla_z"))
                after_v("gla_z")
                dve.tensor_scalar(B1["g2"], B1["g0"], 0.0, None, ALU.min).then_inc(V.sem, V.mark("gla_min"))
                after_v("gla_min")
                dve.scalar_tensor_tensor(B1["g1"], B1["g2"], -2.0, B1["g0"], ALU.mult, ALU.add)\
                    .then_inc(V.sem, V.mark("gla_abs"))
                evacuate(l, 2, [B1["gq"], B1["mq"][:, 0, :]], scale=(32 ** -0.5, 0.125))
                after_a("gla_l")
                tt(B1["g0"], B1["g2"], B1["g1"], ALU.subtract, "gla_log")
                after_v("gla_log")
                for n in range(4):
                    s = slice(64 * n, 64 * n + 64)
                    last = dve.tensor_tensor_scan(B1["g2"][:, s], C("ones")[:, 0:64], B1["g0"][:, s], 0.0, ALU.mult,
                                                  ALU.add)
                last.then_inc(V.sem, V.mark("gla_cum"))
                after_v("gla_cum")
                dve.tensor_scalar(small[:, 0:4], B1["g2"].rearrange("p (n c) -> p n c", n=4)[:, :, 63], 1 / 16, None,
                                  ALU.mult).then_inc(V.sem, V.mark("gla_last"))
                evacuate(l, 3, B1["gv"], token_major=True)
                after_v(l, "in", 2)
                after_a("gla_ep")
                for h in range(4):
                    s = slice(32 * h, 32 * h + 32)
                    dve.tensor_tensor(B1["qm"][s, h, :], B1["gq"][s, :], B1["g0"][s, :], ALU.mult)
                after_a("gla_en")
                tt(B1["kd"], B1["gk"], B1["g1"], ALU.mult)
                after_a("gla_ee")
                tt(B1["ke"], B1["gk"], B1["ke"], ALU.mult, "gla_ke")
                evacuate(l, 4, B1["lg"])
                evacuate(l, 5, B1["gout"])
                after_m("gla_scores")
                for t in range(TT):
                    dve.tensor_tensor(B1["att"][:, t, :].rearrange("p (h t) -> p h t", h=4), quads(2 + t),
                                      wide(C("gla_mask"), 4), ALU.mult).then_inc(V.sem, V.mark("gla_att", t))
                evacuate(l, 6, B1["mk"][:, 0:2, :])
                after_m("gla_kv")
                st = B1["st"]
                dve.tensor_copy(st[:, 0, :], pairs(0)[:, 0, :]).then_inc(V.sem, V.mark("gla_state", 0))
                for n, src in ((1, bank[7][:, 0:T]), (2, pairs(0)[:, 1, :])):
                    after_v("gla_state", n - 1)
                    dve.scalar_tensor_tensor(st[:, n, :], st[:, n - 1, :], small[:, 4 + n:5 + n], src, ALU.mult,
                                             ALU.add).then_inc(V.sem, V.mark("gla_state", n))
                after_a("lru_sig")
                for t in range(2):
                    s = slice(t * T, (t + 1) * T)
                    last = dve.tensor_scalar(lru[:, 1, s], lru[:, 1, s], small[:, 44 + t:45 + t], None, ALU.mult)
                last.then_inc(V.sem, V.mark("lru_log"))
                tt(lru[:, 2, :], lru[:, 2, :], lru[:, 0, :], ALU.mult, "lru_ix")
                evacuate(l, 7, [B1["mq"][:, 1, :], B1["mq"][:, 2, :]], scale=(0.125, 0.125))
                after_a("lru_a")
                after_v("lru_ix")
                tt(lru[:, 0, :], lru[:, 4, :], lru[:, 4, :], ALU.mult, "lru_a2")
                after_v("lru_a2")
                dve.scalar_tensor_tensor(lru[:, 3, :], lru[:, 0, :], 1.0, lru[:, 3, :], ALU.add, ALU.mult)\
                    .then_inc(V.sem, V.mark("lru_m2"))
                after_a("lru_mult")
                dve.memset(lru[:, 3, :].rearrange("p (a b) -> p a b", a=2)[:, :, 0:1], 1.0)\
                    .then_inc(V.sem, V.mark("lru_first"))
                after_v("lru_first")
                tt(lru[:, 2, :], lru[:, 2, :], lru[:, 3, :], ALU.mult, "lru_u")
                after_v("lru_u")
                for t in range(2):
                    s = slice(t * T, (t + 1) * T)
                    last = dve.tensor_tensor_scan(lru[:, 0, s], lru[:, 4, s], lru[:, 2, s], 0.0, ALU.mult, ALU.add)
                last.then_inc(V.sem, V.mark("lru_h"))
                after_v("lru_h")
                after_a("lru_gelu")
                evacuate(l, 8, B1["mk"][:, 2:4, :])
                tt(lru[:, 2, :], lru[:, 0, :], lru[:, 5, :], ALU.mult, "lru_y")
                evacuate(l, 9, [B1["mq"][:, 3, :]], scale=(0.125,), single=True)
                after_a("gla_rstd")
                tt(flat(B1["go"]), flat(B1["go"]), flat(B1["gt"]), ALU.mult, "gla_n")
                after_v("gla_n")
                for t in range(2):
                    last = dve.scalar_tensor_tensor(B1["go"][:, t, :], B1["go"][:, t, :], Par("gla_norm", t),
                                                    B1["gout"][:, t, :], ALU.mult, ALU.mult)
                last.then_inc(V.sem, V.mark("gla_y"))
                mix_lo_of(0, lru[:, 2, :].rearrange("p (a b) -> p a b", a=2), ("lru_hi",), "lru_lo")
                mix_lo_of(2, B1["go"], ("gla_hi",), "gla_lo")
                evacuate(l, 10, B1["mv"][:, :, 0:T], token_major=True)
                evacuate(l, 11, B1["mv"][:, :, T:2 * T], token_major=True)
                attention(l, "moba", 8, lambda i: (B1["bias"][:, i, :], B1["bias"][:, i, P:2 * P]))
                mix_lo_of(4, pairs(6), ("moba_hi", 0), "moba_lo", 0)
                mix_lo_of(6, pairs(7), ("moba_hi", 1), "moba_lo")

            def rwkv(l):
                flat = lambda v: v.rearrange("p a b -> p (a b)")
                pm, pf, E, S = B2["pm"], PF["pf"], EARLY, small
                dve.memset(pf[:, :, 0:1], 0.0).then_inc(V.sem, V.mark(l, "zeros"))

                def shift(n, tiles, rows=slice(0, P)):
                    a, b = tiles
                    tt(pm[rows, a:b, :], pf[rows, a:b, 0:T], pf[rows, a:b, 1:T + 1], ALU.subtract, l, "diff", n)
                    after_v(l, "diff", n)
                    for t in range(a, b):
                        last = dve.scalar_tensor_tensor(pm[rows, t, :], pm[rows, t, :],
                                                        Par(f"mu{l}", t)[rows, :], pf[rows, t, 1:T + 1],
                                                        ALU.mult, ALU.add)
                    last.then_inc(V.sem, V.mark(l, "mix", n))

                def evac_shift(i):
                    evacuate(l, i, pf[:, 2 * i:2 * i + 2, 1:T + 1])
                    after_v(l, "in", i)
                    shift(i, (2 * i, 2 * i + 2))

                evac_shift(0)
                evac_shift(1)
                after_v(l, "mix", 1)
                for t in range(2):
                    last = dve.tensor_scalar(B2["kkn"][:, t, :], pm[:, 2 + t, :], Par(f"k_k{l}", t), None, ALU.mult)
                last.then_inc(V.sem, V.mark(l, "kk"))
                column_factor(l)
                after_a(l, "sg")
                for t in range(2):
                    for c in range(TT):
                        s = slice(c * P, (c + 1) * P)
                        last = dve.tensor_tensor_scan(E["cs"][:, t, s], C("ones"), E["sg"][:, t, s], 0.0, ALU.mult,
                                                      ALU.add)
                last.then_inc(V.sem, V.mark(l, "scan"))
                evac_shift(2)
                evac_shift(3)
                evacuate(l, 4, [pf[:, 8, 1:T + 1], B2["ckv"]])
                after_v(l, "in", 4)
                dve.tensor_copy(B2["krope"][0:64, :], pf[0:64, 8, 1:T + 1])
                shift(4, (8, 9), slice(64, 96))
                after_v(l, "scan")
                by_chunk = lambda v: v.rearrange("p a (c t) -> p (a c) t", c=TT)
                cs = by_chunk(E["cs"])
                dve.tensor_copy(S[:, 50:54], cs[:, :, 63]).then_inc(V.sem, V.mark(l, "mid"))
                after_v(l, "mid")
                tt(cs, cs, S[:, 50:54].unsqueeze(2).broadcast_to([P, 4, P]), ALU.subtract, l, "cs")
                after_v(l, "cs")
                tt(S[:, 34:36], E["cs"][:, :, P - 1], S[:, 50:54].rearrange("p (a c) -> p a c", c=TT)[:, :, 1], ALU.add)
                tt(E["cx"], E["cs"], E["sg"], ALU.subtract, l, "cx")
                after_m(l, "kk_ss")
                after_a(l, "kk_sq")
                dve.tensor_scalar(flat(E["t0"]), bank[3][:, :], 1e-24, None, ALU.max)\
                    .then_inc(V.sem, V.mark(l, "kk_max"))
                after_a(l, "a")
                for t in range(2):
                    last = dve.tensor_scalar(B2["kp"][:, t, :], B2["a"][:, t, :], -1.0, Par(f"k_a{l}", t), ALU.add,
                                             ALU.mult)
                last.then_inc(V.sem, V.mark(l, "kp0"))
                after_v(l, "kp0")
                dve.scalar_tensor_tensor(flat(B2["kp"]), flat(B2["kp"]), 1.0, flat(pm[:, 2:4, :]), ALU.add, ALU.mult)\
                    .then_inc(V.sem, V.mark(l, "kp"))
                after_a(l, "kk_rn")
                tt(B2["kkn"], B2["kkn"], E["t0"], ALU.mult, l, "kkn")
                after_a(l, "ep")
                after_v(l, "kkn")
                tt(B2["bh"], B2["kkn"], B2["a"], ALU.mult, l, "b")
                after_v(l, "b")
                tt(B2["bh"], B2["bh"], E["en"], ALU.mult)
                tt(B2["kh"], B2["kp"], E["en"], ALU.mult)
                after_a(l, "ex")
                cut = lambda v: v.rearrange("p (c t) -> p c t", c=TT)
                for t in range(2):
                    tt(B2["kr"][:, t, :, 0, :], cut(B2["kkn"][:, t, :]), cut(E["cx"][:, t, :]), ALU.mult)
                    last = tt(B2["kr"][:, t, :, 1, :], cut(pm[:, 4 + t, :]), cut(E["ep"][:, t, :]), ALU.mult)
                last.then_inc(V.sem, V.mark(l, "kr"))
                evacuate(l, 5, B2["cq"])
                gram = G2["gram"]
                dve.memset(B2["s1"].rearrange("p a b -> p (a b)"), 0.0)
                dve.memset(gram.rearrange("p a b c -> p (a b c)"), 0.0).then_inc(V.sem, V.mark(l, "gram0"))
                after_v(l, "gram0")
                mask = C("before").bitcast(U32)
                for g in range(8):
                    after_m(l, "gram", g)
                    for n in range(2):
                        last = dve.copy_predicated(gram[:, g, 2 * n:2 * n + 2, :].rearrange("p a b -> p (a b)"), mask,
                                                   pairs(g % 4)[:, n, :])
                    last.then_inc(V.sem, V.mark(l, "gram", g))
                evacuate(l, 6, [B2["bq"][:, 0, :], B2["bq"][:, 1, :]], scale=(0.125, 0.125))
                Xm, XT, BT = INV["x"], INV["xt"], INV["bt"]
                q4 = lambda v, q: v[:, 4 * q:4 * q + 4, :]

                def level(n, q, to):
                    return dve.tensor_tensor(q4(to, q), q4(gram[:, :, 0, :], q), wide(C(f"level{n}"), 4), ALU.mult)

                after_v(l, "gram", 7)
                for q in range(2):
                    level(0, q, BT).then_inc(V.sem, V.mark(l, "inv_b0", q))
                for q in range(2):
                    after_v(l, "inv_b0", q)
                    tt(q4(XT, q), wide(C("ident"), 4), q4(BT, q), ALU.subtract, l, "inv0", q)
                for n in range(1, 7):
                    for q in range(2):
                        if n > 1:
                            after_m(l, "inv_y", n - 1, q)
                        else:
                            after_v(l, "inv0", q)
                        level(n, q, BT).then_inc(V.sem, V.mark(l, "inv_bt", n, q))
                    if n == 1:
                        evacuate(l, 7, B2["bk"])
                    if n == 2:
                        evacuate(l, 8, B2["bv"], token_major=True)
                    for q in range(2):
                        if n < 6:
                            after_m(l, "inv_z", n, q)
                            if n == 1:
                                after_a(l, "inv0", q)
                            tt(q4(Xm, q), q4(Xm, q), quads(6 + q), ALU.subtract, l, "inv_x0", n, q)
                        after_m(l, "inv_zt", n, q)
                        tt(q4(XT, q), q4(XT, q), quads(2 + q), ALU.subtract, l, "inv_xt", n, q)
                        if n < 6:
                            dve.wait_ge(V.sem, V.at(l, "inv_xt", n, q))
                            dve.nop().then_inc(V.sem, V.mark(l, "inv_x", n, q))
                for c in range(TT):
                    after_m(l, "sa", c)
                    dve.tensor_scalar(B2["nsa"][:, c, :], bank[1][:, 0:T], -1.0, None, ALU.mult)\
                        .then_inc(V.sem, V.mark(l, "nsa", c))
                    if c == 0:
                        after_m(l, "s1")
                        after_a(l, "ex")
                        for t in range(2):
                            for h in range(2):
                                rows = slice(64 * h, 64 * h + 64)
                                last = dve.tensor_scalar(B2["s1"][rows, t, rows], bank[2][rows, t * 64:(t + 1) * 64],
                                                         S[rows, 36 + t:37 + t], None, ALU.mult)
                        last.then_inc(V.sem, V.mark(l, "s1"))
                after_m(l, "mean")
                dve.scalar_tensor_tensor(flat(B2["y"]), bank[0][:, :], -1 / 64, flat(B2["y"]), ALU.mult, ALU.add)\
                    .then_inc(V.sem, V.mark(l, "yc"))
                for t in range(2):
                    last = dve.scalar_tensor_tensor(E["t0"][:, t, :], pm[:, 4 + t, :], Par(f"r_k{l}", t),
                                                    B2["kp"][:, t, :], ALU.mult, ALU.mult)
                last.then_inc(V.sem, V.mark(l, "bonus_in"))
                after_m(l, "bonus")
                tt(flat(E["t0"]), bank[2][:, :], flat(pm[:, 6:8, :]), ALU.mult, l, "bonus")
                after_a(l, "y_rstd")
                tt(B2["y"], B2["y"], E["cs"], ALU.mult, l, "yn")
                after_v(l, "yn")
                for t in range(2):
                    last = dve.tensor_scalar(B2["y"][:, t, :], B2["y"][:, t, :], Par(f"ln_w{l}", t), Par(f"ln_b{l}", t),
                                             ALU.mult, ALU.add)
                last.then_inc(V.sem, V.mark(l, "yl"))
                after_v(l, "yl")
                tt(B2["y"], B2["y"], E["t0"], ALU.add, l, "yb")
                after_v(l, "yb")
                tt(B2["y"], B2["y"], B2["gate"], ALU.mult, l, "a_y")
                b = AT2
                after_a(l, "rkv")
                for t in range(2):
                    dve.scalar_tensor_tensor(b["cqn"][:, t, :], B2["cq"][:, t, :], Par(f"qn{l}", t), b["rq"],
                                             ALU.mult, ALU.mult)
                dve.scalar_tensor_tensor(b["ckvn"], B2["ckv"], Par(f"kvn{l}", 0), b["rkv"], ALU.mult, ALU.mult)\
                    .then_inc(V.sem, V.mark(l, "c_n"))
                mix_lo_of(0, B2["y"], (l, "a_hi"), l, "a_lo")
                after_a(l, "c_hi")
                tt(cq_lo[:, 0:2, :], b["cqn"], cq_hi[:, 0:2, :].bitcast(F32), ALU.subtract)
                tt(cq_lo[:, 2, :], b["ckvn"], cq_hi[:, 2, :].bitcast(F32), ALU.subtract, l, "c_lo")

                def rotate(n, dst, v, swapped, cos):
                    w = 2 if len(v.shape) == 3 else 1
                    table = lambda i: wide(rope[:, i, :], 2) if w == 2 else rope[:, i, :]
                    tt(b["t0"] if w == 2 else b["t0"][:, 0, :], v, table(cos), ALU.mult)
                    tt(b["t1"] if w == 2 else b["t1"][:, 0, :], swapped, table(cos + 1), ALU.mult, l, "rot", n)
                    after_v(l, "rot", n)
                    return tt(dst, b["t0"] if w == 2 else b["t0"][:, 0, :], b["t1"] if w == 2 else b["t1"][:, 0, :],
                              ALU.add, l, "rotated", n)

                after_m(l, "b_rot")
                after_v(l, "a_lo")
                rotate(0, B2["bq"], B2["bq"], pairs(1), 0)
                after_v(l, "rotated", 0)
                rotate(1, B2["bk"], B2["bk"], pairs(2), 0)
                after_v(l, "rotated", 1)
                dve.nop().then_inc(V.sem, V.mark(l, "b_rope"))
                after_m(l, "k_rot")
                rotate(2, b["kro"], bank[3][:, 0:T], bank[3][:, T:2 * T], 2)
                after_v(l, "rotated", 2)
                after_a(l, "up", 2)
                after_m(l, "q_rot")
                rotate(3, b["qr"], b["qr"], pairs(0), 2)
                after_v(l, "rotated", 3)
                dve.nop().then_inc(V.sem, V.mark(l, "c_rope"))
                attention(l, "dil", 4, lambda i: (C("dilated")[:, 0:T], C("dilated")[:, T:T + P]))
                attention(l, "mla", 4, lambda i: (C("causal")[:, 0:T], C("causal")[:, T:T + P]))
                mix_lo_of(2, pairs(6), (l, "b_hi"), l, "b_lo")
                mix_lo_of(4, pairs(7), (l, "c_hi", 0), l, "c_lo0")
                mix_lo_of(6, pairs(4), (l, "c_hi", 1), l, "bc_lo")

            def ffn(l):
                def feed(j):
                    after_m(l, "gu", j)
                    if j == 0:
                        after_a(l, "ffn", "rstd")
                    if j >= 2:
                        after_a(l, "silu", j - 2)
                        after_v(l, "act", j - 2)
                    tt(FF["gu"][:, j % 2, :, :], pairs(4 + j % 2), wide(rstd[:, :], 2), ALU.mult, l, "gu", j)
                    after_a(l, "silu", j)
                    after_v(l, "gu", j)
                    tt(FF["act"][:, j % 2, :], FF["sg"][:, j % 2, :], FF["gu"][:, j % 2, 1, :], ALU.mult, l, "act", j)
                    after_a(l, "act", "hi", j)
                    if j >= 4:
                        after_m(l, "down", (j - 4) // 2)
                    tt(act_lo[:, j % 4, :], FF["act"][:, j % 2, :], act_hi[:, j % 4, :].bitcast(F32), ALU.subtract,
                       l, "act", "lo", j)

                todo = list(range(CHUNK[l, "gu", 0] + RING, CHUNK[l, "down", FT // 2 - 1] + 1))

                def after(c):
                    if todo and todo[0] <= c + RING:
                        lo_of(todo.pop(0))

                after(CHUNK[l, "gu", 0])
                after(CHUNK[l, "gu", 1])
                feed(0)
                feed(1)
                for p in range(1, FT // 2):
                    for j in (2 * p, 2 * p + 1):
                        after(CHUNK[l, "gu", j])
                        feed(j)
                    after(CHUNK[l, "down", p - 1])

            dve.wait_ge(tables, 48)
            dve.wait_ge(positions, 48)
            after_m("rel_row")
            tt(REL["relrow"][0:8, :], bank[0][0:8, 0:384], REL["relneg"][0:8, :], ALU.add, "rel_row")
            tmp = area(8192, dict(p=(T,), ang=(2, T), n=(T,)))[0]
            dve.tensor_copy(tmp["p"], pos).then_inc(V.sem, V.mark("pos"))
            after_v("pos")
            ROUND = 12582912.0
            for i in range(2):
                dve.tensor_scalar(tmp["ang"][:, i, :], tmp["p"], C("freq")[:, i:i + 1], None, ALU.mult)\
                    .then_inc(V.sem, V.mark("ang", i))
                after_v("ang", i)
                for s in range(2):
                    dst, quarter = rope[:, 2 * i + s, :], 0.25 if s == 0 else 0.0
                    steps = [lambda: dve.tensor_scalar(tmp["n"], tmp["ang"][:, i, :], 1 / (2 * math.pi), quarter,
                                                       ALU.mult, ALU.add),
                             lambda: dve.tensor_scalar(tmp["n"], tmp["n"], ROUND, None, ALU.add),
                             lambda: dve.tensor_scalar(tmp["n"], tmp["n"], -ROUND, None, ALU.add),
                             lambda: dve.scalar_tensor_tensor(dst, tmp["n"], -6.28125, tmp["ang"][:, i, :],
                                                              ALU.mult, ALU.add),
                             lambda: dve.scalar_tensor_tensor(dst, tmp["n"], -0.0019350051879882812, dst,
                                                              ALU.mult, ALU.add),
                             lambda: dve.scalar_tensor_tensor(dst, tmp["n"],
                                                              -(2 * math.pi - 6.28125 - 0.0019350051879882812), dst,
                                                              ALU.mult, ALU.add),
                             lambda: dve.tensor_scalar(dst, dst, 2 * math.pi * quarter, 3.1415925, ALU.add, ALU.min),
                             lambda: dve.tensor_scalar(dst, dst, -3.1415925, None, ALU.max)]
                    for n, step in enumerate(steps):
                        step().then_inc(V.sem, V.mark("angle", i, s, n))
                        after_v("angle", i, s, n)
            dve.nop().then_inc(V.sem, V.mark("angles"))
            e, s_, s2, acc = small[:, 40:42], small[:, 56:58], small[:, 58:60], small[:, 60:62]
            after_a("lam_e")
            chain = [lambda: dve.tensor_scalar(s_, e, 2.0, None, ALU.add),
                     lambda: dve.reciprocal(s_, s_),
                     lambda: dve.tensor_tensor(s_, s_, e, ALU.mult),
                     lambda: dve.tensor_tensor(s2, s_, s_, ALU.mult),
                     lambda: dve.memset(acc, 1 / 17)]
            for n in range(7, -1, -1):
                chain += [lambda: dve.tensor_tensor(acc, acc, s2, ALU.mult),
                          lambda n=n: dve.tensor_scalar(acc, acc, 1 / (2 * n + 1), None, ALU.add)]
            chain += [lambda: dve.tensor_tensor(acc, acc, s_, ALU.mult),
                      lambda: dve.tensor_scalar(s_, Par("lam"), -1.0, 0.0, ALU.mult, ALU.max),
                      lambda: dve.scalar_tensor_tensor(acc, acc, 2.0, s_, ALU.mult, ALU.add),
                      lambda: dve.tensor_scalar(small[:, 44:46], acc, -8.0, None, ALU.mult)]
            for n, step in enumerate(chain):
                step().then_inc(V.sem, V.mark("softplus", n))
                after_v("softplus", n)

            for l in range(LAYERS):
                split_h(l, "in", "pre_mix" if l == 0 else f"attn{l}")
                block1() if l == 0 else rwkv(l)
                residual(l, "mixed", "post_mix" if l == 0 else None)
                split_h(l, "ffn", "pre_ffn" if l == 0 else f"ffn{l}")
                ffn(l)
                residual(l, "fed", "post_ffn" if l == 0 else None)
            after_a("final_rstd")
            for k in range(KT):
                dve.scalar_tensor_tensor(xg[:, k, :], x[:, k, :], Par("final", k), rstd[:, :], ALU.mult, ALU.mult)\
                    .then_inc(V.sem, V.mark("final", k))

    return {"V": V.log, "A": A.log, "M": M.log}


def lay_out(inputs):
    f = lambda n: np.asarray(inputs[n])
    rows = lambda w: w.reshape(-1, P, w.shape[-1]).transpose(1, 0, 2)
    wide = lambda v: v.reshape(-1, P).T

    w = np.zeros((NCH, P, CH), np.float32)
    for c, (l, kind, i, n) in enumerate(STREAM):
        m = l - 1
        if kind == "in":
            src = f("w_in")[0] if l == 0 else f("w_in_2")[m]
            part = np.concatenate([src[:, a:b] for a, b in (IN1 if l == 0 else IN2)[i]], 1)
        elif kind == "uq":
            q = f("c_w_uq_2")[m].reshape(256, 4, 192)
            part = np.concatenate([q[:, :, :P].reshape(256, 512), q[:, :, P:].reshape(256, 256)], 1)
        elif kind == "ukv":
            kv = f("c_w_ukv_2")[m].reshape(P, 4, 256)
            part = np.concatenate([kv[:, :, :P].reshape(P, 512), kv[:, :, P:].reshape(P, 512)], 1)
        elif kind == "out":
            part = (f("w_out")[0] if l == 0 else f("w_out_2")[m])[:, i * 256:(i + 1) * 256]
        elif kind == "gu":
            g, u = (f("w_ffn_gate")[0], f("w_ffn_up")[0]) if l == 0 else (f("ffn_w_gate_2")[m], f("ffn_w_up_2")[m])
            part = np.concatenate([v[:, i * P:(i + 1) * P] for v in (g, u)], 1)
        else:
            part = (f("w_ffn_down")[0] if l == 0 else f("ffn_w_down_2")[m])[i * 256:(i + 1) * 256]
        w[c, :, 0:n] = rows(part).reshape(P, n)

    par = np.zeros((P, NPAR), np.float32)

    def put(name, v):
        a, b = PAR_AT[name]
        par[:, a:b] = v

    for name, key in (("pre_mix", "pre_mix_norm"), ("post_mix", "post_mix_norm"), ("pre_ffn", "pre_ffn_norm"),
                      ("post_ffn", "post_ffn_norm"), ("conv_b", "lru_conv_b"), ("ba", "lru_ba"), ("bx", "lru_bx"),
                      ("lam", "lru_lambda"), ("gate_b", "gla_gate_b"), ("gla_norm", "gla_norm")):
        put(name, wide(f(key)[0]))
    put("conv_w", f("lru_conv_w")[0].reshape(4, 2, P).transpose(2, 0, 1).reshape(P, 8))
    put("final", wide(f("final_norm_g_2")))
    for l in (1, 2):
        for name, key in (("attn", "attn_norm_g_2"), ("w0", "a_w0_2"), ("a0", "a_a0_2"), ("k_k", "a_k_k_2"),
                          ("k_a", "a_k_a_2"), ("ln_w", "a_ln_w_2"), ("ln_b", "a_ln_b_2"), ("qn", "c_q_norm_g_2"),
                          ("kvn", "c_kv_norm_g_2"), ("ffn", "ffn_norm_g_2"), ("r_k", "a_r_k_2")):
            put(f"{name}{l}", wide(f(key)[l - 1].reshape(-1)))
        mu = f("a_mu_2")[l - 1]
        r, k, v, lora, g = mu[0:256], mu[256:512], mu[512:768], mu[768:896], mu[896:1056]
        cols = np.zeros((P, 9), np.float32)
        cols[:, 0], cols[:, 1] = lora, g[:P]
        cols[:, 2:4], cols[:, 4:6], cols[:, 6:8] = wide(k), wide(r), wide(v)
        cols[64:96, 8] = g[P:]
        put(f"mu{l}", cols)

    mat = np.zeros((LAYERS, P, NMAT), np.float32)
    for name, key in (("wa", "lru_wa"), ("wx", "lru_wx")):
        a, _ = MAT1_AT[name]
        for j in range(4):
            rows_, at = slice(64 * (j % 2), 64 * (j % 2) + 64), a + P * (j // 2) + 64 * (j % 2)
            mat[0, rows_, at:at + 64] = f(key)[0, j]
    mat[0, 0:16, slice(*MAT1_AT["gate_w2"])] = f("gla_gate_w2")[0]
    mat[0, 0:32, slice(*MAT1_AT["rel"])] = f("rel_bias")
    for l in (1, 2):
        mat[l, 0:64, slice(*MAT2_AT["lora"])] = f("a_decay_up_2")[l - 1]
        mat[l, 64:128, slice(*MAT2_AT["lora"])] = f("a_iclr_up_2")[l - 1]
        mat[l, :, slice(*MAT2_AT["gate_up"])] = f("a_gate_up_2")[l - 1, :P]
        mat[l, 64:96, slice(*MAT2_AT["gate_up2"])] = f("a_gate_up_2")[l - 1, P:]

    dist = 255 - np.arange(384)
    onehot = np.zeros((40, 384), np.float32)
    onehot[t5_bucket(dist), np.arange(384)] = dist >= 0
    onehot[32:40] = np.where(dist >= 0, 0.0, NEG)
    return {
        "w": w, "params": par, "mat": mat, "onehot": onehot,
        "consts": np.concatenate(list(CONST_ARRAYS.values()), 1),
        "x": f("x")[0].T.reshape(KT, P, T).transpose(1, 0, 2).reshape(P, KT * T),
        "pos": f("positions_2"),
    }


def kernel(**inputs):
    from concourse import bacc
    from concourse.bass_utils import run_bass_kernel_spmd

    arrays = {f"in_{name}": np.ascontiguousarray(a) for name, a in lay_out(inputs).items()}

    def build(plan):
        nc = bacc.Bacc("TRN2", target_bir_lowering=False, num_devices=1)
        ins = {name[3:]: nc.dram_tensor(name, a.shape, mybir.dt.from_np(a.dtype), kind="ExternalInput").ap()
               for name, a in arrays.items()}
        ins["pos"] = ins["pos"].broadcast_to([P, T])
        scratch = nc.dram_tensor("bias_rows", [8, 384], F32, kind="Internal")
        ins["scratch"] = scratch.ap()
        ins["hankel"] = bass.AP(scratch, 0, [[1, P], [384, 8], [1, T]])
        out = nc.dram_tensor("out", [P, KT * T], F32, kind="ExternalOutput").ap()
        return nc, program(nc, ins, out, plan)

    _, plan = build({})
    nc, _ = build(plan)
    got = run_bass_kernel_spmd(nc, [arrays], core_ids=[0]).results[0]["out"]
    return got.reshape(P, KT, T).transpose(2, 1, 0).reshape(1, T, D)
```

```python
import math
from contextlib import ExitStack

import numpy as np

import concourse.bass as bass
from concourse import mybir

ALU = mybir.AluOpType
ACT = mybir.ActivationFunctionType
AX = mybir.AxisListType
F32 = mybir.dt.float32
F32R = mybir.dt.float32r
I32 = mybir.dt.int32
U32 = mybir.dt.uint32

P = 128
D = 1024
KT = D // P
T = 256
TT = T // P
D_FF = 2816
FT = D_FF // P
CH = 2048
RING = 3
NEG = -1e30
EPS = 1e-6
LAYERS = 3

B1_SPLITS = dict(lru_x=256, lru_g=256, gq=128, gk=128, gv=256, g_lr=16, g_out=256, mq=512, mk=512, mv=512)
B2_SPLITS = dict(r=256, k=256, v=256, xw=64, xa=64, xg=160, bq=256, bk=256, bv=256, cq=256, ckv=128, kr=64)


def columns(splits):
    at, out = 0, {}
    for name, width in splits.items():
        out[name] = at
        at += width
    return out


C1, C2 = columns(B1_SPLITS), columns(B2_SPLITS)


def span(c, name, a, b):
    return (c[name] + a, c[name] + b)


IN1 = [
    [span(C1, "lru_x", 0, 256)],
    [span(C1, "g_lr", 0, 16), span(C1, "gk", 0, 128)],
    [span(C1, "gq", 0, 128), span(C1, "mq", 0, 128)],
    [span(C1, "gv", 0, 256)],
    [span(C1, "lru_g", 0, 256)],
    [span(C1, "g_out", 0, 256)],
    [span(C1, "mk", 0, 256)],
    [span(C1, "mq", 128, 384)],
    [span(C1, "mk", 256, 512)],
    [span(C1, "mq", 384, 512)],
    [span(C1, "mv", 0, 256)],
    [span(C1, "mv", 256, 512)],
]
IN2 = [
    [span(C2, "xw", 0, 64), span(C2, "xa", 0, 64), span(C2, "xg", 0, 128)],
    [span(C2, "k", 0, 256)],
    [span(C2, "r", 0, 256)],
    [span(C2, "v", 0, 256)],
    [span(C2, "kr", 0, 64), span(C2, "xg", 128, 160), span(C2, "ckv", 0, 128)],
    [span(C2, "cq", 0, 256)],
    [span(C2, "bq", 0, 256)],
    [span(C2, "bk", 0, 256)],
    [span(C2, "bv", 0, 256)],
]


def stream():
    out = []
    for l in range(LAYERS):
        for i, spans in enumerate(IN1 if l == 0 else IN2):
            out.append((l, "in", i, KT * sum(b - a for a, b in spans)))
        if l:
            out += [(l, "uq", 0, 2 * 768), (l, "ukv", 0, 1024)]
        out += [(l, "out", i, CH) for i in range(4)]
        out += [(l, "gu", 0, CH), (l, "gu", 1, CH)]
        for p in range(1, FT // 2):
            out += [(l, "gu", 2 * p, CH), (l, "gu", 2 * p + 1, CH), (l, "down", p - 1, CH)]
        out.append((l, "down", FT // 2 - 1, CH))
    return out


STREAM = stream()
NCH = len(STREAM)
CHUNK = {(l, kind, i): n for n, (l, kind, i, _) in enumerate(STREAM)}

CONSTS = {}


def t5_bucket(n):
    n = np.maximum(n, 0)
    nf = np.maximum(n, 1).astype(np.float32)
    large = 16 + (np.log(nf / 16).astype(np.float32) / np.float32(math.log(8)) * 16).astype(np.int32)
    return np.where(n < 16, n, np.minimum(large, 31))


def block_ones(size):
    i = np.arange(P) // size
    return (i[:, None] == i[None, :]).astype(np.float32)


def constants():
    i = np.arange(P)
    out = {"ident": np.eye(P), "ones": np.ones((P, P)), "bones": block_ones(64)}
    out["gla_mask"] = block_ones(64) * (i[:, None] <= i[None, :])
    out["flip"] = np.eye(P)[::-1]
    out["before"] = np.stack([i[:, None] < i[None, :], i[:, None] <= i[None, :]], 1).reshape(P, 2 * P)
    for n in range(7):
        b = i >> n
        out[f"level{n}"] = (b[None, :] % 2 == 1) & (b[:, None] == b[None, :] - 1)
    q = np.concatenate([np.tile(P + i[:, None], (1, T)), np.tile(i[:, None], (1, P))], 1)
    k = np.concatenate([np.tile(np.arange(T), (P, 1)), np.tile(i, (P, 1))], 1)
    dist = q - k
    out["causal"] = np.where(dist >= 0, 0.0, NEG)
    count = (dist <= 128).astype(int) + (dist % 4 == 0) + (dist % 16 == 0)
    out["dilated"] = np.where((dist >= 0) & (count > 0), np.log(np.maximum(count, 1)), NEG)
    rb, rc = np.zeros((P, P)), np.zeros((P, P))
    for h in (0, 64):
        for j in range(8):
            rb[h + j + 8, h + j], rb[h + j, h + j + 8] = -1, 1
        for j in range(32):
            rc[h + j + 32, h + j], rc[h + j, h + j + 32] = -1, 1
    dup = np.zeros((P, P))
    dup[i % 64, i] = 1
    out |= {"rot_b": rb, "rot_c": rc, "dup": dup}
    dupr = np.zeros((P, P))
    dupr[:64] = rc[:64, :64] @ dup[:64]
    out["dup_rot"] = dupr
    freq = np.zeros((P, 4), np.float32)
    for h in (0, 64):
        for j in range(8):
            freq[[h + j, h + j + 8], 0] = np.float32(1.0) / np.float32(500000.0) ** np.float32(2 * j / 16)
        for j in range(32):
            freq[[h + j, h + j + 32], 1] = np.float32(1.0) / np.float32(500000.0) ** np.float32(2 * j / 64)
    freq[:, 2], freq[:, 3] = EPS, 64e-5
    out["freq"] = freq
    return {k: np.asarray(v, np.float32) for k, v in out.items()}


def offsets(widths):
    at, out = 0, {}
    for name, width in widths:
        out[name] = (at, at + width)
        at += width
    return out, at


CONST_ARRAYS = constants()
CONST_AT, NCONST = offsets([(k, v.shape[1]) for k, v in CONST_ARRAYS.items()])
PAR_AT, NPAR = offsets([("pre_mix", 8), ("post_mix", 8), ("pre_ffn", 8), ("post_ffn", 8), ("conv_w", 8),
                        ("conv_b", 2), ("ba", 2), ("bx", 2), ("lam", 2), ("gate_b", 1), ("gla_norm", 2)]
                       + [(f"{n}{l}", w) for l in (1, 2) for n, w in
                          (("attn", 8), ("mu", 9), ("w0", 2), ("a0", 2), ("k_k", 2), ("k_a", 2), ("r_k", 2),
                           ("ln_w", 2), ("ln_b", 2), ("qn", 2), ("kvn", 1), ("ffn", 8))]
                       + [("final", 8)])
MAT1_AT, NMAT1 = offsets([("wa", 256), ("wx", 256), ("gate_w2", 128), ("rel", 8)])
MAT2_AT, NMAT2 = offsets([("lora", 256), ("gate_up", 256), ("gate_up2", 256)])
NMAT = max(NMAT1, NMAT2)


class Steps:

    def __init__(self, sem, names):
        self.sem, self.names, self.n = sem, names or [], 0
        self.value = {name: i + 1 for i, name in enumerate(self.names)}
        self.log = []

    def at(self, *name):
        name = "_".join(map(str, name))
        return self.value[name] if self.names else 1

    def mark(self, *name):
        name = "_".join(map(str, name))
        self.log.append(name)
        if self.names:
            assert self.names[self.n] == name, (self.names[self.n], name)
        self.n += 1
        return 1


def program(nc, ins, out, plan):
    with ExitStack() as ctx:
        def sb(name, shape, dt=F32):
            return ctx.enter_context(nc.sbuf_tensor(name, shape, dt))

        def sem(name):
            return ctx.enter_context(nc.semaphore(name))

        x = sb("x", [P, KT, T])
        h_at = nc.sbuf_base
        h_hi, h_lo = sb("h_hi", [P, KT, T], F32R), sb("h_lo", [P, KT, T], F32R)
        mix_hi, mix_lo = sb("mix_hi", [P, KT, T], F32R), sb("mix_lo", [P, KT, T], F32R)
        assert nc.sbuf_base == h_at + 4 * KT * T * 4
        spare = nc.alloc_sbuf_tensor_at("spare", [P, 4, KT, T], F32, offset=h_at)
        raw = sb("raw", [P, RING, CH])
        w_hi, w_lo = sb("w_hi", [P, RING, CH], F32R), sb("w_lo", [P, RING, CH], F32R)
        cst = sb("cst", [P, NCONST])
        par = sb("par", [P, NPAR])
        mat = sb("mat", [P, NMAT])
        rope = sb("rope", [P, 4, T])
        rstd = sb("rstd", [P, T])
        rstd_col = sb("rstd_col", [P, TT])
        ARENA = 18688
        arena = sb("arena", [P, ARENA])
        bank = [ctx.enter_context(nc.psum_tensor(f"bank{i}", [P, 512], F32)) for i in range(8)]

        def pairs(b):
            return bank[b][:, :].rearrange("p (a t) -> p a t", a=2)

        def quads(b):
            return bank[b][:, :].rearrange("p (a t) -> p a t", a=4)

        def C(name):
            a, b = CONST_AT[name]
            return cst[:, a:b]

        def Par(name, i=None, j=None):
            a, b = PAR_AT[name]
            return par[:, a:b] if i is None else par[:, a + i:a + (i + 1 if j is None else j)]

        def area(*tiles):
            at, views = tiles[0], {}
            for name, shape in tiles[1].items():
                n = int(np.prod(shape))
                v = arena[:, at:at + n]
                if len(shape) == 2:
                    v = v.rearrange("p (a b) -> p a b", a=shape[0])
                if len(shape) == 3:
                    v = v.rearrange("p (a b c) -> p a b c", a=shape[0], b=shape[1])
                if len(shape) == 4:
                    v = v.rearrange("p (a b c d) -> p a b c d", a=shape[0], b=shape[1], c=shape[2])
                views[name] = v
                at += n
            assert at <= ARENA, (at, list(tiles[1]))
            return views, at

        NORM, _ = area(ARENA - 4096, dict(xg=(KT, T), sq=(KT, T)))
        xg, sq = NORM["xg"], NORM["sq"]
        FF, _ = area(0, dict(gu=(2, 2, T), sg=(2, T), act=(2, T)))
        act_hi, act_lo = mix_hi[:, 0:4, :], mix_lo[:, 0:4, :]
        B1, b1_end = area(0, dict(
            lx=(2, 259), lg=(2, T), glr=(T,), gk=(T,), gq=(T,), gv=(TT, T), gout=(2, T), mq=(4, T), mk=(4, T),
            mv=(TT, 512), bias=(8, T), lru=(6, 512), qm=(4, T), kd=(T,), ke=(T,), g0=(T,), g1=(T,), g2=(T,),
            keT=(TT, P), att=(TT, 512), st=(3, T), go=(2, T), gt=(2, T), att_l=(2, 384), att_p=(2, 384)))
        REL, _ = area(b1_end - 4 * 768 - 2048, dict(onehot=(384,), relrow=(384,), relneg=(384,), hankel=(8, T)))
        B2, at2 = area(0, dict(
            pm=(9, T), a=(2, T), kkn=(2, T), gate=(2, T), kp=(2, T), kr=(2, 2, 2, P), bh=(2, T), kh=(2, T),
            vt=(TT, T), kbt=(2, T), rs=(T,), nsa=(2, T), s1=(2, P), y=(2, T),
            bq=(2, T), bk=(2, T), bv=(TT, T), cq=(2, T), ckv=(T,), krope=(T,)))
        G2, at3 = area(at2, dict(gram=(8, 4, P)))
        PF, _ = area(at2, dict(pf=(9, 257)))
        INV, _ = area(at3, dict(x=(8, P), xt=(8, P), bt=(8, P)))
        INV["yy"] = area(9 * T, dict(yy=(8, P)))[0]["yy"]
        EARLY, _ = area(at3, dict(sg=(2, T), cs=(2, T), cx=(2, T), ep=(2, T), en=(2, T), t0=(2, T)))
        s_h, s_hl, s_m, s_ml = (spare[:, i, :, :] for i in range(4))
        AT2 = dict(cqs=s_m[:, 0:2, :], ckvs=s_m[:, 2, :], rkv=s_m[:, 3, :],
                   cqn=s_ml[:, 0:2, :], ckvn=s_ml[:, 2, :], rq=s_ml[:, 3, :],
                   t0=s_m[:, 0:2, :], t1=s_m[:, 2:4, :], qn=s_m[:, 4:8, :], kn=s_ml[:, 4:8, :],
                   cv=s_h[:, 3:7, :].rearrange("p (c a) t -> p c (a t)", a=2),
                   qr=s_hl[:, 3:5, :], kro=s_hl[:, 5, :])
        AT2 |= area(0, dict(att_l=(2, 384), att_p=(2, 384)))[0]
        cq_hi, cq_lo = h_hi[:, 0:3, :], h_lo[:, 0:3, :]
        small = sb("small", [P, 96])
        ANG, _ = area(8192 + T, dict(p=(T,), ang=(2, T), n=(T,)))
        pos = arena[:, 8192:8192 + T].bitcast(I32)

        loaded = [sem(f"weights_loaded{i}") for i in range(RING)]
        hi_pool, hi_act = sem("hi_split_by_gpsimd"), sem("hi_split_by_scalar")
        lo_pool, lo_dve = sem("lo_split_by_gpsimd"), sem("lo_split_by_vector")
        tables = sem("constants_loaded")
        x_loaded = sem("x_and_parameters_loaded")
        positions = sem("positions_loaded")
        mats, first_mats = sem("mixer_matrices_loaded"), sem("first_mixer_matrices_loaded")
        bias_tables = sem("bias_tables_loaded")
        rel_out, rel_in = sem("bias_row_stored"), sem("bias_hankel_loaded")
        stored = sem("output_stored")
        V = Steps(sem("vector_step"), plan.get("V"))
        A = Steps(sem("scalar_step"), plan.get("A"))
        M = Steps(sem("tensor_step"), plan.get("M"))

        onehot_in, rel_scratch = ins["onehot"], ins["scratch"]

        by_act = [kind in ("gu", "down") or n == 0 for n, (_, kind, _, _) in enumerate(STREAM)]
        n_hi = [sum(b == by_act[n] for b in by_act[:n + 1]) for n in range(NCH)]

        def split(engine, c):
            engine.wait_ge(lo_dve if by_act[c] else lo_pool, n_hi[c])

        def released(c):
            l, kind, i, _ = STREAM[c]
            return M.at(l, *{"in": ("in", i), "uq": ("up", 2), "ukv": ("up", 6), "out": ("mixed", i),
                             "gu": ("gu", i), "down": ("down", i) if i < FT // 2 - 1 else ("fed", 3)}[kind])

        def of_chunk_sum(n):
            return bank[2][:, n * T:(n + 1) * T].rearrange("p (a t) -> p a t", a=2)

        def projected(l, i):
            return pairs(0 if (l, i) == (0, len(IN1) - 1) else 4 + i % 2)

        block = ctx.enter_context(nc.Block())

        @block.sync
        def _(sp):
            sp.dma_start(par[:, :], ins["params"]).then_inc(x_loaded, 16)
            sp.dma_start(x[:, :, :], ins["x"].rearrange("p (k t) -> p k t", k=KT)).then_inc(x_loaded, 16)
            for c, (l, kind, i, n) in enumerate(STREAM):
                if c == 1:
                    sp.dma_start(cst[:, :], ins["consts"]).then_inc(tables, 16)
                if c >= RING:
                    split(sp, c - RING)
                sp.dma_start(raw[:, c % RING, 0:n], ins["w"][c, :, 0:n]).then_inc(loaded[c % RING], 16)

        @block.gpsimd
        def _(pool):
            for c, (l, kind, i, n) in enumerate(STREAM):
                s = c % RING
                if (kind, i) == ("gu", 0) and l == 0:
                    pool.wait_ge(M.sem, M.at(l, "mixed", 0))
                    pool.wait_ge(V.sem, V.at(l, "mixed", 3))
                    pool.dma_start(pos, ins["pos"]).then_inc(positions, 16)
                if by_act[c]:
                    continue
                pool.wait_ge(loaded[s], 16 * (c // RING + 1))
                if c >= RING:
                    pool.wait_ge(M.sem, released(c - RING))
                pool.tensor_scalar(w_hi[:, s, 0:n], raw[:, s, 0:n], 1.0, 0.0, ALU.mult, ALU.add).then_inc(hi_pool, 1)
                pool.wait_ge(hi_pool, n_hi[c])
                pool.tensor_tensor(w_lo[:, s, 0:n], raw[:, s, 0:n], w_hi[:, s, 0:n].bitcast(F32),
                                   ALU.subtract).then_inc(lo_pool, 1)
                if kind == "out" and i == 3 and l + 1 < LAYERS:
                    pool.wait_ge(M.sem, released(c))
                    pool.dma_start(mat[:, 0:NMAT2], ins["mat"][l + 1, :, 0:NMAT2]).then_inc(mats, 16)

        @block.tensor
        def _(pe):
            def weights(c, view):
                s = c % RING
                return view(w_hi[:, s, :]), view(w_lo[:, s, :])

            def product(dst, w, k_tiles, act, start=True, stop=True, loose=False, fresh=None):
                n = len(k_tiles)
                for i, k in enumerate(k_tiles):
                    if fresh and k % 2 == 0:
                        pe.wait_ge(V.sem, V.at(*fresh, k // 2))
                    for j, (a, b) in enumerate(((0, 0), (0, 1), (1, 0))):
                        last = pe.matmul(dst, w[a](k), act[b](k), start=start and i == 0 and j == 0,
                                         stop=stop and i == n - 1 and j == 2, skip_group_check=loose)
                return last

            def tile_of(c, k_tiles, width, at, size=P):
                s = c % RING
                return [lambda k, part=part: part[:, s, k * width + at:k * width + at + size]
                        for part in (w_hi, w_lo)]

            H = [lambda k: h_hi[:, k, :], lambda k: h_lo[:, k, :]]
            MX = [lambda k: mix_hi[:, k, :], lambda k: mix_lo[:, k, :]]
            IDENT, ONES, BONES = C("ident"), C("ones"), C("bones")

            def norm_sum(l, what, into=6):
                for k in range(KT):
                    if k % 2 == 0 and what in ("mixed", "fed", "final"):
                        pe.wait_ge(A.sem, A.at(l, what, "sq", k // 2))
                    last = pe.matmul(bank[into][:, 0:T], ONES, sq[:, k, :], start=(k == 0), stop=(k == KT - 1))
                last.then_inc(M.sem, M.mark(l, what, "sum"))

            def project(l, *which):
                for i in which:
                    c = CHUNK[l, "in", i]
                    width = STREAM[c][3] // KT
                    split(pe, c)
                    to = projected(l, i)
                    if i >= 2:
                        pe.wait_ge(V.sem, V.at(l, "in", i - 2))
                    token_major = i in ((3, 10, 11) if l == 0 else (8,))
                    if token_major:
                        s = c % RING
                        for t in range(TT):
                            last = product(to[:, t, 0:width],
                                           [lambda k, p=p: p[:, k, t * P:(t + 1) * P] for p in (h_hi, h_lo)],
                                           range(KT),
                                           [lambda k, p=p: p[:, s, k * width:(k + 1) * width] for p in (w_hi, w_lo)])
                    else:
                        for t in range(2 if width > P else 1):
                            at = t * P if width == 2 * P else t * (width - P)
                            last = product(to[:, t, :], tile_of(c, KT, width, at), range(KT), H,
                                           fresh=(l, "in", "lo") if i == 0 and t == 0 else None)
                    last.then_inc(M.sem, M.mark(l, "in", i))
                    if i == 0:
                        if l == 0:
                            pe.wait_ge(tables, 16)
                        pe.wait_ge(A.sem, A.at(l, "in", "sq"))
                        norm_sum(l, "in")
                    if i == 1:
                        pe.wait_ge(A.sem, A.at(l, "in", "rstd"))
                        for t in range(TT):
                            last = pe.transpose(bank[7][:, t * P:(t + 1) * P], rstd[:, t * P:(t + 1) * P], IDENT)
                        last.then_inc(M.sem, M.mark(l, "in", "rstd"))

            def attend(l, i, heads, scores, value, out_bank):
                v = B1 if l == 0 else AT2
                if i < heads:
                    if i >= 2:
                        pe.wait_ge(A.sem, A.at(l, "turned", i - 2))
                    scores(i, bank[4 + i % 2]).then_inc(M.sem, M.mark(l, "scores", i))
                if 1 <= i <= heads:
                    j = i - 1
                    pe.wait_ge(V.sem, V.at(l, "probs", j))
                    L, b = v["att_l"][:, j % 2, :], bank[4 + j % 2]
                    pe.transpose(b[:, 0:P], L[:, 2 * P:3 * P], IDENT)
                    pe.transpose(b[:, P:2 * P], L[:, 0:P], IDENT)
                    pe.transpose(b[:, 2 * P:3 * P], L[:, P:2 * P], IDENT).then_inc(M.sem, M.mark(l, "turn", j))
                if 2 <= i <= heads + 1:
                    j = i - 2
                    pe.wait_ge(A.sem, A.at(l, "turned", j))
                    PT = v["att_p"][:, j % 2, :]
                    dst = out_bank(j)
                    pe.matmul(dst, value(j, 0), PT[:, 0:T], start=True, stop=False)
                    pe.matmul(dst[:, P:T], value(j, 1), PT[:, T:T + P], start=False, stop=True)\
                        .then_inc(M.sem, M.mark(l, "values", j))

            def w_out(l, m, k_tiles):
                c = CHUNK[l, "out", m]
                begin = not w_out_done[l, m]
                if begin:
                    split(pe, c)
                w_out_done[l, m] += len(k_tiles)
                end = w_out_done[l, m] == KT
                for t in range(2):
                    last = product(pairs(m)[:, t, :], tile_of(c, KT, 2 * P, t * P), k_tiles, MX,
                                   start=begin and t == 0, stop=end and t == 1, loose=True)
                if end:
                    last.then_inc(M.sem, M.mark(l, "mixed", m))

            w_out_done = {(l, m): 0 for l in range(LAYERS) for m in range(4)}

            def ffn(l):
                def gate_up(j):
                    c = CHUNK[l, "gu", j]
                    split(pe, c)
                    if j >= 2:
                        pe.wait_ge(V.sem, V.at(l, "gu", j - 2))
                    for t in range(2):
                        last = product(pairs(4 + j % 2)[:, t, :], tile_of(c, KT, 2 * P, t * P), range(KT), H,
                                       fresh=(l, "ffn", "lo") if j == 0 and t == 0 else None)
                    last.then_inc(M.sem, M.mark(l, "gu", j))
                    if j == 1:
                        pe.wait_ge(A.sem, A.at(l, "ffn", "sq"))
                        norm_sum(l, "ffn")

                def down(p):
                    c = CHUNK[l, "down", p]
                    split(pe, c)
                    for s in range(2):
                        j = 2 * p + s
                        pe.wait_ge(V.sem, V.at(l, "act", "lo", j))
                        for d in range(KT):
                            last = product(pairs(d // 2)[:, d % 2, :], tile_of(c, 2, D, d * P), [s],
                                           [lambda k, q=q: q[:, j % 4, :] for q in (act_hi, act_lo)],
                                           start=(j == 0 and d % 2 == 0), stop=(j == FT - 1), loose=True)
                            if j == FT - 1 and d % 2:
                                last.then_inc(M.sem, M.mark(l, "fed", d // 2))
                    if p < FT // 2 - 1:
                        last.then_inc(M.sem, M.mark(l, "down", p))

                gate_up(0)
                gate_up(1)
                for p in range(1, FT // 2):
                    gate_up(2 * p)
                    gate_up(2 * p + 1)
                    down(p - 1)
                down(FT // 2 - 1)

            def block1():
                l = 0
                Mt = lambda n: mat[:, MAT1_AT[n][0]:MAT1_AT[n][1]]
                pe.wait_ge(first_mats, 16)
                pe.wait_ge(bias_tables, 32)
                pe.matmul(bank[0][0:8, 0:384], Mt("rel")[0:32, :], REL["onehot"][0:32, :], start=True, stop=True)\
                    .then_inc(M.sem, M.mark("rel_row"))
                project(l, 0, 1)
                pe.wait_ge(rel_in, 16)
                for i in range(4):
                    if i >= 2:
                        pe.wait_ge(A.sem, A.at("bias", i - 2))
                    pe.matmul(bank[i % 2][:, :], C("flip"), REL["hankel"][:, 2 * i:2 * i + 2, :].rearrange("p a b -> p (a b)"),
                              start=True, stop=True).then_inc(M.sem, M.mark("bias", i))
                pe.wait_ge(V.sem, V.at(l, "in", 1))
                pe.matmul(bank[6][:, 0:T], Mt("gate_w2")[0:16, :], B1["glr"][0:16, :], start=True, stop=True)\
                    .then_inc(M.sem, M.mark("gla_gate"))
                project(l, 2, 3)
                pe.wait_ge(V.sem, V.at("lru_conv"))
                pe.wait_ge(A.sem, A.at("bias", 3))
                for b, name in ((0, "wa"), (1, "wx")):
                    for t in range(2):
                        last = pe.matmul(pairs(b)[:, t, :], Mt(name)[:, t * P:(t + 1) * P],
                                         B1["lru"][:, 0, t * T:(t + 1) * T], start=True, stop=True)
                last.then_inc(M.sem, M.mark("lru_gates"))
                project(l, 4, 5)
                pe.wait_ge(V.sem, V.at("gla_ke"))
                for t in range(TT):
                    last = pe.matmul(bank[2 + t][:, :].rearrange("p (h t) -> p h t", h=4), B1["kd"][:, t * P:(t + 1) * P],
                                     B1["qm"][:, :, t * P:(t + 1) * P], start=True, stop=True)
                last.then_inc(M.sem, M.mark("gla_scores"))
                for t in range(TT):
                    last = pe.transpose(bank[6][:, t * P:(t + 1) * P], B1["ke"][:, t * P:(t + 1) * P], IDENT)
                last.then_inc(M.sem, M.mark("gla_turn"))
                project(l, 6)
                pe.wait_ge(A.sem, A.at("gla_turned"))
                pe.wait_ge(A.sem, A.at("lru_sig"))
                for n in range(3):
                    half = slice(64 * (n % 2), 64 * (n % 2) + 64)
                    dst = bank[7][:, 0:T] if n == 1 else pairs(0)[:, n // 2, :]
                    last = pe.matmul(dst, B1["keT"][half, n // 2, :], B1["gv"][half, n // 2, :], start=True, stop=True)
                last.then_inc(M.sem, M.mark("gla_kv"))
                project(l, 7)
                pe.wait_ge(V.sem, V.at("gla_att", 1))
                pe.wait_ge(V.sem, V.at("gla_state", 2))
                for pr in range(2):
                    for t in range(TT):
                        for s in range(2):
                            h = 2 * pr + s
                            dst = bank[1][64 * s:64 * s + 64, pr * T + t * P:pr * T + (t + 1) * P]
                            pe.matmul(dst, B1["gv"][:, t, h * 64:(h + 1) * 64],
                                      B1["att"][:, t, h * P:(h + 1) * P], start=True, stop=False)
                            for n in range(2 * t, 2 * t + 2):
                                if n:
                                    last = pe.matmul(dst[:, (n % 2) * 64:(n % 2) * 64 + 64],
                                                     B1["st"][:, n - 1, h * 64:(h + 1) * 64],
                                                     B1["qm"][:, h, n * 64:(n + 1) * 64], start=False,
                                                     stop=(n % 2 == 1))
                last.then_inc(M.sem, M.mark("gla_out"))
                project(l, 8)
                pe.wait_ge(A.sem, A.at("gla_sq"))
                pe.matmul(bank[0][:, :], BONES, B1["gt"].rearrange("p a b -> p (a b)"), start=True, stop=True)\
                    .then_inc(M.sem, M.mark("gla_ss"))

                project(l, 9, 10)
                pe.wait_ge(V.sem, V.at(l, "in", 10))

                def scores(i, b):
                    rows = slice(64 * (i % 2), 64 * (i % 2) + 64)
                    q, k = B1["mq"][rows, i // 2, :], B1["mk"][rows, i // 2, :]
                    pe.matmul(b[:, 0:T], q[:, P:T], k, start=True, stop=True)
                    return pe.matmul(b[:, T:T + P], q[:, 0:P], k[:, 0:P], start=True, stop=True)

                def out_bank(j):
                    return pairs(6 + j // 4)[64 * (j % 2):64 * (j % 2) + 64, (j // 2) % 2, :]

                for i in range(10):
                    if i == 6:
                        pe.wait_ge(V.sem, V.at(l, "in", 11))
                    attend(l, i, 8, scores, lambda j, t: B1["mv"][:, t, j * 64:(j + 1) * 64], out_bank)
                    if i == 1:
                        pe.wait_ge(A.sem, A.at("gla_rstd"))
                        project(l, 11)
                    if i == 3:
                        pe.wait_ge(V.sem, V.at("gla_lo"))
                        pe.wait_ge(V.sem, V.at(l, "in", 11))
                    if 3 <= i < 9:
                        w_out(l, (i - 3) // 2, (0, 1) if i % 2 else (2, 3))

            def rwkv(l):
                Mt = lambda n: mat[:, MAT2_AT[n][0]:MAT2_AT[n][1]]
                pm, kr, bh, kh, gram = B2["pm"], B2["kr"], B2["bh"], B2["kh"], G2["gram"]
                project(l, 0, 1)
                pe.wait_ge(A.sem, A.at(l, "lora_in"))
                for t in range(2):
                    pe.matmul(pairs(0)[:, t, :], Mt("lora")[0:64, t * P:(t + 1) * P], pm[0:64, 0, :],
                              start=True, stop=True)
                for t in range(2):
                    last = pe.matmul(pairs(1)[:, t, :], Mt("lora")[64:128, t * P:(t + 1) * P], pm[64:128, 0, :],
                                     start=True, stop=True)
                last.then_inc(M.sem, M.mark(l, "lora"))
                project(l, 2)
                pe.wait_ge(A.sem, A.at(l, "kk_sq"))
                pe.matmul(bank[3][:, :], BONES, EARLY["t0"].rearrange("p a b -> p (a b)"), start=True, stop=True)\
                    .then_inc(M.sem, M.mark(l, "kk_ss"))
                project(l, 3, 4)
                pe.wait_ge(A.sem, A.at(l, "gate_in"))
                for t in range(2):
                    pe.matmul(pairs(2)[:, t, :], Mt("gate_up")[:, t * P:(t + 1) * P], pm[:, 1, :],
                              start=True, stop=False)
                    last = pe.matmul(pairs(2)[:, t, :], Mt("gate_up2")[64:96, t * P:(t + 1) * P], pm[64:96, 8, :],
                                     start=False, stop=True)
                last.then_inc(M.sem, M.mark(l, "gate"))
                for c in range(TT):
                    for t in range(2):
                        last = pe.transpose(bank[6][:, c * T + t * P:c * T + (t + 1) * P],
                                            pm[:, 6 + t, c * P:(c + 1) * P], IDENT)
                last.then_inc(M.sem, M.mark(l, "v_turn"))
                project(l, 5)
                pe.wait_ge(V.sem, V.at(l, "bonus_in"))
                pe.matmul(bank[3][:, :], BONES, EARLY["t0"].rearrange("p a b -> p (a b)"), start=True, stop=True)\
                    .then_inc(M.sem, M.mark(l, "bonus"))
                pe.wait_ge(V.sem, V.at(l, "kr"))
                for n, m in enumerate((kh, bh)):
                    for t in range(2):
                        last = pe.transpose(bank[7][:, n * T + t * P:n * T + (t + 1) * P], m[:, t, 0:P], IDENT)
                last.then_inc(M.sem, M.mark(l, "kb_turn"))
                for g in range(8):
                    c, t, rows = g // 4, (g % 4) // 2, slice(64 * (g % 2), 64 * (g % 2) + 64)
                    if g >= 4:
                        pe.wait_ge(V.sem, V.at(l, "gram", g - 4))
                    elif g == 2:
                        pe.wait_ge(A.sem, A.at(l, "gate"))
                    elif g == 3:
                        pe.wait_ge(V.sem, V.at(l, "bonus"))
                    for n, m in enumerate((bh, kh)):
                        last = pe.matmul(pairs(g % 4)[:, n, :], m[rows, t, c * P:(c + 1) * P],
                                         kr[rows, t, c, :, :].rearrange("p a b -> p (a b)"), start=True, stop=True)
                    last.then_inc(M.sem, M.mark(l, "gram", g))
                project(l, 6)
                pe.wait_ge(A.sem, A.at(l, "c_sq"))
                pe.matmul(bank[6][:, 0:T], ONES, AT2["cqs"][:, 0, :], start=True, stop=False)
                pe.matmul(bank[6][:, 0:T], ONES, AT2["cqs"][:, 1, :], start=False, stop=True)
                pe.matmul(bank[6][:, T:2 * T], ONES, AT2["ckvs"], start=True, stop=True)\
                    .then_inc(M.sem, M.mark(l, "c_ss"))
                Xm, XT, BT, Y = INV["x"], INV["xt"], INV["bt"], INV["yy"]
                for q in range(2):
                    pe.wait_ge(V.sem, V.at(l, "inv0", q))
                    for m in range(4):
                        last = pe.transpose(bank[q][:, m * P:(m + 1) * P], XT[:, 4 * q + m, :], IDENT)
                    last.then_inc(M.sem, M.mark(l, "inv0", q))
                project(l, 7)
                for n in range(1, 7):
                    for q in range(2):
                        pe.wait_ge(V.sem, V.at(l, "inv_bt", n, q))
                        pe.wait_ge(A.sem, A.at(l, "inv0", q)) if n == 1 else pe.wait_ge(V.sem, V.at(l, "inv_x", n - 1, q))
                        for m in range(4 * q, 4 * q + 4):
                            last = pe.matmul(quads(q)[:, m % 4, :], BT[:, m, :], Xm[:, m, :], start=True, stop=True)
                        last.then_inc(M.sem, M.mark(l, "inv_y", n, q))
                    beside_inverse(l, n)
                    for q in range(2):
                        pe.wait_ge(A.sem, A.at(l, "inv_y", n, q))
                        for m in range(4 * q, 4 * q + 4):
                            last = pe.matmul(quads(2 + q)[:, m % 4, :], Y[:, m, :], XT[:, m, :], start=True, stop=True)
                        last.then_inc(M.sem, M.mark(l, "inv_zt", n, q))
                        if n < 6:
                            for m in range(4 * q, 4 * q + 4):
                                last = pe.matmul(quads(q)[:, m % 4, :], XT[:, m, :], Y[:, m, :], start=True,
                                                 stop=True)
                            last.then_inc(M.sem, M.mark(l, "inv_z", n, q))
                    if n >= 5:
                        attention(l, 2 * n - 9)
                def of_chunk(v, c):
                    return v[:, :, c * P:(c + 1) * P]

                def mean_of(c):
                    pe.wait_ge(A.sem, A.at(l, "y", c))
                    pe.matmul(of_chunk_sum(0), BONES, of_chunk(B2["y"], c), start=True, stop=True)\
                        .then_inc(M.sem, M.mark(l, "mean", c))

                def variance_of(c):
                    pe.wait_ge(A.sem, A.at(l, "y_sq", c))
                    pe.matmul(of_chunk_sum(1), BONES, of_chunk(EARLY["sg"], c), start=True, stop=True)\
                        .then_inc(M.sem, M.mark(l, "var", c))

                vt, kbt, rs, nsa, s1 = B2["vt"], B2["kbt"], B2["rs"], B2["nsa"], B2["s1"]
                for c in range(TT):
                    pe.wait_ge(V.sem, V.at(l, "inv_xt", 6, c))
                    if c:
                        pe.wait_ge(V.sem, V.at(l, "s1"))
                    for h in range(4):
                        t, cols = h // 2, slice(h * 64, (h + 1) * 64)
                        if c and h % 2 == 0:
                            pe.matmul(bank[0][:, t * P:(t + 1) * P], kr[:, t, 1, 0, :], s1[:, t, :],
                                      start=True, stop=False)
                        last = pe.matmul(bank[0][:, cols], gram[:, 4 * c + h, 2, :], vt[:, c, cols],
                                         start=(c == 0), stop=(c == 0 or h % 2 == 1))
                    last.then_inc(M.sem, M.mark(l, "r", c))
                    if c:
                        mean_of(0)
                    attention(l, 4 + 3 * c)
                    pe.wait_ge(A.sem, A.at(l, "r", c))
                    for h in range(4):
                        cols = slice(h * 64, (h + 1) * 64)
                        last = pe.matmul(bank[1][:, cols], INV["xt"][:, 4 * c + h, :], rs[:, cols],
                                         start=True, stop=True)
                    last.then_inc(M.sem, M.mark(l, "sa", c))
                    if c:
                        variance_of(0)
                    attention(l, 5 + 3 * c)
                    pe.wait_ge(V.sem, V.at(l, "nsa", c))
                    if c == 0:
                        for h in range(4):
                            t, rows, cols = h // 2, slice(64 * (h % 2), 64 * (h % 2) + 64), slice(h * 64, (h + 1) * 64)
                            pe.matmul(bank[2][rows, t * 64:(t + 1) * 64], kbt[:, 0, cols], vt[:, 0, cols],
                                      start=True, stop=False)
                            last = pe.matmul(bank[2][rows, t * 64:(t + 1) * 64], kbt[:, 1, cols], nsa[:, 0, cols],
                                             start=False, stop=True)
                        last.then_inc(M.sem, M.mark(l, "s1"))
                    for h in range(4):
                        t, rows, cols = h // 2, slice(64 * (h % 2), 64 * (h % 2) + 64), slice(h * 64, (h + 1) * 64)
                        both = pairs(3)[:, t, 0:P]
                        dst = both[rows, :]
                        if c and h == 0:
                            pe.wait_ge(A.sem, A.at(l, "y", 0))
                        if c and h % 2 == 0:
                            pe.matmul(both, s1[:, t, :], kr[:, t, 1, 1, :], start=True, stop=False)
                        pe.matmul(dst, vt[:, c, cols], gram[:, 4 * c + h, 3, :], start=(c == 0), stop=False)
                        last = pe.matmul(dst, nsa[:, c, cols], gram[:, 4 * c + h, 1, :], start=False, stop=True)
                    last.then_inc(M.sem, M.mark(l, "y", c))
                    attention(l, 6 + 3 * c)
                mean_of(1)
                pe.wait_ge(V.sem, V.at(l, "nsa", 1))
                pe.wait_ge(V.sem, V.at(l, "b_lo"))
                w_out(l, 0, (2, 3))
                variance_of(1)
                pe.wait_ge(V.sem, V.at(l, "c_lo", 1))
                w_out(l, 0, range(4, KT))
                w_out(l, 1, range(2, KT))

            def beside_inverse(l, n):
                b = AT2
                CQ = [lambda k: cq_hi[:, k, :], lambda k: cq_lo[:, k, :]]
                CKV = [lambda k: cq_hi[:, 2, :], lambda k: cq_lo[:, 2, :]]

                def up(i):
                    c = CHUNK[l, "uq" if i < 3 else "ukv", 0]
                    if i in (0, 3):
                        split(pe, c)
                    if i >= 2:
                        pe.wait_ge(A.sem, A.at(l, "up", i - 2))
                    if i < 3:
                        for t in range(2):
                            last = product(pairs(4 + i % 2)[:, t, :], tile_of(c, 2, 768, (2 * i + t) * P), range(2), CQ)
                    elif i < 5:
                        for t in range(2):
                            last = product(pairs(4 + i % 2)[:, t, :], tile_of(c, 1, 1024, (2 * (i - 3) + t) * P), [0],
                                           CKV)
                    else:
                        s, t = c % RING, i - 5
                        last = product(bank[4 + i % 2][:, :],
                                       [lambda k, p=p: p[:, 2, t * P:(t + 1) * P] for p in (cq_hi, cq_lo)], [0],
                                       [lambda k, p=p: p[:, s, 512:1024] for p in (w_hi, w_lo)])
                    last.then_inc(M.sem, M.mark(l, "up", i))

                if n == 1:
                    project(l, 8)
                if n == 2:
                    pe.wait_ge(V.sem, V.at(l, "in", 7))
                    pe.wait_ge(A.sem, A.at(l, "rkv"))
                    pe.wait_ge(A.sem, A.at(l, "kb_turned"))
                    pe.matmul(bank[6][:, :], C("rot_b"), B2["bq"].rearrange("p a b -> p (a b)"), start=True, stop=True)
                    pe.matmul(bank[7][:, :], C("rot_b"), B2["bk"].rearrange("p a b -> p (a b)"), start=True, stop=True)\
                        .then_inc(M.sem, M.mark(l, "b_rot"))
                    pe.wait_ge(V.sem, V.at(l, "c_lo"))
                    up(0)
                    up(1)
                if n == 3:
                    pe.wait_ge(V.sem, V.at(l, "rotated", 0))
                    pe.matmul(bank[6][:, 0:T], C("dup")[0:64, :], B2["krope"][0:64, :], start=True, stop=True)
                    pe.matmul(bank[6][:, T:2 * T], C("dup_rot")[0:64, :], B2["krope"][0:64, :], start=True, stop=True)\
                        .then_inc(M.sem, M.mark(l, "k_rot"))
                    for i in range(2, 5):
                        up(i)
                if n == 4:
                    pe.wait_ge(V.sem, V.at(l, "rotated", 1))
                    pe.matmul(bank[7][:, :], C("rot_c"), b["qr"].rearrange("p a b -> p (a b)"), start=True, stop=True)\
                        .then_inc(M.sem, M.mark(l, "q_rot"))
                    up(5)
                    up(6)
                if n >= 5:
                    attention(l, 2 * n - 10)

            def attention(l, i):
                def scores(i, b):
                    rows = slice(64 * (i % 2), 64 * (i % 2) + 64)
                    if i < 4:
                        q, k = B2["bq"][rows, i // 2, :], B2["bk"][rows, i // 2, :]
                        pe.matmul(b[:, 0:T], q[:, P:T], k, start=True, stop=True)
                        return pe.matmul(b[:, T:T + P], q[:, 0:P], k[:, 0:P], start=True, stop=True)
                    q, k = AT2["qn"][:, i - 4, :], AT2["kn"][:, i - 4, :]
                    qr, kr = AT2["qr"][rows, i // 2 - 2, :], AT2["kro"][rows, :]
                    pe.matmul(b[:, 0:T], q[:, P:T], k, start=True, stop=False)
                    pe.matmul(b[:, 0:T], qr[:, P:T], kr, start=False, stop=True)
                    pe.matmul(b[:, T:T + P], q[:, 0:P], k[:, 0:P], start=True, stop=False)
                    return pe.matmul(b[:, T:T + P], qr[:, 0:P], kr[:, 0:P], start=False, stop=True)

                def value(j, t):
                    return B2["bv"][:, t, j * 64:(j + 1) * 64] if j < 4 else AT2["cv"][:, t, (j - 4) * P:(j - 3) * P]

                def out_bank(j):
                    if j < 4:
                        return pairs(6)[64 * (j % 2):64 * (j % 2) + 64, j // 2, :]
                    return pairs(7 if j < 6 else 6)[:, j % 2, :]

                if i == 0:
                    pe.wait_ge(V.sem, V.at(l, "c_rope"))
                    pe.wait_ge(A.sem, A.at(l, "up", 6))
                if i == 8:
                    pe.wait_ge(V.sem, V.at(l, "b_lo"))
                attend(l, i, 8, scores, value, out_bank)

            for l in range(LAYERS):
                if l:
                    pe.wait_ge(mats, 16 * l)
                if l == 0:
                    block1()
                    pe.wait_ge(V.sem, V.at("moba_lo", 0))
                    for m in range(3):
                        w_out(l, m, (4, 5))
                    pe.wait_ge(V.sem, V.at("moba_lo"))
                    for m in range(4):
                        w_out(l, m, (6, 7) if m < 3 else range(KT))
                else:
                    rwkv(l)
                    pe.wait_ge(V.sem, V.at(l, "a_lo", 1))
                    for m in range(4):
                        w_out(l, m, (0, 1) if m < 2 else range(KT))
                if l == 0:
                    norm_sum(l, "mixed")
                ffn(l)
                if l == 0:
                    norm_sum(l, "fed")
            norm_sum(LAYERS, "final")

        @block.scalar
        def _(act):
            Mc = lambda name: C("freq")[:, 2:3] if name == "eps" else C("freq")[:, 3:4]

            def copy(dst, src, **kw):
                return act.activation(dst, src, ACT.Copy, **kw)

            def hi_of(c):
                l, kind, i, n = STREAM[c]
                act.wait_ge(loaded[c % RING], 16 * (c // RING + 1))
                act.wait_ge(M.sem, released(c - RING))
                copy(w_hi[:, c % RING, 0:n], raw[:, c % RING, 0:n]).then_inc(hi_act, 1)

            def inverse_root(dst, src, scale, bias, name, power=-0.5):
                act.activation(dst, src, ACT.Ln, bias=bias, scale=scale).then_inc(A.sem, A.mark(*name, "ln"))
                act.wait_ge(A.sem, A.at(*name, "ln"))
                act.activation(dst, dst, ACT.Exp, scale=power).then_inc(A.sem, A.mark(*name))

            def hi_of_x(l, what, g, m):
                if not (l == 0 and what == "in"):
                    act.wait_ge(V.sem, V.at(*((l, "mixed") if what == "ffn" else (l - 1, "fed")), m))
                for k in (2 * m, 2 * m + 1):
                    last = act.activation(h_hi[:, k, :], x[:, k, :], ACT.Copy, scale=Par(g, k))
                last.then_inc(A.sem, A.mark(l, what, "hi", m))

            def square(l, what):
                act.activation(sq[:, :, :], x[:, :, :], ACT.Square).then_inc(A.sem, A.mark(l, what, "sq"))

            def norm_factor(l, what, tag):
                act.wait_ge(M.sem, M.at(l, tag, "sum"))
                inverse_root(rstd[:, :], bank[6][:, 0:T], 1.0 / D, Mc("eps"), (l, what, "rstd"))

            def attend(l, i, heads):
                v = B1 if l == 0 else AT2
                if 1 <= i <= heads:
                    j = i - 1
                    act.wait_ge(M.sem, M.at(l, "turn", j))
                    if j >= 2:
                        act.wait_ge(M.sem, M.at(l, "values", j - 2))
                    copy(v["att_p"][:, j % 2, :], bank[4 + j % 2][:, 0:3 * P])\
                        .then_inc(A.sem, A.mark(l, "turned", j))
                if i < heads:
                    act.wait_ge(V.sem, V.at(l, "max", i))
                    L, o = v["att_l"][:, i % 2, :], 2 * (i % 2)
                    act.activation(L[:, 0:T], L[:, 0:T], ACT.Exp, bias=small[:, 8 + o:9 + o],
                                   accum_out=small[:, 16 + o:17 + o])
                    act.activation(L[:, T:T + P], L[:, T:T + P], ACT.Exp, bias=small[:, 9 + o:10 + o],
                                   accum_out=small[:, 17 + o:18 + o]).then_inc(A.sem, A.mark(l, "exp", i))

            def mix(t, src, name):
                copy(mix_hi[:, t:t + 2, :], src).then_inc(A.sem, A.mark(*name))

            def ffn(l):
                c0 = CHUNK[l, "gu", 0]
                square(l, "ffn")
                todo = list(range(c0 + RING, CHUNK[l, "down", FT // 2 - 1] + 1))

                def after(c):
                    if todo and todo[0] <= c + RING:
                        hi_of(todo.pop(0))

                def silu(j):
                    if j >= 1:
                        act.wait_ge(V.sem, V.at(l, "act", "lo", j - 1))
                    act.wait_ge(V.sem, V.at(l, "gu", j))
                    act.activation(FF["sg"][:, j % 2, :], FF["gu"][:, j % 2, 0, :], ACT.Silu)\
                        .then_inc(A.sem, A.mark(l, "silu", j))
                    act.wait_ge(V.sem, V.at(l, "act", j))
                    copy(act_hi[:, j % 4, :], FF["act"][:, j % 2, :]).then_inc(A.sem, A.mark(l, "act", "hi", j))

                after(c0)
                after(c0 + 1)
                norm_factor(l, "ffn", "ffn")
                silu(0)
                silu(1)
                for p in range(1, FT // 2):
                    for j in (2 * p, 2 * p + 1):
                        after(CHUNK[l, "gu", j])
                        silu(j)
                    after(CHUNK[l, "down", p - 1])
                    if l == 0 and p == 5:
                        act.wait_ge(V.sem, V.at("angles"))
                        for i in range(4):
                            last = act.activation(rope[:, i, :], rope[:, i, :], ACT.Sin)
                        last.then_inc(A.sem, A.mark("rope"))
                assert not todo

            def block1():
                l, lru = 0, B1["lru"]
                flat = lambda v: v.rearrange("p a b -> p (a b)")
                act.wait_ge(V.sem, V.at("rel_row"))
                act.dma_start(rel_scratch, REL["relrow"][0:8, :]).then_inc(rel_out, 16)
                act.wait_ge(rel_out, 16)
                act.dma_start(REL["hankel"], ins["hankel"]).then_inc(rel_in, 16)
                for i in range(4):
                    act.wait_ge(M.sem, M.at("bias", i))
                    copy(B1["bias"][:, 2 * i:2 * i + 2, :], pairs(i % 2)).then_inc(A.sem, A.mark("bias", i))
                act.wait_ge(V.sem, V.at("gla_abs"))
                act.activation(B1["g1"], B1["g1"], ACT.Exp, scale=-1.0).then_inc(A.sem, A.mark("gla_e"))
                act.wait_ge(A.sem, A.at("gla_e"))
                act.activation(B1["g1"], B1["g1"], ACT.Ln, bias=1.0).then_inc(A.sem, A.mark("gla_l"))
                act.wait_ge(V.sem, V.at("gla_last"))
                act.activation(B1["g0"], B1["g2"], ACT.Exp, scale=1 / 16).then_inc(A.sem, A.mark("gla_ep"))
                act.activation(B1["g1"], B1["g2"], ACT.Exp, scale=-1 / 16).then_inc(A.sem, A.mark("gla_en"))
                act.activation(small[:, 4:8], small[:, 0:4], ACT.Exp)
                for n in range(4):
                    s = slice(64 * n, 64 * n + 64)
                    last = act.activation(B1["ke"][:, s], B1["g2"][:, s], ACT.Exp, scale=-1 / 16, bias=small[:, n:n + 1])
                last.then_inc(A.sem, A.mark("gla_ee"))
                act.wait_ge(M.sem, M.at("gla_turn"))
                copy(flat(B1["keT"]), bank[6][:, 0:T]).then_inc(A.sem, A.mark("gla_turned"))
                act.wait_ge(M.sem, M.at("lru_gates"))
                for b, name in ((0, "ba"), (1, "bx")):
                    for t in range(2):
                        last = act.activation(lru[:, 1 + b, t * T:(t + 1) * T], pairs(b)[:, t, :], ACT.Sigmoid,
                                              bias=Par(name, t))
                last.then_inc(A.sem, A.mark("lru_sig"))
                act.wait_ge(V.sem, V.at("lru_log"))
                act.activation(lru[:, 3, :], lru[:, 1, :], ACT.Tanh, scale=-1.0).then_inc(A.sem, A.mark("lru_tanh"))
                act.activation(lru[:, 4, :], lru[:, 1, :], ACT.Exp).then_inc(A.sem, A.mark("lru_a"))
                act.wait_ge(V.sem, V.at("lru_m2"))
                act.activation(lru[:, 3, :], lru[:, 3, :], ACT.Sqrt).then_inc(A.sem, A.mark("lru_mult"))
                act.wait_ge(V.sem, V.at(l, "in", 5))
                act.activation(lru[:, 5, :], flat(B1["lg"]), ACT.Gelu_apprx_tanh).then_inc(A.sem, A.mark("lru_gelu"))
                act.activation(flat(B1["gout"]), flat(B1["gout"]), ACT.Silu).then_inc(A.sem, A.mark("gla_silu"))
                act.wait_ge(M.sem, M.at("gla_out"))
                copy(flat(B1["go"]), bank[1][:, :])
                act.activation(flat(B1["gt"]), bank[1][:, :], ACT.Square).then_inc(A.sem, A.mark("gla_sq"))
                act.wait_ge(M.sem, M.at("gla_ss"))
                inverse_root(flat(B1["gt"]), bank[0][:, :], 1 / 64, Mc("eps"), ("gla_rstd",))
                act.wait_ge(V.sem, V.at("lru_y"))
                mix(0, lru[:, 2, :].rearrange("p (a b) -> p a b", a=2), ("lru_hi",))
                act.wait_ge(V.sem, V.at("gla_y"))
                mix(2, B1["go"], ("gla_hi",))
                for i in range(9):
                    attend(l, i, 8)
                act.wait_ge(M.sem, M.at(l, "values", 7))
                mix(4, pairs(6), ("moba_hi", 0))
                mix(6, pairs(7), ("moba_hi", 1))

            def rwkv(l):
                flat = lambda v: v.rearrange("p a b -> p (a b)")
                pm, E, b = B2["pm"], EARLY, AT2
                scale = 192 ** -0.5
                up_to = [b["qn"][:, 0:2, :], b["qn"][:, 2:4, :], b["qr"], b["kn"][:, 0:2, :], b["kn"][:, 2:4, :],
                         b["cv"][:, 0, :], b["cv"][:, 1, :]]

                def beside_inverse(n):
                    if n == 1:
                        act.wait_ge(M.sem, M.at(l, "c_ss"))
                        inverse_root(b["rq"], bank[6][:, 0:T], 1 / 256, Mc("eps"), (l, "rq"))
                        inverse_root(b["rkv"], bank[6][:, T:2 * T], 1 / 128, Mc("eps"), (l, "rkv"))
                        act.wait_ge(M.sem, M.at(l, "in", 8))
                        act.wait_ge(V.sem, V.at(l, "c_n"))
                        copy(cq_hi[:, 0:2, :], b["cqn"])
                        copy(cq_hi[:, 2, :], b["ckvn"]).then_inc(A.sem, A.mark(l, "c_hi"))
                    for i in {2: (0, 1), 3: (2, 3, 4), 4: (5, 6)}.get(n, ()):
                        act.wait_ge(M.sem, M.at(l, "up", i))
                        src = bank[4 + i % 2][:, :] if i >= 5 else pairs(4 + i % 2)
                        act.activation(up_to[i], src, ACT.Copy, scale=scale if i < 3 else 1.0)\
                            .then_inc(A.sem, A.mark(l, "up", i))
                    if n >= 5:
                        attend(l, 2 * n - 10, 8)
                        attend(l, 2 * n - 9, 8)

                def square_of(c):
                    act.wait_ge(V.sem, V.at(l, "yc", c))
                    act.activation(of_chunk(E["sg"], c), of_chunk(B2["y"], c), ACT.Square)\
                        .then_inc(A.sem, A.mark(l, "y_sq", c))

                def root_of(c):
                    act.wait_ge(M.sem, M.at(l, "var", c))
                    inverse_root(of_chunk(E["cs"], c), of_chunk_sum(1), 1 / 64, Mc("gn"), (l, "y_rstd", c))

                def a_hi(c):
                    act.wait_ge(V.sem, V.at(l, "a_y", c))
                    copy(of_chunk(mix_hi[:, 0:2, :], c), of_chunk(B2["y"], c)).then_inc(A.sem, A.mark(l, "a_hi", c))

                of_chunk = lambda v, c: v[:, :, c * P:(c + 1) * P]
                act.wait_ge(V.sem, V.at(l, "mix", 0))
                act.activation(pm[0:64, 0, :], pm[0:64, 0, :], ACT.Tanh)
                act.activation(pm[:, 1, :], pm[:, 1, :], ACT.Sigmoid).then_inc(A.sem, A.mark(l, "lora_in"))
                act.wait_ge(M.sem, M.at(l, "lora"))
                for t in range(2):
                    last = act.activation(E["sg"][:, t, :], pairs(0)[:, t, :], ACT.Sigmoid, bias=Par(f"w0{l}", t))
                last.then_inc(A.sem, A.mark(l, "sg"))
                for t in range(2):
                    last = act.activation(B2["a"][:, t, :], pairs(1)[:, t, :], ACT.Sigmoid, bias=Par(f"a0{l}", t))
                last.then_inc(A.sem, A.mark(l, "a"))
                act.wait_ge(V.sem, V.at(l, "kk"))
                act.activation(flat(E["t0"]), flat(B2["kkn"]), ACT.Square).then_inc(A.sem, A.mark(l, "kk_sq"))
                act.wait_ge(V.sem, V.at(l, "mix", 4))
                act.activation(pm[64:96, 8, :], pm[64:96, 8, :], ACT.Sigmoid).then_inc(A.sem, A.mark(l, "gate_in"))
                c0 = math.exp(-0.5)
                act.wait_ge(V.sem, V.at(l, "kk_max"))
                inverse_root(flat(E["t0"]), flat(E["t0"]), 1.0, 0.0, (l, "kk_rn"))
                act.wait_ge(V.sem, V.at(l, "cx"))
                act.activation(flat(E["ep"]), flat(E["cs"]), ACT.Exp, scale=-c0)
                act.activation(flat(E["en"]), flat(E["cs"]), ACT.Exp, scale=c0).then_inc(A.sem, A.mark(l, "ep"))
                act.activation(flat(E["cx"]), flat(E["cx"]), ACT.Exp, scale=-c0)
                act.activation(small[:, 36:38], small[:, 34:36], ACT.Exp, scale=-c0).then_inc(A.sem, A.mark(l, "ex"))
                act.wait_ge(V.sem, V.at(l, "mix", 4))
                act.activation(G2["gram"].rearrange("p a b c -> p (a b) c"),
                               C("ones").unsqueeze(1).broadcast_to([P, 32, P]), ACT.Copy, scale=0.0)\
                    .then_inc(A.sem, A.mark(l, "gram0"))
                act.wait_ge(M.sem, M.at(l, "gate"))
                copy(flat(B2["gate"]), bank[2][:, :]).then_inc(A.sem, A.mark(l, "gate"))
                act.wait_ge(M.sem, M.at(l, "v_turn"))
                copy(flat(B2["vt"]), bank[6][:, :]).then_inc(A.sem, A.mark(l, "v_turned"))
                act.wait_ge(M.sem, M.at(l, "kb_turn"))
                copy(flat(B2["kbt"]), bank[7][:, :]).then_inc(A.sem, A.mark(l, "kb_turned"))
                act.wait_ge(V.sem, V.at(l, "in", 5))
                act.activation(b["cqs"], B2["cq"], ACT.Square)
                act.activation(b["ckvs"], B2["ckv"], ACT.Square).then_inc(A.sem, A.mark(l, "c_sq"))
                Xm, Y = INV["x"], INV["yy"]
                for q in range(2):
                    act.wait_ge(M.sem, M.at(l, "inv0", q))
                    copy(Xm[:, 4 * q:4 * q + 4, :], quads(q)).then_inc(A.sem, A.mark(l, "inv0", q))
                for n in range(1, 7):
                    for q in range(2):
                        act.wait_ge(M.sem, M.at(l, "inv_y", n, q))
                        if n >= 2:
                            act.wait_ge(M.sem, M.at(l, "inv_z", n - 1, q))
                        copy(Y[:, 4 * q:4 * q + 4, :], quads(q)).then_inc(A.sem, A.mark(l, "inv_y", n, q))
                    beside_inverse(n)
                for c in range(TT):
                    act.wait_ge(M.sem, M.at(l, "r", c))
                    if c:
                        act.wait_ge(M.sem, M.at(l, "sa", 0))
                    copy(B2["rs"], bank[0][:, 0:T]).then_inc(A.sem, A.mark(l, "r", c))
                    attend(l, 4 + 3 * c, 8)
                    if c:
                        square_of(0)
                    attend(l, 5 + 3 * c, 8)
                    if c:
                        root_of(0)
                    act.wait_ge(M.sem, M.at(l, "y", c))
                    copy(of_chunk(B2["y"], c), pairs(3)[:, :, 0:P]).then_inc(A.sem, A.mark(l, "y", c))
                    if c == 0:
                        attend(l, 6, 8)
                        act.wait_ge(M.sem, M.at(l, "values", 3))
                        mix(2, pairs(6), (l, "b_hi"))
                square_of(1)
                act.wait_ge(M.sem, M.at(l, "values", 5))
                mix(4, pairs(7), (l, "c_hi", 0))
                act.wait_ge(M.sem, M.at(l, "values", 7))
                mix(6, pairs(6), (l, "c_hi", 1))
                root_of(1)
                a_hi(0)
                a_hi(1)

            act.dma_start(mat[:, 0:NMAT1], ins["mat"][0, :, 0:NMAT1]).then_inc(first_mats, 16)
            act.dma_start(REL["onehot"][0:32, :], ins["onehot"][0:32, :]).then_inc(bias_tables, 16)
            act.dma_start(REL["relneg"][0:8, :], ins["onehot"][32:40, :]).then_inc(bias_tables, 16)
            act.wait_ge(x_loaded, 32)
            act.activation(small[:, 40:42], Par("lam"), ACT.Abs).then_inc(A.sem, A.mark("lam_abs"))
            act.wait_ge(A.sem, A.at("lam_abs"))
            act.activation(small[:, 40:42], small[:, 40:42], ACT.Exp, scale=-1.0).then_inc(A.sem, A.mark("lam_e"))
            for l in range(LAYERS):
                for m in range(4):
                    hi_of_x(l, "in", "pre_mix" if l == 0 else f"attn{l}", m)
                if l == 0:
                    act.wait_ge(loaded[0], 16)
                    copy(w_hi[:, 0, :], raw[:, 0, :]).then_inc(hi_act, 1)
                    act.wait_ge(tables, 16)
                square(l, "in")
                norm_factor(l, "in", "in")
                block1() if l == 0 else rwkv(l)
                gain, c0 = "pre_ffn" if l == 0 else f"ffn{l}", CHUNK[l, "gu", 0]
                if l == 0:
                    for m in range(4):
                        act.wait_ge(M.sem, M.at(l, "mixed", m))
                        act.activation(sq[:, 2 * m:2 * m + 2, :], pairs(m), ACT.Square)\
                            .then_inc(A.sem, A.mark(l, "mixed", "sq", m))
                        if 1 <= m < 3:
                            hi_of(c0 + m - 1)
                    norm_factor(l, "mixed", "mixed")
                    for m in range(4):
                        hi_of_x(l, "ffn", gain, m)
                else:
                    hi_of(c0)
                    for m in range(3):
                        hi_of_x(l, "ffn", gain, m)
                    hi_of(c0 + 1)
                    hi_of_x(l, "ffn", gain, 3)
                hi_of(c0 + 2)
                ffn(l)
                if l == 0:
                    for m in range(4):
                        act.wait_ge(M.sem, M.at(l, "fed", m))
                        act.activation(sq[:, 2 * m:2 * m + 2, :], pairs(m), ACT.Square)\
                            .then_inc(A.sem, A.mark(l, "fed", "sq", m))
                    norm_factor(l, "fed", "fed")
            for m in range(4):
                act.wait_ge(V.sem, V.at(2, "fed", m))
                act.activation(sq[:, 2 * m:2 * m + 2, :], x[:, 2 * m:2 * m + 2, :], ACT.Square)\
                    .then_inc(A.sem, A.mark(LAYERS, "final", "sq", m))
            norm_factor(LAYERS, "final", "final")
            for m in range(4):
                act.wait_ge(V.sem, V.at("final", m))
                act.dma_start(out[:, 2 * m * T:2 * (m + 1) * T], xg[:, 2 * m:2 * m + 2, :].rearrange("p k t -> p (k t)"))\
                    .then_inc(stored, 16)
            act.wait_ge(stored, 64)

        @block.vector
        def _(dve):
            def wide(v, n):
                return v.unsqueeze(1).broadcast_to([P, n, v.shape[-1]])

            def tt(dst, a, b, op, *name):
                ins_ = dve.tensor_tensor(dst, a, b, op)
                if name:
                    ins_.then_inc(V.sem, V.mark(*name))
                return ins_

            def after_v(*name):
                dve.wait_ge(V.sem, V.at(*name))

            def after_a(*name):
                dve.wait_ge(A.sem, A.at(*name))

            def after_m(*name):
                dve.wait_ge(M.sem, M.at(*name))

            def lo_of(c):
                s, n = c % RING, STREAM[c][3]
                dve.wait_ge(hi_act, n_hi[c])
                dve.tensor_tensor(w_lo[:, s, 0:n], raw[:, s, 0:n], w_hi[:, s, 0:n].bitcast(F32), ALU.subtract)\
                    .then_inc(lo_dve, 1)

            def lo_of_x(l, what, g, m):
                after_a(l, what, "hi", m)
                for k in (2 * m, 2 * m + 1):
                    last = dve.scalar_tensor_tensor(h_lo[:, k, :], x[:, k, :], Par(g, k), h_hi[:, k, :].bitcast(F32),
                                                    ALU.mult, ALU.subtract)
                last.then_inc(V.sem, V.mark(l, what, "lo", m))

            def residual(l, what, m):
                after_m(l, what, m)
                tt(x[:, 2 * m:2 * m + 2, :], x[:, 2 * m:2 * m + 2, :], pairs(m), ALU.add, l, what, m)

            def normed(l, what, gain, m):
                for k in (2 * m, 2 * m + 1):
                    last = dve.scalar_tensor_tensor(xg[:, k, :], pairs(m)[:, k % 2, :], Par(gain, k), rstd[:, :],
                                                    ALU.mult, ALU.mult)
                last.then_inc(V.sem, V.mark(l, what, "normed", m))

            def normed_residual(l, what, gain, after, g):
                after_a(l, what, "rstd")
                normed(l, what, gain, 0)
                for m in range(4):
                    if m < 3:
                        normed(l, what, gain, m + 1)
                    after_v(l, what, "normed", m)
                    tt(x[:, 2 * m:2 * m + 2, :], x[:, 2 * m:2 * m + 2, :], xg[:, 2 * m:2 * m + 2, :], ALU.add,
                       l, what, m)
                    if m:
                        lo_of_x(*after, g, m - 1)
                lo_of_x(*after, g, 3)

            def evacuate(l, i, dst, scale=None, token_major=False, single=False):
                after_m(l, "in", i)
                src = projected(l, i)
                if i == 0:
                    after_a(l, "in", "rstd")
                if token_major:
                    for t in range(TT):
                        last = dve.tensor_scalar(dst[:, t, :], src[:, t, :], rstd_col[:, t:t + 1], None, ALU.mult)
                else:
                    parts = list(dst) if isinstance(dst, (list, tuple)) else [dst]
                    for t, d in enumerate(parts):
                        s = src if len(parts) == 1 and not single else src[:, t, :]
                        r = wide(rstd[:, :], 2) if len(parts) == 1 and not single else rstd[:, :]
                        if scale and scale[t]:
                            last = dve.scalar_tensor_tensor(d, s, scale[t], r, ALU.mult, ALU.mult)
                        else:
                            last = dve.tensor_tensor(d, s, r, ALU.mult)
                last.then_inc(V.sem, V.mark(l, "in", i))

            def column_factor(l):
                after_m(l, "in", "rstd")
                dve.tensor_copy(rstd_col[:, :], bank[7][:, 0:2 * P].rearrange("p (a b) -> p a b", a=2)[:, :, 0])\
                    .then_inc(V.sem, V.mark(l, "in", "rstd_col"))
                after_v(l, "in", "rstd_col")

            def attend(l, i, heads, mask):
                v = B1 if l == 0 else AT2
                if 1 <= i <= heads:
                    j = i - 1
                    L, o = v["att_l"][:, j % 2, :], 2 * (j % 2)
                    after_a(l, "exp", j)
                    dve.reciprocal(small[:, 28 + o:30 + o], small[:, 16 + o:18 + o])\
                        .then_inc(V.sem, V.mark(l, "inv", j))
                    after_v(l, "inv", j)
                    dve.tensor_scalar(L[:, 0:T], L[:, 0:T], small[:, 28 + o:29 + o], None, ALU.mult)
                    dve.tensor_scalar(L[:, T:T + P], L[:, T:T + P], small[:, 29 + o:30 + o], None, ALU.mult)\
                        .then_inc(V.sem, V.mark(l, "probs", j))
                if i < heads:
                    after_m(l, "scores", i)
                    if i >= 2:
                        after_m(l, "turn", i - 2)
                    L, b, o = v["att_l"][:, i % 2, :], bank[4 + i % 2], 2 * (i % 2)
                    late, early = mask(i)
                    dve.tensor_tensor_reduce(L[:, 0:T], b[:, 0:T], late, 1.0, -3e38, ALU.add, ALU.max,
                                             small[:, 24 + o:25 + o])
                    dve.tensor_tensor_reduce(L[:, T:T + P], b[:, T:T + P], early, 1.0, -3e38, ALU.add, ALU.max,
                                             small[:, 25 + o:26 + o]).then_inc(V.sem, V.mark(l, "logits", i))
                    after_v(l, "logits", i)
                    dve.tensor_scalar(small[:, 8 + o:10 + o], small[:, 24 + o:26 + o], -1.0, None, ALU.mult)\
                        .then_inc(V.sem, V.mark(l, "max", i))

            def mix_lo_of(t, src, hi_name, *name):
                after_a(*hi_name)
                tt(mix_lo[:, t:t + 2, :], src, mix_hi[:, t:t + 2, :].bitcast(F32), ALU.subtract, *name)

            def block1():
                l, lru = 0, B1["lru"]
                flat = lambda v: v.rearrange("p a b -> p (a b)")
                small_ = small
                dve.memset(B1["lx"][:, :, 0:3], 0.0)
                dve.memset(flat(B1["qm"]), 0.0).then_inc(V.sem, V.mark("zeros"))
                evacuate(l, 0, B1["lx"][:, :, 3:259])
                after_v(l, "in", 0)
                for j in range(4):
                    if j:
                        after_v("lru_conv", j - 1)
                    for t in range(2):
                        dst, src = lru[:, 0, t * T:(t + 1) * T], B1["lx"][:, t, j:j + T]
                        w = Par("conv_w", 2 * j + t)
                        if j == 0:
                            last = dve.tensor_scalar(dst, src, w, Par("conv_b", t), ALU.mult, ALU.add)
                        else:
                            last = dve.scalar_tensor_tensor(dst, src, w, dst, ALU.mult, ALU.add)
                    last.then_inc(V.sem, V.mark("lru_conv", j) if j < 3 else V.mark("lru_conv"))
                evacuate(l, 1, [B1["glr"], B1["gk"]])
                column_factor(l)
                after_m("gla_gate")
                dve.tensor_scalar(B1["g0"], bank[6][:, 0:T], Par("gate_b"), None, ALU.add)\
                    .then_inc(V.sem, V.mark("gla_z"))
                after_v("gla_z")
                dve.tensor_scalar(B1["g2"], B1["g0"], 0.0, None, ALU.min).then_inc(V.sem, V.mark("gla_min"))
                after_v("gla_min")
                dve.scalar_tensor_tensor(B1["g1"], B1["g2"], -2.0, B1["g0"], ALU.mult, ALU.add)\
                    .then_inc(V.sem, V.mark("gla_abs"))
                evacuate(l, 2, [B1["gq"], B1["mq"][:, 0, :]], scale=(32 ** -0.5, 0.125))
                after_a("gla_l")
                tt(B1["g0"], B1["g2"], B1["g1"], ALU.subtract, "gla_log")
                after_v("gla_log")
                for n in range(4):
                    s = slice(64 * n, 64 * n + 64)
                    last = dve.tensor_tensor_scan(B1["g2"][:, s], C("ones")[:, 0:64], B1["g0"][:, s], 0.0, ALU.mult,
                                                  ALU.add)
                last.then_inc(V.sem, V.mark("gla_cum"))
                after_v("gla_cum")
                dve.tensor_scalar(small[:, 0:4], B1["g2"].rearrange("p (n c) -> p n c", n=4)[:, :, 63], 1 / 16, None,
                                  ALU.mult).then_inc(V.sem, V.mark("gla_last"))
                evacuate(l, 3, B1["gv"], token_major=True)
                after_v(l, "in", 2)
                after_a("gla_ep")
                for h in range(4):
                    s = slice(32 * h, 32 * h + 32)
                    dve.tensor_tensor(B1["qm"][s, h, :], B1["gq"][s, :], B1["g0"][s, :], ALU.mult)
                after_a("gla_en")
                tt(B1["kd"], B1["gk"], B1["g1"], ALU.mult)
                after_a("gla_ee")
                tt(B1["ke"], B1["gk"], B1["ke"], ALU.mult, "gla_ke")
                evacuate(l, 4, B1["lg"])
                evacuate(l, 5, B1["gout"])
                after_m("gla_scores")
                for t in range(TT):
                    dve.tensor_tensor(B1["att"][:, t, :].rearrange("p (h t) -> p h t", h=4), quads(2 + t),
                                      wide(C("gla_mask"), 4), ALU.mult).then_inc(V.sem, V.mark("gla_att", t))
                evacuate(l, 6, B1["mk"][:, 0:2, :])
                after_m("gla_kv")
                st = B1["st"]
                dve.tensor_copy(st[:, 0, :], pairs(0)[:, 0, :]).then_inc(V.sem, V.mark("gla_state", 0))
                for n, src in ((1, bank[7][:, 0:T]), (2, pairs(0)[:, 1, :])):
                    after_v("gla_state", n - 1)
                    dve.scalar_tensor_tensor(st[:, n, :], st[:, n - 1, :], small[:, 4 + n:5 + n], src, ALU.mult,
                                             ALU.add).then_inc(V.sem, V.mark("gla_state", n))
                after_a("lru_sig")
                for t in range(2):
                    s = slice(t * T, (t + 1) * T)
                    last = dve.tensor_scalar(lru[:, 1, s], lru[:, 1, s], small[:, 44 + t:45 + t], None, ALU.mult)
                last.then_inc(V.sem, V.mark("lru_log"))
                tt(lru[:, 2, :], lru[:, 2, :], lru[:, 0, :], ALU.mult, "lru_ix")
                evacuate(l, 7, [B1["mq"][:, 1, :], B1["mq"][:, 2, :]], scale=(0.125, 0.125))
                after_a("lru_a")
                after_v("lru_ix")
                tt(lru[:, 0, :], lru[:, 4, :], lru[:, 4, :], ALU.mult, "lru_a2")
                after_v("lru_a2")
                dve.scalar_tensor_tensor(lru[:, 3, :], lru[:, 0, :], 1.0, lru[:, 3, :], ALU.add, ALU.mult)\
                    .then_inc(V.sem, V.mark("lru_m2"))
                after_a("lru_mult")
                dve.memset(lru[:, 3, :].rearrange("p (a b) -> p a b", a=2)[:, :, 0:1], 1.0)\
                    .then_inc(V.sem, V.mark("lru_first"))
                after_v("lru_first")
                tt(lru[:, 2, :], lru[:, 2, :], lru[:, 3, :], ALU.mult, "lru_u")
                after_v("lru_u")
                for t in range(2):
                    s = slice(t * T, (t + 1) * T)
                    last = dve.tensor_tensor_scan(lru[:, 0, s], lru[:, 4, s], lru[:, 2, s], 0.0, ALU.mult, ALU.add)
                last.then_inc(V.sem, V.mark("lru_h"))
                after_v("lru_h")
                after_a("lru_gelu")
                evacuate(l, 8, B1["mk"][:, 2:4, :])
                tt(lru[:, 2, :], lru[:, 0, :], lru[:, 5, :], ALU.mult, "lru_y")
                evacuate(l, 9, [B1["mq"][:, 3, :]], scale=(0.125,), single=True)
                after_a("gla_rstd")
                tt(flat(B1["go"]), flat(B1["go"]), flat(B1["gt"]), ALU.mult, "gla_n")
                after_v("gla_n")
                for t in range(2):
                    last = dve.scalar_tensor_tensor(B1["go"][:, t, :], B1["go"][:, t, :], Par("gla_norm", t),
                                                    B1["gout"][:, t, :], ALU.mult, ALU.mult)
                last.then_inc(V.sem, V.mark("gla_y"))
                mix_lo_of(0, lru[:, 2, :].rearrange("p (a b) -> p a b", a=2), ("lru_hi",), "lru_lo")
                mix_lo_of(2, B1["go"], ("gla_hi",), "gla_lo")
                evacuate(l, 10, B1["mv"][:, :, 0:T], token_major=True)
                for i in range(9):
                    if i == 2:
                        evacuate(l, 11, B1["mv"][:, :, T:2 * T], token_major=True)
                    attend(l, i, 8, lambda i: (B1["bias"][:, i, :], B1["bias"][:, i, P:2 * P]))
                mix_lo_of(4, pairs(6), ("moba_hi", 0), "moba_lo", 0)
                mix_lo_of(6, pairs(7), ("moba_hi", 1), "moba_lo")

            def rwkv(l):
                flat = lambda v: v.rearrange("p a b -> p (a b)")
                pm, pf, E, S, b = B2["pm"], PF["pf"], EARLY, small, AT2

                def rotate(n, dst, v, swapped, cos):
                    w = 2 if len(v.shape) == 3 else 1
                    table = lambda i: wide(rope[:, i, :], 2) if w == 2 else rope[:, i, :]
                    t0, t1 = (b["t0"], b["t1"]) if w == 2 else (b["t0"][:, 0, :], b["t1"][:, 0, :])
                    tt(t0, v, table(cos), ALU.mult)
                    tt(t1, swapped, table(cos + 1), ALU.mult, l, "rot", n)
                    after_v(l, "rot", n)
                    tt(dst, t0, t1, ALU.add, l, "rotated", n)
                    after_v(l, "rotated", n)

                of_chunk = lambda v, c: v[:, :, c * P:(c + 1) * P]

                def center(c):
                    y = of_chunk(B2["y"], c)
                    after_m(l, "mean", c)
                    dve.scalar_tensor_tensor(y, of_chunk_sum(0), -1 / 64, y, ALU.mult, ALU.add)\
                        .then_inc(V.sem, V.mark(l, "yc", c))

                def finish(c):
                    y = of_chunk(B2["y"], c)
                    after_a(l, "y_rstd", c)
                    tt(y, y, of_chunk(E["cs"], c), ALU.mult, l, "yn", c)
                    after_v(l, "yn", c)
                    for t in range(2):
                        last = dve.tensor_scalar(y[:, t, :], y[:, t, :], Par(f"ln_w{l}", t), Par(f"ln_b{l}", t),
                                                 ALU.mult, ALU.add)
                    last.then_inc(V.sem, V.mark(l, "yl", c))
                    after_v(l, "yl", c)
                    tt(y, y, of_chunk(pm[:, 6:8, :], c), ALU.add, l, "yb", c)
                    after_v(l, "yb", c)
                    tt(y, y, of_chunk(B2["gate"], c), ALU.mult, l, "a_y", c)

                def attention(i):
                    attend(l, i, 8, lambda i: (C("dilated" if i < 4 else "causal")[:, 0:T],
                                               C("dilated" if i < 4 else "causal")[:, T:T + P]))

                def beside_inverse(n):
                    if n == 1:
                        after_a(l, "rkv")
                        for t in range(2):
                            dve.scalar_tensor_tensor(b["cqn"][:, t, :], B2["cq"][:, t, :], Par(f"qn{l}", t), b["rq"],
                                                     ALU.mult, ALU.mult)
                        dve.scalar_tensor_tensor(b["ckvn"], B2["ckv"], Par(f"kvn{l}", 0), b["rkv"], ALU.mult, ALU.mult)\
                            .then_inc(V.sem, V.mark(l, "c_n"))
                        evacuate(l, 7, B2["bk"])
                        evacuate(l, 8, B2["bv"], token_major=True)
                        after_a(l, "c_hi")
                        tt(cq_lo[:, 0:2, :], b["cqn"], cq_hi[:, 0:2, :].bitcast(F32), ALU.subtract)
                        tt(cq_lo[:, 2, :], b["ckvn"], cq_hi[:, 2, :].bitcast(F32), ALU.subtract, l, "c_lo")
                        after_v(l, "c_lo")
                    if n == 2:
                        after_m(l, "b_rot")
                        rotate(0, B2["bq"], B2["bq"], pairs(6), 0)
                        rotate(1, B2["bk"], B2["bk"], pairs(7), 0)
                    if n == 3:
                        after_m(l, "k_rot")
                        rotate(2, b["kro"], bank[6][:, 0:T], bank[6][:, T:2 * T], 2)
                    if n == 4:
                        after_a(l, "up", 2)
                        after_m(l, "q_rot")
                        rotate(3, b["qr"], b["qr"], pairs(7), 2)
                        dve.nop().then_inc(V.sem, V.mark(l, "c_rope"))
                    if n >= 5:
                        attention(2 * n - 10)

                dve.memset(pf[:, :, 0:1], 0.0).then_inc(V.sem, V.mark(l, "zeros"))

                def shift(n, tiles, rows=slice(0, P)):
                    a, b = tiles
                    tt(pm[rows, a:b, :], pf[rows, a:b, 0:T], pf[rows, a:b, 1:T + 1], ALU.subtract, l, "diff", n)
                    after_v(l, "diff", n)
                    for t in range(a, b):
                        last = dve.scalar_tensor_tensor(pm[rows, t, :], pm[rows, t, :],
                                                        Par(f"mu{l}", t)[rows, :], pf[rows, t, 1:T + 1],
                                                        ALU.mult, ALU.add)
                    last.then_inc(V.sem, V.mark(l, "mix", n))

                def evac_shift(i):
                    evacuate(l, i, pf[:, 2 * i:2 * i + 2, 1:T + 1])
                    after_v(l, "in", i)
                    shift(i, (2 * i, 2 * i + 2))

                evac_shift(0)
                evac_shift(1)
                after_v(l, "mix", 1)
                for t in range(2):
                    last = dve.tensor_scalar(B2["kkn"][:, t, :], pm[:, 2 + t, :], Par(f"k_k{l}", t), None, ALU.mult)
                last.then_inc(V.sem, V.mark(l, "kk"))
                column_factor(l)
                after_a(l, "sg")
                for t in range(2):
                    for c in range(TT):
                        s = slice(c * P, (c + 1) * P)
                        last = dve.tensor_tensor_scan(E["cs"][:, t, s], C("ones"), E["sg"][:, t, s], 0.0, ALU.mult,
                                                      ALU.add)
                last.then_inc(V.sem, V.mark(l, "scan"))
                evac_shift(2)
                evac_shift(3)
                evacuate(l, 4, [pf[:, 8, 1:T + 1], B2["ckv"]])
                after_v(l, "in", 4)
                dve.tensor_copy(B2["krope"][0:64, :], pf[0:64, 8, 1:T + 1])
                shift(4, (8, 9), slice(64, 96))
                after_v(l, "scan")
                by_chunk = lambda v: v.rearrange("p a (c t) -> p (a c) t", c=TT)
                cs = by_chunk(E["cs"])
                dve.tensor_copy(S[:, 50:54], cs[:, :, 63]).then_inc(V.sem, V.mark(l, "mid"))
                after_v(l, "mid")
                tt(cs, cs, S[:, 50:54].unsqueeze(2).broadcast_to([P, 4, P]), ALU.subtract, l, "cs")
                after_v(l, "cs")
                tt(S[:, 34:36], E["cs"][:, :, P - 1], S[:, 50:54].rearrange("p (a c) -> p a c", c=TT)[:, :, 1], ALU.add)
                tt(E["cx"], E["cs"], E["sg"], ALU.subtract, l, "cx")
                after_m(l, "kk_ss")
                after_a(l, "kk_sq")
                dve.tensor_scalar(flat(E["t0"]), bank[3][:, :], 1e-24, None, ALU.max)\
                    .then_inc(V.sem, V.mark(l, "kk_max"))
                after_a(l, "a")
                for t in range(2):
                    last = dve.tensor_scalar(B2["kp"][:, t, :], B2["a"][:, t, :], -1.0, Par(f"k_a{l}", t), ALU.add,
                                             ALU.mult)
                last.then_inc(V.sem, V.mark(l, "kp0"))
                after_v(l, "kp0")
                dve.scalar_tensor_tensor(flat(B2["kp"]), flat(B2["kp"]), 1.0, flat(pm[:, 2:4, :]), ALU.add, ALU.mult)\
                    .then_inc(V.sem, V.mark(l, "kp"))
                after_a(l, "kk_rn")
                tt(B2["kkn"], B2["kkn"], E["t0"], ALU.mult, l, "kkn")
                after_v(l, "kkn")
                for t in range(2):
                    last = dve.scalar_tensor_tensor(E["t0"][:, t, :], pm[:, 4 + t, :], Par(f"r_k{l}", t),
                                                    B2["kp"][:, t, :], ALU.mult, ALU.mult)
                last.then_inc(V.sem, V.mark(l, "bonus_in"))
                after_a(l, "ep")
                after_v(l, "kkn")
                tt(B2["bh"], B2["kkn"], B2["a"], ALU.mult, l, "b")
                after_v(l, "b")
                tt(B2["bh"], B2["bh"], E["en"], ALU.mult)
                tt(B2["kh"], B2["kp"], E["en"], ALU.mult)
                after_a(l, "ex")
                cut = lambda v: v.rearrange("p (c t) -> p c t", c=TT)
                for t in range(2):
                    tt(B2["kr"][:, t, :, 0, :], cut(B2["kkn"][:, t, :]), cut(E["cx"][:, t, :]), ALU.mult)
                    last = tt(B2["kr"][:, t, :, 1, :], cut(pm[:, 4 + t, :]), cut(E["ep"][:, t, :]), ALU.mult)
                last.then_inc(V.sem, V.mark(l, "kr"))
                evacuate(l, 5, B2["cq"])
                gram = G2["gram"]
                dve.memset(B2["s1"].rearrange("p a b -> p (a b)"), 0.0)
                after_m(l, "v_turn")
                after_m(l, "bonus")
                tt(flat(pm[:, 6:8, :]), bank[3][:, :], flat(pm[:, 6:8, :]), ALU.mult, l, "bonus")
                after_a(l, "gram0")
                mask = C("before").bitcast(U32)
                for g in range(8):
                    after_m(l, "gram", g)
                    for n in range(2):
                        last = dve.copy_predicated(gram[:, g, 2 * n:2 * n + 2, :].rearrange("p a b -> p (a b)"), mask,
                                                   pairs(g % 4)[:, n, :])
                    last.then_inc(V.sem, V.mark(l, "gram", g))
                Xm, XT, BT = INV["x"], INV["xt"], INV["bt"]
                q4 = lambda v, q: v[:, 4 * q:4 * q + 4, :]

                def level(n, q, to):
                    return dve.tensor_tensor(q4(to, q), q4(gram[:, :, 0, :], q), wide(C(f"level{n}"), 4), ALU.mult)

                after_v(l, "gram", 7)
                for q in range(2):
                    level(0, q, BT).then_inc(V.sem, V.mark(l, "inv_b0", q))
                for q in range(2):
                    after_v(l, "inv_b0", q)
                    tt(q4(XT, q), wide(C("ident"), 4), q4(BT, q), ALU.subtract, l, "inv0", q)
                for q in range(2):
                    after_v(l, "inv0", q)
                    level(1, q, BT).then_inc(V.sem, V.mark(l, "inv_bt", 1, q))
                evacuate(l, 6, [B2["bq"][:, 0, :], B2["bq"][:, 1, :]], scale=(0.125, 0.125))
                for n in range(1, 7):
                    if n < 6:
                        for q in range(2):
                            after_m(l, "inv_y", n, q)
                            level(n + 1, q, BT).then_inc(V.sem, V.mark(l, "inv_bt", n + 1, q))
                    beside_inverse(n)
                    for q in range(2):
                        if n < 6:
                            after_m(l, "inv_z", n, q)
                            if n == 1:
                                after_a(l, "inv0", q)
                            tt(q4(Xm, q), q4(Xm, q), quads(q), ALU.subtract, l, "inv_x0", n, q)
                        after_m(l, "inv_zt", n, q)
                        tt(q4(XT, q), q4(XT, q), quads(2 + q), ALU.subtract, l, "inv_xt", n, q)
                        if n < 6:
                            dve.wait_ge(V.sem, V.at(l, "inv_xt", n, q))
                            dve.nop().then_inc(V.sem, V.mark(l, "inv_x", n, q))
                    if n >= 5:
                        attention(2 * n - 9)
                for c in range(TT):
                    if c:
                        center(0)
                    attention(4 + 3 * c)
                    after_m(l, "sa", c)
                    dve.tensor_scalar(B2["nsa"][:, c, :], bank[1][:, 0:T], -1.0, None, ALU.mult)\
                        .then_inc(V.sem, V.mark(l, "nsa", c))
                    attention(5 + 3 * c)
                    if c == 0:
                        after_m(l, "s1")
                        after_a(l, "ex")
                        for t in range(2):
                            for h in range(2):
                                rows = slice(64 * h, 64 * h + 64)
                                last = dve.tensor_scalar(B2["s1"][rows, t, rows], bank[2][rows, t * 64:(t + 1) * 64],
                                                         S[rows, 36 + t:37 + t], None, ALU.mult)
                        last.then_inc(V.sem, V.mark(l, "s1"))
                        attention(6)
                        mix_lo_of(2, pairs(6), (l, "b_hi"), l, "b_lo")
                center(1)
                mix_lo_of(4, pairs(7), (l, "c_hi", 0), l, "c_lo", 0)
                finish(0)
                mix_lo_of(6, pairs(6), (l, "c_hi", 1), l, "c_lo", 1)
                finish(1)
                for c in range(TT):
                    after_a(l, "a_hi", c)
                    tt(of_chunk(mix_lo[:, 0:2, :], c), of_chunk(B2["y"], c), of_chunk(mix_hi[:, 0:2, :].bitcast(F32), c),
                       ALU.subtract, l, "a_lo", c)

            def ffn(l):
                def feed(j):
                    after_m(l, "gu", j)
                    if j == 0:
                        after_a(l, "ffn", "rstd")
                    if j >= 2:
                        after_a(l, "silu", j - 2)
                        after_v(l, "act", j - 2)
                    tt(FF["gu"][:, j % 2, :, :], pairs(4 + j % 2), wide(rstd[:, :], 2), ALU.mult, l, "gu", j)
                    after_a(l, "silu", j)
                    after_v(l, "gu", j)
                    tt(FF["act"][:, j % 2, :], FF["sg"][:, j % 2, :], FF["gu"][:, j % 2, 1, :], ALU.mult, l, "act", j)
                    after_a(l, "act", "hi", j)
                    if j >= 4:
                        after_m(l, "down", (j - 4) // 2)
                    tt(act_lo[:, j % 4, :], FF["act"][:, j % 2, :], act_hi[:, j % 4, :].bitcast(F32), ALU.subtract,
                       l, "act", "lo", j)

                todo = list(range(CHUNK[l, "gu", 0] + RING, CHUNK[l, "down", FT // 2 - 1] + 1))

                def after(c):
                    if todo and todo[0] <= c + RING:
                        lo_of(todo.pop(0))

                after(CHUNK[l, "gu", 0])
                after(CHUNK[l, "gu", 1])
                feed(0)
                feed(1)
                for p in range(1, FT // 2):
                    for j in (2 * p, 2 * p + 1):
                        after(CHUNK[l, "gu", j])
                        feed(j)
                        if l == 0 and 4 <= j < 8:
                            angles((j - 4) // 2, j % 2)
                    after(CHUNK[l, "down", p - 1])

            def angles(i, s):
                if i == 0 and s == 0:
                    dve.wait_ge(positions, 16)
                    dve.tensor_copy(ANG["p"], pos).then_inc(V.sem, V.mark("pos"))
                    after_v("pos")
                if s == 0:
                    dve.tensor_scalar(ANG["ang"][:, i, :], ANG["p"], C("freq")[:, i:i + 1], None, ALU.mult)\
                        .then_inc(V.sem, V.mark("ang", i))
                    after_v("ang", i)
                ROUND = 12582912.0
                turns, a, dst, quarter = ANG["n"], ANG["ang"][:, i, :], rope[:, 2 * i + s, :], 0.0 if s else 0.25
                parts = (6.28125, 0.0019350051879882812, 2 * math.pi - 6.28125 - 0.0019350051879882812)
                steps = [lambda: dve.tensor_scalar(turns, a, 1 / (2 * math.pi), quarter, ALU.mult, ALU.add),
                         lambda: dve.tensor_scalar(turns, turns, ROUND, None, ALU.add),
                         lambda: dve.tensor_scalar(turns, turns, -ROUND, None, ALU.add),
                         lambda: dve.scalar_tensor_tensor(dst, turns, -parts[0], a, ALU.mult, ALU.add),
                         lambda: dve.scalar_tensor_tensor(dst, turns, -parts[1], dst, ALU.mult, ALU.add),
                         lambda: dve.scalar_tensor_tensor(dst, turns, -parts[2], dst, ALU.mult, ALU.add),
                         lambda: dve.tensor_scalar(dst, dst, 2 * math.pi * quarter, 3.1415925, ALU.add, ALU.min),
                         lambda: dve.tensor_scalar(dst, dst, -3.1415925, None, ALU.max)]
                for n, step in enumerate(steps):
                    step().then_inc(V.sem, V.mark("angles" if (i, s, n) == (1, 1, 7) else f"angle_{i}_{s}_{n}"))
                    after_v("angles" if (i, s, n) == (1, 1, 7) else f"angle_{i}_{s}_{n}")

            dve.wait_ge(x_loaded, 32)
            for m in range(4):
                lo_of_x(0, "in", "pre_mix", m)
            lo_of(0)
            e, s_, s2, acc = small[:, 40:42], small[:, 56:58], small[:, 58:60], small[:, 60:62]
            after_a("lam_e")
            chain = [lambda: dve.tensor_scalar(s_, e, 2.0, None, ALU.add),
                     lambda: dve.reciprocal(s_, s_),
                     lambda: dve.tensor_tensor(s_, s_, e, ALU.mult),
                     lambda: dve.tensor_tensor(s2, s_, s_, ALU.mult),
                     lambda: dve.memset(acc, 1 / 17)]
            for n in range(7, -1, -1):
                chain += [lambda: dve.tensor_tensor(acc, acc, s2, ALU.mult),
                          lambda n=n: dve.tensor_scalar(acc, acc, 1 / (2 * n + 1), None, ALU.add)]
            chain += [lambda: dve.tensor_tensor(acc, acc, s_, ALU.mult),
                      lambda: dve.tensor_scalar(s_, Par("lam"), -1.0, 0.0, ALU.mult, ALU.max),
                      lambda: dve.scalar_tensor_tensor(acc, acc, 2.0, s_, ALU.mult, ALU.add),
                      lambda: dve.tensor_scalar(small[:, 44:46], acc, -8.0, None, ALU.mult)]
            for n, step in enumerate(chain):
                step().then_inc(V.sem, V.mark("softplus", n))
                after_v("softplus", n)

            dve.wait_ge(bias_tables, 32)
            after_m("rel_row")
            tt(REL["relrow"][0:8, :], bank[0][0:8, 0:384], REL["relneg"][0:8, :], ALU.add, "rel_row")
            dve.wait_ge(tables, 16)
            for l in range(LAYERS):
                c0, gain = CHUNK[l, "gu", 0], "pre_ffn" if l == 0 else f"ffn{l}"
                if l == 0:
                    block1()
                    lo_of(c0)
                    lo_of(c0 + 1)
                    normed_residual(l, "mixed", "post_mix", (l, "ffn"), gain)
                else:
                    rwkv(l)
                    residual(l, "mixed", 0)
                    residual(l, "mixed", 1)
                    lo_of(c0)
                    lo_of_x(l, "ffn", gain, 0)
                    lo_of_x(l, "ffn", gain, 1)
                    residual(l, "mixed", 2)
                    lo_of_x(l, "ffn", gain, 2)
                    lo_of(c0 + 1)
                    residual(l, "mixed", 3)
                    lo_of_x(l, "ffn", gain, 3)
                lo_of(c0 + 2)
                ffn(l)
                if l == 0:
                    normed_residual(l, "fed", "post_ffn", (l + 1, "in"), f"attn{l + 1}")
                    continue
                for m in range(4):
                    residual(l, "fed", m)
                    if m and l + 1 < LAYERS:
                        lo_of_x(l + 1, "in", f"attn{l + 1}", m - 1)
                if l + 1 < LAYERS:
                    lo_of_x(l + 1, "in", f"attn{l + 1}", 3)
            after_a(LAYERS, "final", "rstd")
            for m in range(4):
                for k in (2 * m, 2 * m + 1):
                    last = dve.scalar_tensor_tensor(xg[:, k, :], x[:, k, :], Par("final", k), rstd[:, :],
                                                    ALU.mult, ALU.mult)
                last.then_inc(V.sem, V.mark("final", m))

    return {"V": V.log, "A": A.log, "M": M.log}


def lay_out(inputs):
    f = lambda n: np.asarray(inputs[n])
    rows = lambda w: w.reshape(-1, P, w.shape[-1]).transpose(1, 0, 2)
    wide = lambda v: v.reshape(-1, P).T

    w = np.zeros((NCH, P, CH), np.float32)
    for c, (l, kind, i, n) in enumerate(STREAM):
        m = l - 1
        if kind == "in":
            src = f("w_in")[0] if l == 0 else f("w_in_2")[m]
            part = np.concatenate([src[:, a:b] for a, b in (IN1 if l == 0 else IN2)[i]], 1)
        elif kind == "uq":
            q = f("c_w_uq_2")[m].reshape(256, 4, 192)
            part = np.concatenate([q[:, :, :P].reshape(256, 512), q[:, :, P:].reshape(256, 256)], 1)
        elif kind == "ukv":
            kv = f("c_w_ukv_2")[m].reshape(P, 4, 256)
            part = np.concatenate([kv[:, :, :P].reshape(P, 512), kv[:, :, P:].reshape(P, 512)], 1)
        elif kind == "out":
            part = (f("w_out")[0] if l == 0 else f("w_out_2")[m])[:, i * 256:(i + 1) * 256]
        elif kind == "gu":
            g, u = (f("w_ffn_gate")[0], f("w_ffn_up")[0]) if l == 0 else (f("ffn_w_gate_2")[m], f("ffn_w_up_2")[m])
            part = np.concatenate([v[:, i * P:(i + 1) * P] for v in (g, u)], 1)
        else:
            part = (f("w_ffn_down")[0] if l == 0 else f("ffn_w_down_2")[m])[i * 256:(i + 1) * 256]
        w[c, :, 0:n] = rows(part).reshape(P, n)

    par = np.zeros((P, NPAR), np.float32)

    def put(name, v):
        a, b = PAR_AT[name]
        par[:, a:b] = v

    for name, key in (("pre_mix", "pre_mix_norm"), ("post_mix", "post_mix_norm"), ("pre_ffn", "pre_ffn_norm"),
                      ("post_ffn", "post_ffn_norm"), ("conv_b", "lru_conv_b"), ("ba", "lru_ba"), ("bx", "lru_bx"),
                      ("lam", "lru_lambda"), ("gate_b", "gla_gate_b"), ("gla_norm", "gla_norm")):
        put(name, wide(f(key)[0]))
    put("conv_w", f("lru_conv_w")[0].reshape(4, 2, P).transpose(2, 0, 1).reshape(P, 8))
    put("final", wide(f("final_norm_g_2")))
    for l in (1, 2):
        for name, key in (("attn", "attn_norm_g_2"), ("w0", "a_w0_2"), ("a0", "a_a0_2"), ("k_k", "a_k_k_2"),
                          ("k_a", "a_k_a_2"), ("ln_w", "a_ln_w_2"), ("ln_b", "a_ln_b_2"), ("qn", "c_q_norm_g_2"),
                          ("kvn", "c_kv_norm_g_2"), ("ffn", "ffn_norm_g_2"), ("r_k", "a_r_k_2")):
            put(f"{name}{l}", wide(f(key)[l - 1].reshape(-1)))
        mu = f("a_mu_2")[l - 1]
        r, k, v, lora, g = mu[0:256], mu[256:512], mu[512:768], mu[768:896], mu[896:1056]
        cols = np.zeros((P, 9), np.float32)
        cols[:, 0], cols[:, 1] = lora, g[:P]
        cols[:, 2:4], cols[:, 4:6], cols[:, 6:8] = wide(k), wide(r), wide(v)
        cols[64:96, 8] = g[P:]
        put(f"mu{l}", cols)

    mat = np.zeros((LAYERS, P, NMAT), np.float32)
    for name, key in (("wa", "lru_wa"), ("wx", "lru_wx")):
        a, _ = MAT1_AT[name]
        for j in range(4):
            rows_, at = slice(64 * (j % 2), 64 * (j % 2) + 64), a + P * (j // 2) + 64 * (j % 2)
            mat[0, rows_, at:at + 64] = f(key)[0, j]
    mat[0, 0:16, slice(*MAT1_AT["gate_w2"])] = f("gla_gate_w2")[0]
    mat[0, 0:32, slice(*MAT1_AT["rel"])] = f("rel_bias")
    for l in (1, 2):
        mat[l, 0:64, slice(*MAT2_AT["lora"])] = f("a_decay_up_2")[l - 1]
        mat[l, 64:128, slice(*MAT2_AT["lora"])] = f("a_iclr_up_2")[l - 1]
        mat[l, :, slice(*MAT2_AT["gate_up"])] = f("a_gate_up_2")[l - 1, :P]
        mat[l, 64:96, slice(*MAT2_AT["gate_up2"])] = f("a_gate_up_2")[l - 1, P:]

    dist = 255 - np.arange(384)
    onehot = np.zeros((40, 384), np.float32)
    onehot[t5_bucket(dist), np.arange(384)] = dist >= 0
    onehot[32:40] = np.where(dist >= 0, 0.0, NEG)
    return {
        "w": w, "params": par, "mat": mat, "onehot": onehot,
        "consts": np.concatenate(list(CONST_ARRAYS.values()), 1),
        "x": f("x")[0].T.reshape(KT, P, T).transpose(1, 0, 2).reshape(P, KT * T),
        "pos": f("positions_2"),
    }


def kernel(**inputs):
    from concourse import bacc
    from concourse.bass_utils import run_bass_kernel_spmd

    arrays = {f"in_{name}": np.ascontiguousarray(a) for name, a in lay_out(inputs).items()}

    def build(plan):
        nc = bacc.Bacc("TRN2", target_bir_lowering=False, num_devices=1)
        ins = {name[3:]: nc.dram_tensor(name, a.shape, mybir.dt.from_np(a.dtype), kind="ExternalInput").ap()
               for name, a in arrays.items()}
        ins["pos"] = ins["pos"].broadcast_to([P, T])
        scratch = nc.dram_tensor("bias_rows", [8, 384], F32, kind="Internal")
        ins["scratch"] = scratch.ap()
        ins["hankel"] = bass.AP(scratch, 0, [[1, P], [384, 8], [1, T]])
        out = nc.dram_tensor("out", [P, KT * T], F32, kind="ExternalOutput").ap()
        return nc, program(nc, ins, out, plan)

    _, plan = build({})
    nc, _ = build(plan)
    got = run_bass_kernel_spmd(nc, [arrays], core_ids=[0]).results[0]["out"]
    return got.reshape(P, KT, T).transpose(2, 1, 0).reshape(1, T, D)
```
